# Optimizing a Trainium2 kernel written in Bass

```python
import math
import jax, jax.numpy as jnp
from jax import lax
import numpy as np

D_MODEL = 1024
BATCH = 1
SEQ = 512
DEPTH = 1

D_MIX = D_MODEL
N_GROUPS = 4
GROUP = D_MIX // N_GROUPS
HEAD_DIM = 64
LRU_BLOCKS = GROUP // HEAD_DIM
LRU_BLOCK_DIM = GROUP // LRU_BLOCKS
LRU_CONV = 4
LRU_C = 8.0
SC_CONV = 3
FOX_HEADS = GROUP // HEAD_DIM
NSA_HEADS = GROUP // HEAD_DIM
CMP_LEN = 32
CMP_STRIDE = 16
CMP_HIDDEN = 128
SLC_BLOCK = 64
SLC_TOPK = 16
WINDOW = 512
Q_BLOCK = 128
REL_BUCKETS = 32
REL_MAX_DIST = 128
D_FF = ((8 * D_MODEL // 3 + 255) // 256) * 256
NEG_INF = -1e30
BIG = 1e30
RMS_EPS = 1e-6

C_LRU_X = 0
C_LRU_G = C_LRU_X + GROUP
C_SC_B = C_LRU_G + GROUP
C_SC_C = C_SC_B + GROUP
C_SC_X = C_SC_C + GROUP
C_FOX_Q = C_SC_X + GROUP
C_FOX_K = C_FOX_Q + GROUP
C_FOX_V = C_FOX_K + GROUP
C_FOX_F = C_FOX_V + GROUP
C_NSA_Q = C_FOX_F + FOX_HEADS
C_NSA_KV = C_NSA_Q + GROUP
C_NSA_G = C_NSA_KV + 6 * HEAD_DIM
N_IN = C_NSA_G + 3 * NSA_HEADS


def rms_norm(x, g):
    xf = x.astype(jnp.float32)
    y = xf * lax.rsqrt(jnp.mean(xf * xf, axis=-1, keepdims=True) + RMS_EPS)
    return (y * g.astype(jnp.float32)).astype(x.dtype)

def cols(z, start, width):
    return z[..., start:start + width]

def causal_dwconv(x, w):
    k_len, ch = w.shape
    return lax.conv_general_dilated(x, w[:, None, :], window_strides=(1,), padding=[(k_len - 1, 0)],
                                    dimension_numbers=('NWC', 'WIO', 'NWC'), feature_group_count=ch)

def masked_softmax(s, mask):
    p = jax.nn.softmax(jnp.where(mask, s, NEG_INF), axis=-1)
    return jnp.where(mask, p, 0.0)

def rel_bucket(dist):
    max_exact = REL_BUCKETS // 2
    d = jnp.maximum(dist, 0)
    large = max_exact + (jnp.log(jnp.maximum(d, 1).astype(jnp.float32) / max_exact)
                         / math.log(REL_MAX_DIST / max_exact) * (REL_BUCKETS - max_exact)).astype(jnp.int32)
    large = jnp.minimum(large, REL_BUCKETS - 1)
    return jnp.where(d < max_exact, d, large)

def rg_lru_mixer(xr, gate, conv_w, conv_b, w_gates, b_gates, lam):
    bsz, s_len, _ = xr.shape
    xc = causal_dwconv(xr, conv_w) + conv_b
    xb = xc.reshape(bsz, s_len, LRU_BLOCKS, LRU_BLOCK_DIM)
    r = jax.nn.sigmoid(jnp.einsum('bshi,hij->bshj', xb, w_gates[0]).reshape(bsz, s_len, GROUP) + b_gates[0])
    i = jax.nn.sigmoid(jnp.einsum('bshi,hij->bshj', xb, w_gates[1]).reshape(bsz, s_len, GROUP) + b_gates[1])
    log_a = (-LRU_C * jax.nn.softplus(-lam.astype(jnp.float32))) * r.astype(jnp.float32)
    a = jnp.exp(log_a)
    b = jnp.sqrt(-jnp.expm1(2.0 * log_a)) * (i * xc).astype(jnp.float32)

    def combine(left, right):
        a1, b1 = left
        a2, b2 = right
        return a1 * a2, a2 * b1 + b2

    _, h = lax.associative_scan(combine, (a, b), axis=1)
    return h.astype(xr.dtype) * jax.nn.gelu(gate)

def short_conv_mixer(bg, cg, xs, conv_w):
    return bg * causal_dwconv(cg * xs, conv_w)

def fox_mixer(q, k, v, f_logit, f_bias, qk_gain):
    bsz, s_len, _ = q.shape
    h, d = FOX_HEADS, HEAD_DIM
    q = rms_norm(q.reshape(bsz, s_len, h, d), qk_gain[0])
    k = rms_norm(k.reshape(bsz, s_len, h, d), qk_gain[1])
    v = v.reshape(bsz, s_len, h, d)
    logf = jax.nn.log_sigmoid((f_logit + f_bias).astype(jnp.float32))
    c = lax.cumsum(logf, axis=1).transpose(0, 2, 1)
    nb = s_len // Q_BLOCK
    qb = q.reshape(bsz, nb, Q_BLOCK, h, d).swapaxes(0, 1)
    cb = c.reshape(bsz, h, nb, Q_BLOCK).transpose(2, 0, 1, 3)
    kpos = jnp.arange(s_len)
    scale = HEAD_DIM ** -0.5

    def block(args):
        qi, ci, bi = args
        t = bi * Q_BLOCK + jnp.arange(Q_BLOCK)
        s = jnp.einsum('bqhd,bkhd->bhqk', qi, k).astype(jnp.float32) * scale + (ci[..., :, None] - c[..., None, :])
        p = masked_softmax(s, kpos[None, :] <= t[:, None])
        return jnp.einsum('bhqk,bkhd->bqhd', p.astype(v.dtype), v)

    o = lax.map(block, (qb, cb, jnp.arange(nb)))
    return o.swapaxes(0, 1).reshape(bsz, s_len, GROUP)

def compress(kx, pos, w1, w2):
    s_len = kx.shape[1]
    n_cmp = (s_len - CMP_LEN) // CMP_STRIDE + 1
    idx = jnp.arange(n_cmp)[:, None] * CMP_STRIDE + jnp.arange(CMP_LEN)[None, :]
    blocks = kx[:, idx] + pos
    hid = jax.nn.gelu(jnp.einsum('bnld,ldm->bnm', blocks, w1))
    return hid @ w2

def nsa_mixer(q, kc_in, vc_in, ks_in, vs_in, kw_in, vw_in, g_logit, g_bias, qk_gain, cmp_pos, cmp_w1, cmp_w2, rel_bias):
    bsz, s_len, _ = q.shape
    h, d = NSA_HEADS, HEAD_DIM
    f32 = jnp.float32
    q = rms_norm(q.reshape(bsz, s_len, h, d), qk_gain[0])
    kc = rms_norm(compress(kc_in, cmp_pos[0], cmp_w1[0], cmp_w2[0]), qk_gain[1])
    vc = compress(vc_in, cmp_pos[1], cmp_w1[1], cmp_w2[1])
    ks_ = rms_norm(ks_in, qk_gain[2])
    kw = rms_norm(kw_in, qk_gain[3])
    gates = jax.nn.sigmoid(g_logit + g_bias).reshape(bsz, s_len, 3, h)
    n_cmp = kc.shape[1]
    n_slc = s_len // SLC_BLOCK
    top = min(SLC_TOPK, n_slc)
    cmp_start = jnp.arange(n_cmp) * CMP_STRIDE
    cmp_end = cmp_start + CMP_LEN - 1
    slc_start = jnp.arange(n_slc) * SLC_BLOCK
    overlap = jnp.clip(jnp.minimum(cmp_start[:, None] + CMP_LEN, slc_start[None, :] + SLC_BLOCK)
                       - jnp.maximum(cmp_start[:, None], slc_start[None, :]), 0, CMP_LEN).astype(f32)
    ks_blk = ks_.reshape(bsz, n_slc, SLC_BLOCK, d)
    vs_blk = vs_in.reshape(bsz, n_slc, SLC_BLOCK, d)
    kw_pad = jnp.pad(kw, ((0, 0), (WINDOW, 0), (0, 0)))
    vw_pad = jnp.pad(vw_in, ((0, 0), (WINDOW, 0), (0, 0)))
    nb = s_len // Q_BLOCK
    qb = q.reshape(bsz, nb, Q_BLOCK, h, d).swapaxes(0, 1)
    gb = gates.reshape(bsz, nb, Q_BLOCK, 3, h).swapaxes(0, 1)
    bidx = jnp.arange(bsz)[:, None, None]
    jblk = jnp.arange(n_slc)
    scale = HEAD_DIM ** -0.5

    def block(args):
        qi, gi, bi = args
        t = bi * Q_BLOCK + jnp.arange(Q_BLOCK)
        dist_c = t[:, None] - cmp_end[None, :]
        s_c = (jnp.einsum('bqhd,bnd->bhqn', qi, kc).astype(f32) * scale
               + rel_bias[rel_bucket(dist_c)].transpose(2, 0, 1))
        p_c = masked_softmax(s_c, dist_c >= 0)
        o_c = jnp.einsum('bhqn,bnd->bqhd', p_c.astype(vc.dtype), vc)
        imp = jnp.einsum('bhqn,nm->bqm', p_c, overlap)
        cur = t // SLC_BLOCK
        forced = (jblk[None, :] == 0) | (jblk[None, :] == cur[:, None]) | (jblk[None, :] == cur[:, None] - 1)
        imp = jnp.where(forced, BIG, imp)
        imp = jnp.where(jblk[None, :] <= cur[:, None], imp, -jnp.inf)
        _, sel = lax.top_k(imp, top)
        k_sel = ks_blk[bidx, sel].reshape(bsz, Q_BLOCK, top * SLC_BLOCK, d)
        v_sel = vs_blk[bidx, sel].reshape(bsz, Q_BLOCK, top * SLC_BLOCK, d)
        pos_sel = (sel[..., None] * SLC_BLOCK + jnp.arange(SLC_BLOCK)).reshape(bsz, Q_BLOCK, top * SLC_BLOCK)
        dist_s = t[None, :, None] - pos_sel
        s_s = (jnp.einsum('bqhd,bqnd->bhqn', qi, k_sel).astype(f32) * scale
               + rel_bias[rel_bucket(dist_s)].transpose(0, 3, 1, 2))
        p_s = masked_softmax(s_s, (dist_s >= 0)[:, None])
        o_s = jnp.einsum('bhqn,bqnd->bqhd', p_s.astype(v_sel.dtype), v_sel)
        k_win = lax.dynamic_slice_in_dim(kw_pad, bi * Q_BLOCK, WINDOW + Q_BLOCK, axis=1)
        v_win = lax.dynamic_slice_in_dim(vw_pad, bi * Q_BLOCK, WINDOW + Q_BLOCK, axis=1)
        pos_w = bi * Q_BLOCK - WINDOW + jnp.arange(WINDOW + Q_BLOCK)
        dist_w = t[:, None] - pos_w[None, :]
        mask_w = (dist_w >= 0) & (dist_w < WINDOW) & (pos_w[None, :] >= 0)
        s_w = (jnp.einsum('bqhd,bnd->bhqn', qi, k_win).astype(f32) * scale
               + rel_bias[rel_bucket(dist_w)].transpose(2, 0, 1))
        p_w = masked_softmax(s_w, mask_w)
        o_w = jnp.einsum('bhqn,bnd->bqhd', p_w.astype(v_win.dtype), v_win)
        return gi[:, :, 0, :, None] * o_c + gi[:, :, 1, :, None] * o_s + gi[:, :, 2, :, None] * o_w

    o = lax.map(block, (qb, gb, jnp.arange(nb)))
    return o.swapaxes(0, 1).reshape(bsz, s_len, GROUP)

def first_inputs(seed: int = 0) -> dict:
    key = jax.random.key(seed)
    ks = jax.random.split(key, 24)
    f32 = jnp.float32
    nl = DEPTH

    def nrm(k, shape, scale):
        return jax.random.normal(k, shape, f32) * scale

    u = jax.random.uniform(ks[7], (nl, GROUP), f32, 0.9, 0.999)
    return {
        'x': jax.random.normal(ks[0], (BATCH, SEQ, D_MODEL), f32),
        'norm_mix': 1.0 + nrm(ks[1], (nl, D_MODEL), 0.02),
        'w_in': nrm(ks[2], (nl, D_MODEL, N_IN), D_MODEL ** -0.5),
        'lru_conv_w': nrm(ks[3], (nl, LRU_CONV, GROUP), LRU_CONV ** -0.5),
        'lru_conv_b': nrm(ks[4], (nl, GROUP), 0.02),
        'lru_w_gates': nrm(ks[5], (nl, 2, LRU_BLOCKS, LRU_BLOCK_DIM, LRU_BLOCK_DIM), LRU_BLOCK_DIM ** -0.5),
        'lru_b_gates': nrm(ks[6], (nl, 2, GROUP), 0.02),
        'lru_lambda': jnp.log(u) - jnp.log1p(-u),
        'sc_conv_w': nrm(ks[8], (nl, SC_CONV, GROUP), SC_CONV ** -0.5),
        'fox_f_bias': 3.0 + nrm(ks[9], (nl, FOX_HEADS), 0.1),
        'fox_qk_norm': 1.0 + nrm(ks[10], (nl, 2, HEAD_DIM), 0.02),
        'nsa_qk_norm': 1.0 + nrm(ks[11], (nl, 4, HEAD_DIM), 0.02),
        'nsa_cmp_pos': nrm(ks[12], (nl, 2, CMP_LEN, HEAD_DIM), 0.1),
        'nsa_cmp_w1': nrm(ks[13], (nl, 2, CMP_LEN, HEAD_DIM, CMP_HIDDEN), (CMP_LEN * HEAD_DIM) ** -0.5),
        'nsa_cmp_w2': nrm(ks[14], (nl, 2, CMP_HIDDEN, HEAD_DIM), CMP_HIDDEN ** -0.5),
        'nsa_gate_bias': nrm(ks[15], (nl, 3 * NSA_HEADS), 0.02),
        'rel_bias': nrm(ks[16], (REL_BUCKETS, NSA_HEADS), 0.2),
        'out_norm': 1.0 + nrm(ks[17], (nl, N_GROUPS, GROUP), 0.02),
        'w_out': nrm(ks[18], (nl, D_MIX, D_MODEL), D_MIX ** -0.5),
        'norm_ffn': 1.0 + nrm(ks[19], (nl, D_MODEL), 0.02),
        'w_gate_up': nrm(ks[20], (nl, D_MODEL, 2 * D_FF), D_MODEL ** -0.5),
        'w_down': nrm(ks[21], (nl, D_FF, D_MODEL), D_FF ** -0.5),
    }

def first_block(x, norm_mix, w_in, lru_conv_w, lru_conv_b, lru_w_gates, lru_b_gates, lru_lambda, sc_conv_w,
              fox_f_bias, fox_qk_norm, nsa_qk_norm, nsa_cmp_pos, nsa_cmp_w1, nsa_cmp_w2, nsa_gate_bias,
              rel_bias, out_norm, w_out, norm_ffn, w_gate_up, w_down):
    for l in range(DEPTH):
        z = rms_norm(x, norm_mix[l]) @ w_in[l]
        y_a = rg_lru_mixer(cols(z, C_LRU_X, GROUP), cols(z, C_LRU_G, GROUP), lru_conv_w[l], lru_conv_b[l],
                           lru_w_gates[l], lru_b_gates[l], lru_lambda[l])
        y_b = short_conv_mixer(cols(z, C_SC_B, GROUP), cols(z, C_SC_C, GROUP), cols(z, C_SC_X, GROUP), sc_conv_w[l])
        y_c = fox_mixer(cols(z, C_FOX_Q, GROUP), cols(z, C_FOX_K, GROUP), cols(z, C_FOX_V, GROUP),
                        cols(z, C_FOX_F, FOX_HEADS), fox_f_bias[l], fox_qk_norm[l])
        kv = [cols(z, C_NSA_KV + j * HEAD_DIM, HEAD_DIM) for j in range(6)]
        y_d = nsa_mixer(cols(z, C_NSA_Q, GROUP), kv[0], kv[1], kv[2], kv[3], kv[4], kv[5],
                        cols(z, C_NSA_G, 3 * NSA_HEADS), nsa_gate_bias[l], nsa_qk_norm[l],
                        nsa_cmp_pos[l], nsa_cmp_w1[l], nsa_cmp_w2[l], rel_bias)
        mixed = jnp.concatenate([rms_norm(y_a, out_norm[l, 0]), rms_norm(y_b, out_norm[l, 1]),
                                 rms_norm(y_c, out_norm[l, 2]), rms_norm(y_d, out_norm[l, 3])], axis=-1)
        x = x + mixed @ w_out[l]
        gu = rms_norm(x, norm_ffn[l]) @ w_gate_up[l]
        x = x + (jax.nn.silu(gu[..., :D_FF]) * gu[..., D_FF:]) @ w_down[l]
    return x


DEPTH_2 = 4

N_MIXERS = 3
GRID_W = 64
EPS = 1e-6
CONV_WIDTH = 31
NAT_HEADS = 16
NAT_HEAD_DIM = D_MODEL // NAT_HEADS
NAT_MAX_KH = 8
NAT_KW = 16
RET_HEADS = 4
RET_KEY_DIM = D_MODEL // RET_HEADS
RET_VAL_DIM = 2 * RET_KEY_DIM
RET_CHUNK = 128
RET_ROPE_BASE = 10000.0
FFN_DIM = ((8 * D_MODEL // 3 + 127) // 128) * 128
FFN_CONV_WIDTH = 3
N_CONV_LAYERS = (DEPTH_2 + 2) // 3
N_NAT_LAYERS = (DEPTH_2 + 1) // 3
N_RET_LAYERS = DEPTH_2 // 3


def rmsnorm(x, g):
    xf = x.astype(jnp.float32)
    y = xf * lax.rsqrt(jnp.mean(xf * xf, axis=-1, keepdims=True) + EPS)
    return y.astype(x.dtype) * g

def layernorm(x, g, b):
    xf = x.astype(jnp.float32)
    mu = jnp.mean(xf, axis=-1, keepdims=True)
    var = jnp.mean(jnp.square(xf - mu), axis=-1, keepdims=True)
    y = (xf - mu) * lax.rsqrt(var + EPS)
    return y.astype(x.dtype) * g + b

def dwconv(x, w, b):
    k, c = w.shape
    y = lax.conv_general_dilated(
        x, w[:, None, :].astype(x.dtype), window_strides=(1,),
        padding=[(k // 2, k // 2)], dimension_numbers=('NWC', 'WIO', 'NWC'),
        feature_group_count=c)
    return y + b

def conv_module(h, w_in, b_in, dw_w, dw_b, ln_g, ln_b, w_out):
    a, gt = jnp.split(h @ w_in + b_in, 2, axis=-1)
    u = a * jax.nn.sigmoid(gt)
    u = dwconv(u, dw_w, dw_b)
    u = layernorm(u, ln_g, ln_b)
    return jax.nn.silu(u) @ w_out

def nat_mixer(h, w_qkv, q_g, k_g, rpb, w_out):
    b, s, _ = h.shape
    rows = s // GRID_W
    kh = min(NAT_MAX_KH, rows)
    qkv = (h @ w_qkv).reshape(b, s, 3, NAT_HEADS, NAT_HEAD_DIM)
    q = rmsnorm(qkv[:, :, 0], q_g) * (NAT_HEAD_DIM ** -0.5)
    k = rmsnorm(qkv[:, :, 1], k_g)
    v = qkv[:, :, 2]

    def to_grid(t):
        return t.reshape(b, rows, GRID_W, NAT_HEADS, NAT_HEAD_DIM).transpose(0, 3, 1, 2, 4)

    qg, kg, vg = to_grid(q), to_grid(k), to_grid(v)
    cols = jnp.arange(GRID_W)
    col_start = jnp.clip(cols - NAT_KW // 2, 0, GRID_W - NAT_KW)
    col_idx = col_start[:, None] + jnp.arange(NAT_KW)[None, :]
    dc_idx = col_idx - cols[:, None] + (NAT_KW - 1)

    def row_fn(r):
        rs = jnp.clip(r - kh // 2, 0, rows - kh)
        q_r = lax.dynamic_index_in_dim(qg, r, axis=2, keepdims=False)
        k_win = lax.dynamic_slice_in_dim(kg, rs, kh, axis=2)[:, :, :, col_idx]
        v_win = lax.dynamic_slice_in_dim(vg, rs, kh, axis=2)[:, :, :, col_idx]
        dr_idx = rs + jnp.arange(kh) - r + (NAT_MAX_KH - 1)
        bias = rpb[:, dr_idx[:, None, None], dc_idx[None, :, :]]
        sc = jnp.einsum('bhqd,bhrqwd->bhqrw', q_r, k_win).astype(jnp.float32)
        sc = sc + bias.transpose(0, 2, 1, 3)[None].astype(jnp.float32)
        p = jax.nn.softmax(sc.reshape(b, NAT_HEADS, GRID_W, kh * NAT_KW), axis=-1)
        p = p.reshape(b, NAT_HEADS, GRID_W, kh, NAT_KW).astype(v_win.dtype)
        return jnp.einsum('bhqrw,bhrqwd->bhqd', p, v_win)

    out = lax.map(row_fn, jnp.arange(rows))
    out = out.transpose(1, 0, 3, 2, 4).reshape(b, s, D_MODEL)
    return out @ w_out

def rotary(x):
    s, d = x.shape[1], x.shape[-1]
    half = d // 2
    theta = 1.0 / (RET_ROPE_BASE ** jnp.linspace(0.0, 1.0, half, dtype=jnp.float32))
    ang = jnp.arange(s, dtype=jnp.float32)[:, None] * theta[None, :]
    cos, sin = jnp.cos(ang)[:, None, :], jnp.sin(ang)[:, None, :]
    x1, x2 = x[..., :half].astype(jnp.float32), x[..., half:].astype(jnp.float32)
    return jnp.concatenate([x1 * cos - x2 * sin, x1 * sin + x2 * cos], axis=-1)

def retention_scan(q, k, v, log_gamma, include_diag):
    b, h, s, dk = q.shape
    dv = v.shape[-1]
    nc = s // RET_CHUNK

    def chunks(t):
        return jnp.moveaxis(t.reshape(b, h, nc, RET_CHUNK, t.shape[-1]), 2, 0)

    pos = jnp.arange(RET_CHUNK, dtype=jnp.float32)
    diff = pos[:, None] - pos[None, :]
    mask = (diff >= 0) if include_diag else (diff > 0)
    expo = jnp.where(mask, diff, 0.0)[None] * log_gamma[:, None, None]
    decay_intra = jnp.where(mask[None], jnp.exp(expo), 0.0)
    q_decay = jnp.exp((pos + 1.0)[None, :] * log_gamma[:, None])
    k_decay = jnp.exp((RET_CHUNK - 1.0 - pos)[None, :] * log_gamma[:, None])
    chunk_decay = jnp.exp(RET_CHUNK * log_gamma)

    def step(state, inp):
        qc, kc, vc = inp
        inter = jnp.einsum('bhcd,bhde->bhce', qc, state) * q_decay[None, :, :, None]
        sc = jnp.einsum('bhid,bhjd->bhij', qc, kc) * decay_intra[None]
        out = inter + jnp.einsum('bhij,bhje->bhie', sc, vc)
        state = state * chunk_decay[None, :, None, None] + jnp.einsum(
            'bhjd,bhje->bhde', kc * k_decay[None, :, :, None], vc)
        return state, out

    state0 = jnp.zeros((b, h, dk, dv), jnp.float32)
    _, outs = lax.scan(step, state0, (chunks(q), chunks(k), chunks(v)))
    return jnp.moveaxis(outs, 0, 2).reshape(b, h, s, dv)

def retention_mixer(h, w_in, log2_inv_decay, gn_g, w_out):
    b, s, _ = h.shape
    hk = RET_HEADS * RET_KEY_DIM
    hv = RET_HEADS * RET_VAL_DIM
    q, k, v, g = jnp.split(h @ w_in, [hk, 2 * hk, 2 * hk + hv], axis=-1)
    q = rotary(q.reshape(b, s, RET_HEADS, RET_KEY_DIM)).transpose(0, 2, 1, 3)
    k = (rotary(k.reshape(b, s, RET_HEADS, RET_KEY_DIM)) * (RET_KEY_DIM ** -0.5)).transpose(0, 2, 1, 3)
    v = v.reshape(b, s, RET_HEADS, RET_VAL_DIM).transpose(0, 2, 1, 3).astype(jnp.float32)
    log_gamma = jnp.log1p(-jnp.exp2(-log2_inv_decay.astype(jnp.float32)))
    o_fwd = retention_scan(q, k, v, log_gamma[0], True)
    o_bwd = jnp.flip(retention_scan(jnp.flip(q, 2), jnp.flip(k, 2), jnp.flip(v, 2),
                                    log_gamma[1], False), 2)
    o = (o_fwd + o_bwd).transpose(0, 2, 1, 3)
    mu = jnp.mean(o, axis=-1, keepdims=True)
    var = jnp.mean(jnp.square(o - mu), axis=-1, keepdims=True)
    o = ((o - mu) * lax.rsqrt(var + EPS)).reshape(b, s, hv).astype(h.dtype) * gn_g
    return (jax.nn.silu(g) * o) @ w_out

def conv_ffn(h, w_up, dw_w, dw_b, w_down):
    u = dwconv(h @ w_up, dw_w, dw_b)
    val, gate = jnp.split(u, 2, axis=-1)
    return (jax.nn.gelu(gate) * val) @ w_down

def second_inputs(seed: int = 0) -> dict:
    key = jax.random.key(seed)
    ks = iter(jax.random.split(key, 32))
    f32 = jnp.float32
    D = D_MODEL

    def nrm(shape, scale):
        return jax.random.normal(next(ks), shape, f32) * scale

    def gain(shape):
        return 1.0 + nrm(shape, 0.02)

    ret_in = 2 * RET_HEADS * RET_KEY_DIM + 2 * RET_HEADS * RET_VAL_DIM
    hv = RET_HEADS * RET_VAL_DIM
    decay_base = 5.0 + jnp.arange(RET_HEADS, dtype=f32)
    return {
        'x': nrm((BATCH, SEQ, D), 1.0),
        'norm1_g': gain((DEPTH_2, D)),
        'norm2_g': gain((DEPTH_2, D)),
        'conv_w_in': nrm((N_CONV_LAYERS, D, 2 * D), D ** -0.5),
        'conv_b_in': nrm((N_CONV_LAYERS, 2 * D), 0.02),
        'conv_dw_w': nrm((N_CONV_LAYERS, CONV_WIDTH, D), CONV_WIDTH ** -0.5),
        'conv_dw_b': nrm((N_CONV_LAYERS, D), 0.02),
        'conv_ln_g': gain((N_CONV_LAYERS, D)),
        'conv_ln_b': nrm((N_CONV_LAYERS, D), 0.02),
        'conv_w_out': nrm((N_CONV_LAYERS, D, D), D ** -0.5),
        'nat_w_qkv': nrm((N_NAT_LAYERS, D, 3 * D), D ** -0.5),
        'nat_q_norm_g': gain((N_NAT_LAYERS, NAT_HEAD_DIM)),
        'nat_k_norm_g': gain((N_NAT_LAYERS, NAT_HEAD_DIM)),
        'nat_rpb': nrm((N_NAT_LAYERS, NAT_HEADS, 2 * NAT_MAX_KH - 1, 2 * NAT_KW - 1), 0.02),
        'nat_w_out': nrm((N_NAT_LAYERS, D, D), D ** -0.5),
        'ret_w_in': nrm((N_RET_LAYERS, D, ret_in), D ** -0.5),
        'ret_log2_inv_decay': decay_base[None, None, :] + nrm((N_RET_LAYERS, 2, RET_HEADS), 0.1),
        'ret_gn_g': gain((N_RET_LAYERS, hv)),
        'ret_w_out': nrm((N_RET_LAYERS, hv, D), hv ** -0.5),
        'ffn_w_up': nrm((DEPTH_2, D, 2 * FFN_DIM), D ** -0.5),
        'ffn_dw_w': nrm((DEPTH_2, FFN_CONV_WIDTH, 2 * FFN_DIM), FFN_CONV_WIDTH ** -0.5),
        'ffn_dw_b': nrm((DEPTH_2, 2 * FFN_DIM), 0.02),
        'ffn_w_down': nrm((DEPTH_2, FFN_DIM, D), FFN_DIM ** -0.5),
    }

def second_block(x, norm1_g, norm2_g, conv_w_in, conv_b_in, conv_dw_w, conv_dw_b,
              conv_ln_g, conv_ln_b, conv_w_out, nat_w_qkv, nat_q_norm_g,
              nat_k_norm_g, nat_rpb, nat_w_out, ret_w_in, ret_log2_inv_decay,
              ret_gn_g, ret_w_out, ffn_w_up, ffn_dw_w, ffn_dw_b, ffn_w_down):
    for i in range(DEPTH_2):
        mixer, j = i % N_MIXERS, i // N_MIXERS
        h = rmsnorm(x, norm1_g[i])
        if mixer == 0:
            y = conv_module(h, conv_w_in[j], conv_b_in[j], conv_dw_w[j], conv_dw_b[j],
                            conv_ln_g[j], conv_ln_b[j], conv_w_out[j])
        elif mixer == 1:
            y = nat_mixer(h, nat_w_qkv[j], nat_q_norm_g[j], nat_k_norm_g[j],
                          nat_rpb[j], nat_w_out[j])
        else:
            y = retention_mixer(h, ret_w_in[j], ret_log2_inv_decay[j], ret_gn_g[j],
                                ret_w_out[j])
        x = x + y.astype(x.dtype)
        h = rmsnorm(x, norm2_g[i])
        x = x + conv_ffn(h, ffn_w_up[i], ffn_dw_w[i], ffn_dw_b[i], ffn_w_down[i]).astype(x.dtype)
    return x


def setup_inputs(seed=0):
    out = dict(first_inputs(seed))
    for name, value in second_inputs(seed + 1).items():
        if name != "x":
            out[name + "_2"] = value
    return out


def reference(
    x, norm_mix, w_in, lru_conv_w, lru_conv_b, lru_w_gates, lru_b_gates, lru_lambda, sc_conv_w,
    fox_f_bias, fox_qk_norm, nsa_qk_norm, nsa_cmp_pos, nsa_cmp_w1, nsa_cmp_w2, nsa_gate_bias,
    rel_bias, out_norm, w_out, norm_ffn, w_gate_up, w_down, norm1_g_2, norm2_g_2, conv_w_in_2,
    conv_b_in_2, conv_dw_w_2, conv_dw_b_2, conv_ln_g_2, conv_ln_b_2, conv_w_out_2, nat_w_qkv_2,
    nat_q_norm_g_2, nat_k_norm_g_2, nat_rpb_2, nat_w_out_2, ret_w_in_2, ret_log2_inv_decay_2,
    ret_gn_g_2, ret_w_out_2, ffn_w_up_2, ffn_dw_w_2, ffn_dw_b_2, ffn_w_down_2,
):
    x = first_block(
        x, norm_mix, w_in, lru_conv_w, lru_conv_b, lru_w_gates, lru_b_gates, lru_lambda,
        sc_conv_w, fox_f_bias, fox_qk_norm, nsa_qk_norm, nsa_cmp_pos, nsa_cmp_w1, nsa_cmp_w2,
        nsa_gate_bias, rel_bias, out_norm, w_out, norm_ffn, w_gate_up, w_down,
    )
    return second_block(
        x, norm1_g_2, norm2_g_2, conv_w_in_2, conv_b_in_2, conv_dw_w_2, conv_dw_b_2,
        conv_ln_g_2, conv_ln_b_2, conv_w_out_2, nat_w_qkv_2, nat_q_norm_g_2, nat_k_norm_g_2,
        nat_rpb_2, nat_w_out_2, ret_w_in_2, ret_log2_inv_decay_2, ret_gn_g_2, ret_w_out_2,
        ffn_w_up_2, ffn_dw_w_2, ffn_dw_b_2, ffn_w_down_2,
    )


_drawn_inputs = setup_inputs


def setup_inputs(seed=0):
    import zlib

    import numpy as np

    out = dict(_drawn_inputs(seed))
    spreads = {}
    factors = {'lru_b_gates': 8.0,
     'fox_f_bias': 27.944,
     'fox_qk_norm': 4.907,
     'nsa_qk_norm': 5.835,
     'nsa_gate_bias': 8.0,
     'norm_ffn': 3.622,
     'norm1_g_2': 2.846,
     'conv_b_in_2': 3.824,
     'conv_ln_g_2': 3.867,
     'conv_ln_b_2': 3.996,
     'nat_q_norm_g_2': 8.0,
     'nat_k_norm_g_2': 8.0,
     'nat_rpb_2': 50.414,
     'ret_gn_g_2': 26.617,
     'norm2_g_2': 5.169,
     'conv_dw_b_2': 3.264,
     'ffn_dw_b_2': 5.319}
    for name, (base, spread) in spreads.items():
        noise = np.random.default_rng([zlib.crc32(name.encode()), seed]).standard_normal(out[name].shape)
        drawn = base * np.exp(spread * noise) if base else spread * noise
        out[name] = __import__('jax').numpy.asarray(drawn.astype(out[name].dtype))
    for name, factor in factors.items():
        out[name] = (out[name] * factor).astype(out[name].dtype)
    return out
```

```python
import math
from collections import deque
from contextlib import ExitStack

import numpy as np
import concourse.bass as bass
from concourse import mybir

T = 512
D = 1024
DC = 8
FFC = 22
EPS = 1e-6
NEG = -1.0e30
ML = 896
FF_PARTS = ((0, 8), (8, 15), (15, 22))
NRAW = 4
NSPLIT = 3
NTILE = 17
NPAD = 4

PARAMS = (
    ("norm_mix", 8), ("lru_conv_w", 8), ("lru_conv_b", 2), ("lru_b", 4), ("lru_lambda", 2),
    ("sc_conv_w", 6), ("fox_qk", 2), ("nsa_qk", 4), ("fg_bias", 1), ("cmp_pos", 32),
    ("out_norm", 8), ("norm_ffn", 8), ("norm1", 32), ("norm2", 32), ("conv_b_in", 32),
    ("conv_dw_w", 496), ("conv_dw_b", 16), ("conv_ln_g", 16), ("conv_ln_b", 16),
    ("nat_q", 1), ("nat_k", 1), ("ret_dec", 8), ("ret_gn", 16), ("ffn_dw_w", 528), ("ffn_dw_b", 176),
)
CONSTS = (("ident", 128), ("ones", 128), ("bones", 128), ("mask", ML), ("selneg", 512),
          ("colmask", 64), ("rowmask", 1))


def offsets(spec):
    out, at = {}, 0
    for name, n in spec:
        out[name] = at
        at += n
    return out, at


POFF, NPRM = offsets(PARAMS)
COFF, NCST = offsets(CONSTS)


def linears():
    out = [("w_in", 8, 23), ("w_out", 8, 8)]

    def ffn(name):
        for i, (a, b) in enumerate(FF_PARTS):
            out.append((f"{name}_up{i}", 8, 2 * (b - a)))
            out.append((f"{name}_down{i}", b - a, 8))

    ffn("ffn")
    for layer in range(4):
        if layer in (0, 3):
            out.append((f"conv_in{layer // 3}", 8, 16))
            out.append((f"conv_out{layer // 3}", 8, 8))
        elif layer == 1:
            out.append(("nat_qkv", 8, 24))
            out.append(("nat_out", 8, 8))
        else:
            for half in range(2):
                for h in (2 * half, 2 * half + 1):
                    out.append((f"ret_in{h}", 8, 12))
                out.append((f"ret_out{half}", 8, 8))
        ffn(f"ffn2_{layer}")
    return out


N_TILES = sum(k * m for _, k, m in linears())
N_BLOCKS = (N_TILES + 7) // 8




class Engine:

    def __init__(self, sem, linked):
        self.sem, self.linked = sem, linked
        self.ops, self.count = [], 0

    def put(self, fn, waits=(), inc=True):
        waits = [w for w in waits if w is not None]
        if self.linked and self.count:
            waits.append((self.sem, self.count))
        self.ops.append((waits, fn, inc))
        if inc:
            self.count += 1
        return (self.sem, self.count)

    def run(self, e):
        passed = {}
        for waits, fn, inc in self.ops:
            for sem, value in waits:
                if passed.get(id(sem), 0) < value:
                    passed[id(sem)] = value
                    e.wait_ge(sem, value)
            ins = fn(e)
            if inc:
                ins.then_inc(self.sem, 1)


class Ring:

    def __init__(self, aps):
        self.free = deque((ap, ()) for ap in aps)

    def get(self):
        ap, waits = self.free.popleft()
        return Buf(self, ap, waits)


class Buf:
    def __init__(self, ring, ap, waits):
        self.ring, self.ap, self.w = ring, ap, waits

    def done(self, *after):
        self.ring.free.append((self.ap, after))


def build(nc, wst, xin, prm, cst, gatew, cmpw1, cmpw2, relm, natb, rope, dist, out):
    f32 = mybir.dt.float32
    f32r = mybir.dt.float32r
    ALU = mybir.AluOpType
    ACT = mybir.ActivationFunctionType
    MUL, ADD, SUB = ALU.mult, ALU.add, ALU.subtract

    with ExitStack() as ctx:
        def sb(name, shape, dt=f32):
            return ctx.enter_context(nc.sbuf_tensor(name, shape, dt))

        def sem(name):
            return ctx.enter_context(nc.semaphore(name))

        X = sb("X", [128, 8, T])
        XH = sb("XH", [128, 8, T], f32r)
        XL = sb("XL", [128, 8, T], f32r)
        HH = sb("HH", [128, 8, T], f32r)
        HL = sb("HL", [128, 8, T], f32r)
        RAW = sb("RAW", [128, NRAW, 1024])
        WH = sb("WH", [128, NSPLIT, 1024], f32r)
        WL = sb("WL", [128, NSPLIT, 1024], f32r)
        PT = sb("PT", [128, 2, 4, T])
        BI = sb("BI", [128, 4, ML])
        PRM = sb("PRM", [128, NPRM])
        CST = sb("CST", [128, NCST])
        TT = sb("TT", [128, NTILE, T])
        PD = sb("PD", [128, NPAD, 544])
        SM = sb("SM", [128, 160])
        G8 = sb("G8", [128, 8])
        GT = sb("GT", [128, 4, 12])
        PSB = [ctx.enter_context(nc.psum_tensor(f"PS{i}", [128, T], f32)) for i in range(8)]

        V = Engine(sem("s_v"), True)
        A = Engine(sem("s_a"), True)
        P = Engine(sem("s_p"), True)
        PE = Engine(sem("s_pe"), False)
        SP = Engine(sem("s_sp"), False)
        s_raw = [sem(f"s_raw{i}") for i in range(NRAW)]
        s_x = [sem(f"s_x{k}") for k in range(8)]
        s_c2 = sem("s_c2")
        s_c = sem("s_c")
        s_w1 = sem("s_w1")
        s_w2 = sem("s_w2")
        s_bi = [sem(f"s_bi{i}") for i in range(4)]
        s_out = sem("s_out")

        def v_tt(o, a, b, op, *w):
            return V.put(lambda e: e.tensor_tensor(o, a, b, op), w)

        def v_ts(o, a, s1, s2, op0, op1, *w):
            if op1 is None:
                return V.put(lambda e: e.tensor_scalar(o, a, s1, None, op0), w)
            return V.put(lambda e: e.tensor_scalar(o, a, s1, s2, op0, op1), w)

        def v_stt(o, a, s, b, op0, op1, *w):
            return V.put(lambda e: e.scalar_tensor_tensor(o, a, s, b, op0, op1), w)

        def v_add_max(o, a, b, mx, *w):
            return V.put(lambda e: e.tensor_tensor_reduce(
                out=o, in0=a, in1=b, scale=1.0, scalar=-3.0e38, op0=ADD, op1=ALU.max, accum_out=mx), w)

        def v_copy(o, a, *w):
            return V.put(lambda e: e.tensor_copy(o, a), w)

        def v_rec(o, a, *w):
            return V.put(lambda e: e.reciprocal(o, a), w)

        def v_set(o, value, *w):
            return V.put(lambda e: e.memset(o, value), w)

        table = [None]
        LNEXP = "natural_log_exp_and_others"

        def a_act(o, a, f, *w, scale=1.0, bias=0.0, acc=None):
            if f in (ACT.Ln, ACT.Exp):
                if table[0] != LNEXP:
                    A.put(lambda e: e.preload_act_table_set(LNEXP), (), False)
                    table[0] = LNEXP
            elif f not in (ACT.Copy, ACT.Square):
                table[0] = f
            if acc is not None:
                return A.put(lambda e: e.activation(o, a, f, scale=scale, bias=bias, accum_out=acc), w)
            return A.put(lambda e: e.activation(o, a, f, scale=scale, bias=bias), w)

        def a_copy(o, a, *w):
            return A.put(lambda e: e.activation(o, a, ACT.Copy), w)

        def p_tt(o, a, b, op, *w):
            return P.put(lambda e: e.tensor_tensor(o, a, b, op), w)

        def mm(o, l, r, start, stop, *w, inc=False):
            return PE.put(lambda e: e.matmul(o, l, r, start=start, stop=stop), w, inc)

        def tr(o, a, *w, inc=False):
            return PE.put(lambda e: e.transpose(o, a, ident), w, inc)

        def load(o, a, s, *w):
            SP.put(lambda e: e.dma_start(o, a).then_inc(s, 16), w, False)

        def pcol(name, i=0):
            return PRM[:, POFF[name] + i:POFF[name] + i + 1]

        def cc(name, n):
            return CST[:, COFF[name]:COFF[name] + n]

        ident, ones, bones = cc("ident", 128), cc("ones", 128), cc("bones", 128)
        tiles = Ring([TT[:, i, :] for i in range(NTILE)])
        pads = Ring([PD[:, i, :] for i in range(NPAD)])
        banks = Ring([p[:, :] for p in PSB])
        small_at = [0]

        def small(n=1):
            if small_at[0] + n > 128:
                small_at[0] = 0
            a = small_at[0]
            small_at[0] += n
            return SM[:, a:a + n]

        eps = SM[:, 159:160]

        load(PRM[:, 0:POFF["norm1"]], prm[:, 0:POFF["norm1"]], s_c)
        load(CST[:, :], cst, s_c)
        for k in range(8):
            load(X[:, k, :], xin[k, :, :], s_x[k])

        def load_once(o, a, s, *w):
            load(o, a, s, *w)
            return (s, 16)

        CTOK = (s_c, 32)
        bi_n = [0, 0, 0, 0]

        def load_bi(slot, src, *w):
            load(BI[:, slot, 0:src.shape[-1]], src, s_bi[slot], *w)
            bi_n[slot] += 16
            return (s_bi[slot], bi_n[slot])

        lo_done, used = [], []
        at = {"tile": 0, "loaded": 0}

        def load_block():
            b = at["loaded"]
            if b < N_BLOCKS:
                load(RAW[:, b % NRAW, :], wst[b, :, :], s_raw[b % NRAW],
                     lo_done[b - NRAW] if b >= NRAW else None)
                at["loaded"] += 1

        def split_block():
            b = len(lo_done)
            raw, wh, wl = RAW[:, b % NRAW, :], WH[:, b % NSPLIT, :], WL[:, b % NSPLIT, :]
            arrived = (s_raw[b % NRAW], 16 * (b // NRAW + 1))
            hi = a_copy(wh, raw, arrived, used[b - NSPLIT] if b >= NSPLIT else None)
            lo_done.append(p_tt(wl, raw, wh.bitcast(f32), SUB, hi))
            load_block()

        def take_tile():
            b, i = divmod(at["tile"], 8)
            if i == 0:
                while len(lo_done) < min(b + NSPLIT, N_BLOCKS):
                    split_block()
            at["tile"] += 1
            s = b % NSPLIT
            last = i == 7 or at["tile"] == N_TILES
            return (WH[:, s, 128 * i:128 * i + 128], WL[:, s, 128 * i:128 * i + 128], lo_done[b], last)

        for _ in range(NRAW):
            load_block()
        load(PRM[:, POFF["norm1"]:NPRM], prm[:, POFF["norm1"]:NPRM], s_c2)
        C2TOK = (s_c2, 16)

        bg = deque()

        def later(fn):
            bg.append(fn)

        def flush(n=10 ** 9):
            while bg and n > 0:
                bg.popleft()()
                n -= 1

        def linear(mv, mc, evac, mid=None, pace=0):
            kc = len(mv)
            for m in range(mc):
                bank = banks.get()
                for k in range(kc):
                    wh, wl, wtok, last = take_tile()
                    h, l, tok = mv[k]
                    w = (*bank.w, wtok, tok) if k == 0 else (wtok, tok)
                    mm(bank.ap, wh, h, k == 0, False, *w)
                    mm(bank.ap, wh, l, False, False)
                    t = mm(bank.ap, wl, h, False, k == kc - 1, inc=last or k == kc - 1)
                    if last:
                        used.append(t)
                    if pace and k % pace == pace - 1:
                        flush(1)
                if m == 0 and mid is not None:
                    mid()
                if not pace:
                    flush()
                evac(m, bank, t)

        def split_to(k, src, tok, buf=None):
            hi = a_copy(HH[:, k, :], src, tok)
            lo = p_tt(HL[:, k, :], src, HH[:, k, :].bitcast(f32), SUB, hi)
            if buf is not None:
                buf.done(lo)
            return (HH[:, k, :], HL[:, k, :], lo)

        def new_norm(name, first=0):
            return {"gain": lambda k: pcol(name, first + k), "mv": []}

        def norm_chunk(n, k, *x_done):
            g = n["gain"](k)
            x = X[:, k, :]
            v_ts(XH[:, k, :], x, g, None, MUL, None, *x_done)
            lo = v_stt(XL[:, k, :], x, g, XH[:, k, :].bitcast(f32), MUL, SUB)
            n["mv"].append((XH[:, k, :], XL[:, k, :], lo))
            if k == 0:
                n["sq"] = tiles.get()
                n["sq_done"] = a_act(n["sq"].ap, x, ACT.Square, *n["sq"].w, *x_done)
            else:
                s = tiles.get()
                squared = a_act(s.ap, x, ACT.Square, *s.w, *x_done)
                n["sq_done"] = v_tt(n["sq"].ap, n["sq"].ap, s.ap, ADD, squared, n["sq_done"])
                s.done(n["sq_done"])

        def norm_stats(n):
            n["rs"] = tiles.get()
            n["rs_done"] = rsqrt_of(n["rs"], n["sq"], n["sq_done"], ones, D)

        def norm_end(n):
            n["rs"].done((V.sem, V.count))

        def rsqrt_of(rs, acc, tok, mat, n):
            bank = banks.get()
            t = mm(bank.ap, mat, acc.ap, True, True, tok, *bank.w, inc=True)
            acc.done(t)
            t = a_act(rs.ap, bank.ap, ACT.Ln, t, *rs.w, eps_tok, scale=1.0 / n, bias=eps)
            bank.done(t)
            return a_act(rs.ap, rs.ap, ACT.Exp, scale=-0.5)

        def add_x(bank, m, tok):
            t = v_tt(X[:, m, :], bank.ap, X[:, m, :], ADD, tok)
            bank.done(t)
            return t

        def scaled(dst, bank, norm, tok, *w):
            t = v_tt(dst, bank.ap, norm["rs"].ap, MUL, tok, norm["rs_done"], *w)
            bank.done(t)
            return t

        def head_norm(buf, tok, gain):
            got = []
            s = tiles.get()
            t = a_act(s.ap, buf.ap, ACT.Square, tok, *s.w)

            def step():
                r = tiles.get()
                q = rsqrt_of(r, s, t, bones, 64)
                got.append(v_stt(buf.ap, buf.ap, gain, r.ap, MUL, MUL, q, tok))
                r.done(got[0])
            later(step)
            return got

        def to_tokens(src, tok, dst, *w, done=None):
            got = []

            def step():
                bank = banks.get()
                for b in range(4):
                    t = tr(bank.ap[:, 128 * b:128 * b + 128], src[:, 128 * b:128 * b + 128],
                           tok, *bank.w, inc=b == 3)
                t2 = a_copy(dst, bank.ap, t, *w)
                bank.done(t2)
                got.append(t2)
                if done is not None:
                    done(t)
            later(step)
            return got

        pt_free = [(), ()]
        pt_at = [0]

        def head(q, k, v, qk_done, v_done, bias, bias_done, causal, out, start, stop, gate=None,
                 extra=None, after=None, bias2d=False):
            return dict(q=q, k=k, v=v, qk_done=qk_done, v_done=v_done, bias=bias, bias_done=bias_done,
                        causal=causal, out=out, start=start, stop=stop, gate=gate, extra=extra,
                        after=after, bias2d=bias2d)

        def scores(hd, u):
            W = 128 * (u + 1) if hd["causal"] else T
            bank = banks.get()
            s = tiles.get()
            ex = hd["extra"]
            t = mm(bank.ap[:, 0:W], hd["q"][:, 128 * u:128 * u + 128], hd["k"][:, 0:W], True, ex is None,
                   *(x[0] for x in hd["qk_done"]), *bank.w, inc=ex is None)
            if ex is not None:
                t = mm(bank.ap[:, 0:W], ex[0], ex[1][:, 0:W], False, True, ex[2], inc=True)
            mx, nm, sm, rc = small(), small(), small(), small()
            b = hd["bias"](u)
            sap, bap = s.ap[:, 0:W], bank.ap[:, 0:W]
            if hd["bias2d"]:
                sap = sap.rearrange("p (a b) -> p a b", b=64)
                bap = bap.rearrange("p (a b) -> p a b", b=64)
            t = v_add_max(sap, bap, b, mx, t, hd["bias_done"](), *s.w)
            bank.done(t)
            t = v_ts(nm, mx, -1.0, None, MUL, None)
            t = a_act(s.ap[:, 0:W], s.ap[:, 0:W], ACT.Exp, t, bias=nm, acc=sm)
            return (W, s, sm, rc, t)

        def normalise(hd, u, W, s, sm, rc, exp_done):
            v_rec(rc, sm, exp_done)
            if hd["gate"] is None:
                t = v_ts(s.ap[:, 0:W], s.ap[:, 0:W], rc, None, MUL, None)
            else:
                t = v_ts(s.ap[:, 0:W], s.ap[:, 0:W], rc, hd["gate"](u), MUL, MUL, st["gt"])
            return (W, s, t)

        def turn(u, W, s, p_done, pt, pt_ok):
            n = W // 128
            bank = banks.get()
            for j in range(n):
                t = tr(bank.ap[:, 128 * j:128 * j + 128], s.ap[:, 128 * j:128 * j + 128], p_done,
                       *bank.w, inc=j == n - 1)
            s.done(t)
            t = a_copy(PT[:, pt, 0:n, 128 * u:128 * u + 128],
                       bank.ap[:, 0:W].rearrange("p (a b) -> p a b", b=128), t, *pt_ok)
            bank.done(t)
            return t

        def values(hd, pt, pt_done):
            out, out_ok = hd["out"]()
            for j in range(4):
                a = 128 * j if hd["causal"] else 0
                t = mm(out[:, a:T], hd["v"](j), PT[:, pt, j, a:T], hd["start"] and j == 0,
                       hd["stop"] and j == 3, pt_done, *(x[0] for x in hd["v_done"]), *out_ok, inc=j == 3)
            return t

        def attend(heads):
            units = [(n, u) for n in range(len(heads)) for u in range(4)]
            flight, turned, pend = {}, {}, []

            def value_step(n, pt, t):
                def f():
                    done = values(heads[n], pt, t)
                    pt_free[pt] = (done,)
                    if heads[n]["after"] is not None:
                        heads[n]["after"](done)
                return f

            def step(i):
                def f():
                    ready = list(pend)
                    pend.clear()
                    if i < len(units):
                        n, u = units[i]
                        flight[i] = scores(heads[n], u)
                    if 0 <= i - 1 < len(units):
                        n, u = units[i - 1]
                        flight[i - 1] = normalise(heads[n], u, *flight[i - 1])
                    if 0 <= i - 2 < len(units):
                        n, u = units[i - 2]
                        if u == 0:
                            turned[n] = (pt_at[0] % 2, pt_free[pt_at[0] % 2])
                            pt_at[0] += 1
                        pt, pt_ok = turned[n]
                        t = turn(u, *flight.pop(i - 2), pt, pt_ok)
                        if u == 3:
                            pend.append(value_step(n, pt, t))
                    for fn in ready:
                        fn()
                return f
            for i in range(len(units) + 3):
                later(step(i))

        v_set(eps, EPS)
        v_set(PD[:, :, :], 0.0)
        eps_tok = (V.sem, V.count)
        pads_tok = eps_tok
        lam = PRM[:, POFF["lru_lambda"]:POFF["lru_lambda"] + 2]
        c_ab, c_e, c_u, c_l, c_w, c_L, c_NL = (SM[:, 128 + 2 * i:130 + 2 * i] for i in range(7))

        def log1p_of(o, e_, sign, u, l, w_, tok):
            t = v_ts(u, e_, sign, 1.0, MUL, ADD, tok)
            t2 = a_act(l, u, ACT.Ln, t)
            v_ts(w_, u, 1.0, 1e-30, SUB, ADD)
            v_rec(w_, w_)
            v_ts(l, l, 1e-30, None, ADD, None, t2)
            v_tt(l, l, w_, MUL)
            v_tt(l, l, e_, MUL)
            return v_ts(o, l, sign, None, MUL, None)

        v_stt(c_ab, lam, -1.0, lam, MUL, ALU.max, CTOK)
        t = (V.sem, V.count)
        t = a_act(c_e, c_ab, ACT.Exp, t, scale=-1.0)
        log1p_of(c_L, c_e, 1.0, c_u, c_l, c_w, t)
        v_ts(c_u, lam, -1.0, 0.0, MUL, ALU.max)
        v_tt(c_L, c_L, c_u, ADD)
        v_ts(c_NL, c_L, 8.0, None, MUL, None)
        lam_tok = v_ts(c_L, c_L, -8.0, None, MUL, None)
        for i, src in enumerate((pcol("fox_qk"), pcol("nsa_qk"))):
            v_ts(G8[:, i:i + 1], src, 0.125, None, MUL, None)

        norm = new_norm("norm_mix")
        for k in range(8):
            norm_chunk(norm, k, (s_x[k], 16), CTOK)
        ys = {}
        n_mix = norm
        mixed = [None] * 8

        def out_norm(g, bufs, toks):
            acc = tiles.get()
            s = tiles.get()
            a_act(acc.ap, bufs[0].ap, ACT.Square, toks[0], *acc.w)
            t = a_act(s.ap, bufs[1].ap, ACT.Square, toks[1], *s.w)
            t = v_tt(acc.ap, acc.ap, s.ap, ADD, t)
            s.done(t)

            def step():
                r = tiles.get()
                q = rsqrt_of(r, acc, t, ones, 256)
                for c in range(2):
                    t3 = v_stt(bufs[c].ap, bufs[c].ap, pcol("out_norm", 2 * g + c), r.ap, MUL, MUL,
                               q, toks[c])
                    mixed[2 * g + c] = split_to(2 * g + c, bufs[c].ap, t3, bufs[c])
                r.done(t3)
            later(step)

        GW = BI[:, 3, 0:512]
        gw_tok = load_bi(3, gatew)
        st = {}

        def conv_taps(o, src, name, c, nch, taps, width, bias, *w):
            last = taps - 1
            if bias is None:
                t = v_ts(o, src[:, last:last + T], pcol(name, last * nch + c), None, MUL, None, *w)
            else:
                t = v_ts(o, src[:, last:last + T], pcol(name, last * nch + c), bias, MUL, ADD, *w)
            for j in range(last - 1, -1, -1):
                t = v_stt(o, src[:, j:j + T], pcol(name, j * nch + c), o, MUL, ADD)
            return t

        def lru_in(c, bank, tok):
            pad = pads.get()
            t = v_set(pad.ap[:, 0:3], 0.0, *pad.w)
            t = scaled(pad.ap[:, 3:515], bank, n_mix, tok)
            xc = tiles.get()
            t = conv_taps(xc.ap, pad.ap, "lru_conv_w", c, 2, 4, T, pcol("lru_conv_b", c), *xc.w)
            pad.done(t)
            r, i = tiles.get(), tiles.get()

            def step():
                b0, b1 = banks.get(), banks.get()
                t0 = mm(b0.ap, GW[:, 128 * c:128 * c + 128], xc.ap, True, True, t, gw_tok, *b0.w,
                        inc=True)
                t1 = mm(b1.ap, GW[:, 256 + 128 * c:384 + 128 * c], xc.ap, True, True, *b1.w, inc=True)
                t0 = a_act(r.ap, b0.ap, ACT.Sigmoid, t0, *r.w, bias=pcol("lru_b", c))
                b0.done(t0)
                t1 = a_act(i.ap, b1.ap, ACT.Sigmoid, t1, *i.w, bias=pcol("lru_b", 2 + c))
                b1.done(t1)
                th = tiles.get()
                t2 = a_act(th.ap, r.ap, ACT.Tanh, lam_tok, *th.w, scale=c_NL[:, c:c + 1])
                ta = a_act(r.ap, r.ap, ACT.Exp, scale=c_L[:, c:c + 1])
                v_tt(i.ap, i.ap, xc.ap, MUL, t1)
                v_ts(xc.ap, th.ap, 1.0, None, ADD, None, t2)
                v_rec(xc.ap, xc.ap)
                tq = v_stt(th.ap, th.ap, 2.0, xc.ap, MUL, MUL)
                tq = a_act(th.ap, th.ap, ACT.Sqrt, tq)
                v_tt(i.ap, i.ap, th.ap, MUL, tq)
                th.done((V.sem, V.count))
                t3 = V.put(lambda e: e.tensor_tensor_scan(xc.ap, r.ap, i.ap, 0.0, MUL, ADD), (ta,))
                r.done(t3)
                i.done(t3)
                st["h", c] = (xc, t3)
            later(step)

        def lru_gate(c, bank, tok):
            g = tiles.get()
            t = scaled(g.ap, bank, n_mix, tok, *g.w)
            t = a_act(g.ap, g.ap, ACT.Gelu_apprx_tanh, t)

            def step():
                h, th = st["h", c]
                t2 = v_tt(h.ap, h.ap, g.ap, MUL, t, th)
                g.done(t2)
                st["ya", c] = (h, t2)
                if c == 1:
                    out_norm(0, [st["ya", 0][0], h], [st["ya", 0][1], t2])
            later(step)

        def sc_b(c, bank, tok):
            b = tiles.get()
            st["b", c] = (b, scaled(b.ap, bank, n_mix, tok, *b.w))

        def sc_c(c, bank, tok):
            b = tiles.get()
            st["c", c] = (b, scaled(b.ap, bank, n_mix, tok, *b.w))

        def sc_x(c, bank, tok):
            pad = pads.get()
            v_set(pad.ap[:, 0:2], 0.0, *pad.w)
            scaled(pad.ap[:, 2:514], bank, n_mix, tok)
            cb = st["c", c][0]
            t = v_tt(pad.ap[:, 2:514], pad.ap[:, 2:514], cb.ap, MUL)
            t = conv_taps(cb.ap, pad.ap, "sc_conv_w", c, 2, 3, T, None)
            pad.done(t)
            bb = st["b", c][0]
            t = v_tt(cb.ap, cb.ap, bb.ap, MUL)
            bb.done(t)
            st["yb", c] = (cb, t)
            if c == 1:
                out_norm(1, [st["yb", 0][0], cb], [st["yb", 0][1], t])

        def fg(c, bank, tok):
            f = tiles.get()
            t = scaled(f.ap, bank, n_mix, tok, *f.w)
            g = tiles.get()
            tg = a_act(g.ap, f.ap, ACT.Sigmoid, t, *g.w, bias=pcol("fg_bias"))

            def gates():
                bank = banks.get()
                for b in range(4):
                    t2 = tr(bank.ap[:, 128 * b:128 * b + 128], g.ap[:, 128 * b:128 * b + 128], tg,
                            *bank.w, inc=b == 3)
                g.done(t2)
                src = bank.ap.rearrange("p (a b) -> p a b", b=128)[:, :, 32:44]
                t3 = v_copy(GT[:, :, :], src, t2)
                bank.done(t3)
                st["gt"] = v_ts(GT[:, 0, 0:4], GT[:, 0, 0:4], cc("rowmask", 1), None, MUL, None)
            later(gates)
            y, e_, u, l, w_, wt = f, *(tiles.get() for _ in range(5))
            free = [x for bb in (e_, u, l, w_, wt) for x in bb.w]
            c4 = slice(0, 4)
            v_ts(y.ap[c4], y.ap[c4], PRM[0:4, POFF["fg_bias"]:POFF["fg_bias"] + 1], None, ADD, None, tg,
                 *free)
            v_ts(w_.ap[c4], y.ap[c4], 0.0, None, ALU.min, None)
            t = v_stt(u.ap[c4], y.ap[c4], -1.0, y.ap[c4], MUL, ALU.max)
            t = a_act(e_.ap[c4], u.ap[c4], ACT.Exp, t, scale=-1.0)
            log1p_of(u.ap[c4], e_.ap[c4], 1.0, u.ap[c4], l.ap[c4], wt.ap[c4], t)
            v_tt(w_.ap[c4], w_.ap[c4], u.ap[c4], SUB)
            v_set(u.ap[c4], 1.0)
            cbuf = tiles.get()
            t = V.put(lambda e: e.tensor_tensor_scan(cbuf.ap[c4], u.ap[c4], w_.ap[c4], 0.0, MUL, ADD),
                      cbuf.w)
            for b in (y, e_, u, l, w_, wt):
                b.done(t, (A.sem, A.count))
            st["cum"] = (cbuf, t)

        mask = cc("mask", ML)

        def master(view):
            return lambda u: view[:, 384 - 128 * u:512]

        def half(ap, p):
            return ap[64 * p:64 * p + 64, :]

        def finish_pair(obank, t, g, c, key):
            y = tiles.get()
            t2 = v_copy(y.ap, obank.ap, t, *y.w)
            obank.done(t2)
            st[key, c] = (y, t2)
            if c == 1:
                out_norm(g, [st[key, 0][0], y], [st[key, 0][1], t2])

        def fox(j, bank, tok):
            c, kind = divmod(j, 3)
            b = tiles.get()
            t = scaled(b.ap, bank, n_mix, tok, *b.w)
            if kind < 2:
                got = head_norm(b, t, G8[:, 0:1] if kind == 0 else pcol("fox_qk", 1))
                st["fox", kind] = (b, got)
                return
            vt = tiles.get()
            got = to_tokens(b.ap, t, vt.ap, *vt.w, done=lambda x: b.done(x))
            q, qt = st["fox", 0]
            k, kt = st["fox", 1]
            ob = []
            cum, ctok = st["cum"]
            heads = []
            for p in range(2):
                h = 2 * c + p
                sel = CST[0:4, COFF["selneg"] + 128 * h:COFF["selneg"] + 128 * h + 128]

                def out(p=p):
                    if p == 0:
                        ob.append(banks.get())
                        return half(ob[0].ap, 0), ob[0].w
                    return half(ob[0].ap, 1), ()

                def after(t, p=p):
                    if p == 1:
                        for x in (q, k, vt):
                            x.done(t)
                        if c == 1:
                            cum.done(t)
                        finish_pair(ob[0], t, 2, c, "yc")
                heads.append(head(
                    half(q.ap, p), half(k.ap, p),
                    lambda jj, p=p: vt.ap[:, 128 * jj + 64 * p:128 * jj + 64 * p + 64], (qt, kt), (got,),
                    master(mask), lambda: CTOK, True, out, True, True, extra=(sel, cum.ap[0:4], ctok),
                    after=after))
            attend(heads)

        W1 = PT[:, :, :, :].rearrange("p a b n -> p (a b n)")

        def nsa_kv(j, bank, tok):
            b = tiles.get()
            t = scaled(b.ap, bank, n_mix, tok, *b.w)
            if j == 0:
                w1t = load_once(W1, cmpw1, s_w1, *pt_free[0], *pt_free[1])
                w2 = tiles.get()
                w2t = load_once(w2.ap[:, 0:192], cmpw2, s_w2, *w2.w)
                blk = [tiles.get(), tiles.get()]
                pos = PRM[:, POFF["cmp_pos"]:POFF["cmp_pos"] + 32]
                for i in range(2):
                    o = blk[i].ap[:, 0:496].rearrange("p (l n) -> p l n", n=31)
                    src = b.ap[:, 16 * i:16 * i + 496].rearrange("p (n l) -> p l n", l=16)
                    pp = pos[:, 16 * i:16 * i + 16].unsqueeze(2).to_broadcast([128, 16, 31])
                    tb = v_tt(o, src, pp, ADD, *blk[i].w)
                b.done(tb)

                def step():
                    hs = []
                    for br in range(2):
                        bk = banks.get()
                        for l in range(32):
                            rhs = blk[l // 16].ap[64 * br:64 * br + 64, 31 * (l % 16):31 * (l % 16) + 31]
                            th = mm(bk.ap[:, 0:31], W1[64 * br:64 * br + 64, 128 * l:128 * l + 128], rhs,
                                    l == 0, l == 31, w1t, tb, *bk.w, inc=l == 31)
                        hid = tiles.get()
                        ta = a_act(hid.ap[:, 0:31], bk.ap[:, 0:31], ACT.Gelu_apprx_tanh, th, *hid.w)
                        bk.done(ta)
                        hs.append((hid, ta))
                    for x in blk:
                        x.done(th)
                    pt_free[0] = pt_free[1] = (th,)
                    bk = banks.get()
                    tk = mm(bk.ap[:, 0:31], w2.ap[:, 0:128], hs[0][0].ap[:, 0:31], True, True, w2t,
                            hs[0][1], *bk.w, inc=True)
                    kc = tiles.get()
                    tk = v_copy(kc.ap[:, 0:31], bk.ap[:, 0:31], tk, *kc.w)
                    bk.done(tk)
                    bv = banks.get()
                    tv = mm(bv.ap[0:31, 0:64], hs[1][0].ap[:, 0:31], w2.ap[:, 128:192], True, True,
                            hs[1][1], *bv.w, inc=True)
                    vc = tiles.get()
                    tv2 = v_copy(vc.ap[0:31, 0:64], bv.ap[0:31, 0:64], tv, *vc.w)
                    bv.done(tv2)
                    w2.done(tv)
                    for x, _ in hs:
                        x.done(tv)
                    sq = tiles.get()
                    ts_ = a_act(sq.ap[:, 0:31], kc.ap[:, 0:31], ACT.Square, tk, *sq.w)
                    r = tiles.get()
                    bk = banks.get()
                    ts_ = mm(bk.ap[:, 0:31], bones, sq.ap[:, 0:31], True, True, ts_, *bk.w, inc=True)
                    sq.done(ts_)
                    ts_ = a_act(r.ap[:, 0:31], bk.ap[:, 0:31], ACT.Ln, ts_, *r.w, scale=1.0 / 64, bias=eps)
                    bk.done(ts_)
                    ts_ = a_act(r.ap[:, 0:31], r.ap[:, 0:31], ACT.Exp, scale=-0.5)
                    tk = v_stt(kc.ap[:, 0:31], kc.ap[:, 0:31], pcol("nsa_qk", 1), r.ap[:, 0:31], MUL, MUL,
                               ts_)
                    r.done(tk)
                    st["kc"] = (kc, tk)
                    st["vc"] = (vc, tv2)
                later(step)
            elif j < 3:
                st["nk", j] = (b, head_norm(b, t, pcol("nsa_qk", 1 + j)))
            else:
                vt = tiles.get()
                st["nv"] = (vt, to_tokens(b.ap, t, vt.ap, *vt.w, done=lambda x: b.done(x)))

        def nsa_q(c, bank, tok):
            b = tiles.get()
            t = scaled(b.ap, bank, n_mix, tok, *b.w)
            qt = head_norm(b, t, G8[:, 1:2])
            vt, vtok = st["nv"]
            ob = []
            heads = []

            def cmp_head(p):
                h = 2 * c + p

                def f():
                    kc, kt = st["kc"]
                    vc, vct = st["vc"]
                    pc = tiles.get()
                    hold = []
                    for u in range(4):
                        bk = banks.get()
                        s = tiles.get()
                        t1 = mm(bk.ap[:, 0:31], half(b.ap, p)[:, 128 * u:128 * u + 128],
                                half(kc.ap, p)[:, 0:31], True, True, qt[0], kt, *bk.w, inc=True)
                        mx, nm, sm, rc = small(), small(), small(), small()
                        a0 = 415 - 128 * u
                        bias = BI[:, h, a0:a0 + 481:16]
                        t1 = v_add_max(s.ap[:, 0:31], bk.ap[:, 0:31], bias, mx, t1, st["rel"], *s.w)
                        bk.done(t1)
                        t1 = v_ts(nm, mx, -1.0, None, MUL, None)
                        t1 = a_act(s.ap[:, 0:31], s.ap[:, 0:31], ACT.Exp, t1, bias=nm, acc=sm)
                        hold.append((s, sm, rc, t1))
                    bk = banks.get()
                    for u in range(4):
                        s, sm, rc, t1 = hold[u]
                        v_rec(rc, sm, t1)
                        t1 = v_ts(s.ap[:, 0:31], s.ap[:, 0:31], rc, GT[:, u, h:h + 1], MUL, MUL, st["gt"])
                        t2 = PE.put(lambda e, s=s, u=u, bk=bk: e.transpose(
                            bk.ap[0:31, 128 * u:128 * u + 128], s.ap[:, 0:31], ident), (t1, *bk.w), True)
                        s.done(t2)
                    t3 = a_copy(pc.ap[0:31, :], bk.ap[0:31, :], t2, *pc.w)
                    bk.done(t3)
                    if p == 0:
                        ob.append(banks.get())
                    t4 = mm(half(ob[0].ap, p), vc.ap[0:31, 0:64], pc.ap[0:31, :], True, False, t3, vct,
                            *(ob[0].w if p == 0 else ()), inc=True)
                    pc.done(t4)
                    if c == 1 and p == 1:
                        vc.done(t4)
                        kc.done(t4)
                return f

            for p in range(2):
                later(cmp_head(p))
                h = 2 * c + p
                for br in range(2):
                    kb, kt = st["nk", 1 + br]

                    def out(p=p):
                        return half(ob[0].ap, p), ()

                    def after(t, p=p, br=br):
                        if br == 1 and p == 1:
                            b.done(t)
                            if c == 1:
                                vt.done(t)
                                for i in (1, 2):
                                    st["nk", i][0].done(t)
                            finish_pair(ob[0], t, 3, c, "yd")
                    heads.append(head(
                        half(b.ap, p), half(kb.ap, p),
                        lambda jj, br=br: vt.ap[:, 128 * jj + 64 * br:128 * jj + 64 * br + 64], (qt, kt),
                        (vtok,), master(BI[:, h, :]), lambda: st["rel"], True, out, False, br == 1,
                        gate=lambda u, br=br, h=h: GT[:, u, 4 + 4 * br + h:5 + 4 * br + h], after=after))
            attend(heads)

        MIX = ([(lru_in, 0), (lru_in, 1), (lru_gate, 0), (lru_gate, 1)]
               + [(f, c) for c in range(2) for f in (sc_b, sc_c, sc_x)] + [(fg, 0)]
               + [(fox, j) for j in range(6)] + [(nsa_kv, j) for j in range(4)] + [(nsa_q, 0), (nsa_q, 1)])

        def mix_evac(m, bank, tok):
            if m == 12:
                for h in range(4):
                    a = load_bi(h, relm[h, :, :], *((st["ya", 1][1],) if h == 3 else ()))
                    st["rel"] = p_tt(BI[:, h, :], BI[:, h, :], mask, ADD, a, CTOK)
            f, arg = MIX[m]
            f(arg, bank, tok)

        linear(norm["mv"], 23, mix_evac, mid=lambda: norm_stats(norm))
        flush()
        norm_end(norm)

        def residual(nxt):
            def evac(m, bank, tok):
                t = add_x(bank, m, tok)
                if nxt is not None:
                    norm_chunk(nxt, m, t)
            return evac

        def ffn(norm, nxt, layer, final=False):
            hid = {}
            cur = {}

            def plain(m, bank, tok, off, base):
                g, up = m % 2 == 0, m % 2 == 1
                b = tiles.get()
                t = scaled(b.ap, bank, norm, tok, *b.w)
                if g:
                    t = a_act(b.ap, b.ap, ACT.Silu, t)
                    cur["g"] = (b, t)
                else:
                    gb, gt = cur["g"]
                    t = v_tt(b.ap, b.ap, gb.ap, MUL, gt)
                    gb.done(t)
                    hid[m // 2] = split_to(m // 2, b.ap, t, b)

            def conv(m, bank, tok, off, base):
                ch = (off + m // 2) + (22 if m % 2 == 0 else 0)
                pad = pads.get()
                v_set(pad.ap[:, 0:1], 0.0, *pad.w)
                v_set(pad.ap[:, 513:514], 0.0)
                scaled(pad.ap[:, 1:513], bank, norm, tok)
                b = tiles.get()
                wn = 132 * layer
                t = v_ts(b.ap, pad.ap[:, 1:513], pcol("ffn_dw_w", wn + 44 + ch),
                         pcol("ffn_dw_b", 44 * layer + ch), MUL, ADD, *b.w)
                v_stt(b.ap, pad.ap[:, 0:512], pcol("ffn_dw_w", wn + ch), b.ap, MUL, ADD)
                t = v_stt(b.ap, pad.ap[:, 2:514], pcol("ffn_dw_w", wn + 88 + ch), b.ap, MUL, ADD)
                pad.done(t)
                if m % 2 == 0:
                    t = a_act(b.ap, b.ap, ACT.Gelu_apprx_tanh, t)
                    cur["g"] = (b, t)
                else:
                    gb, gt = cur["g"]
                    t = v_tt(b.ap, b.ap, gb.ap, MUL, gt)
                    gb.done(t)
                    hid[m // 2] = split_to(m // 2, b.ap, t, b)

            fn = plain if layer is None else conv
            for i, (a, b) in enumerate(FF_PARTS):
                hid.clear()
                linear(norm["mv"], 2 * (b - a), lambda m, bank, tok: fn(m, bank, tok, a, i),
                       mid=lambda: norm_stats(norm) if i == 0 else None)
                mv = [hid[k] for k in range(b - a)]
                if i < len(FF_PARTS) - 1:
                    linear(mv, 8, lambda m, bank, tok: add_x(bank, m, tok))
                else:
                    norm_end(norm)
                    if final:
                        def last(m, bank, tok):
                            t = add_x(bank, m, tok)
                            load(out[m, :, :], X[:, m, :], s_out, t)
                        linear(mv, 8, last)
                    else:
                        linear(mv, 8, residual(nxt))

        v_ts(G8[:, 2:3], pcol("nat_q"), 0.125, None, MUL, None, C2TOK)
        n_ffn = new_norm("norm_ffn")
        linear(mixed, 8, residual(n_ffn))
        norm = new_norm("norm1")
        ffn(n_ffn, norm, None)

        def conv_layer(norm, nxt, ci):
            cur = {}
            outs = []

            def evac(m, bank, tok):
                c = m // 2
                if m % 2 == 0:
                    g = tiles.get()
                    t = scaled(g.ap, bank, norm, tok, *g.w)
                    cur["g"] = (g, a_act(g.ap, g.ap, ACT.Sigmoid, t, bias=pcol("conv_b_in", 16 * ci + 8 + c)))
                    return
                pad = pads.get()
                v_set(pad.ap[:, 0:15], 0.0, *pad.w)
                v_set(pad.ap[:, 527:542], 0.0)
                scaled(pad.ap[:, 15:527], bank, norm, tok)
                g, gt = cur["g"]
                v_stt(pad.ap[:, 15:527], pad.ap[:, 15:527], pcol("conv_b_in", 16 * ci + c), g.ap, ADD, MUL, gt)
                g.done((V.sem, V.count))
                o = tiles.get()
                wn = 248 * ci + 31 * c
                v_ts(o.ap, pad.ap[:, 0:T], pcol("conv_dw_w", wn), pcol("conv_dw_b", 8 * ci + c), MUL, ADD,
                     *o.w)
                for j in range(1, 31):
                    t = v_stt(o.ap, pad.ap[:, j:j + T], pcol("conv_dw_w", wn + j), o.ap, MUL, ADD)
                pad.done(t)
                outs.append((o, t))

            linear(norm["mv"], 16, evac, mid=lambda: norm_stats(norm))
            norm_end(norm)
            bank = banks.get()
            for k, (o, t) in enumerate(outs):
                tm = mm(bank.ap, ones, o.ap, k == 0, k == 7, t, *bank.w, inc=k == 7)
            mu = tiles.get()
            tm = a_act(mu.ap, bank.ap, ACT.Copy, tm, *mu.w, scale=1.0 / D)
            bank.done(tm)
            bank = banks.get()
            for k, (o, t) in enumerate(outs):
                t = v_tt(o.ap, o.ap, mu.ap, SUB, tm)
                s = tiles.get()
                t2 = a_act(s.ap, o.ap, ACT.Square, t, *s.w)
                t3 = mm(bank.ap, ones, s.ap, k == 0, k == 7, t2, *bank.w, inc=True)
                s.done(t3)
            mu.done(t)
            r = tiles.get()
            t3 = a_act(r.ap, bank.ap, ACT.Ln, t3, *r.w, scale=1.0 / D, bias=eps)
            bank.done(t3)
            t3 = a_act(r.ap, r.ap, ACT.Exp, scale=-0.5)
            mv = []
            for k, (o, _) in enumerate(outs):
                t = v_tt(o.ap, o.ap, r.ap, MUL, t3)
                t = a_act(o.ap, o.ap, ACT.Silu, t, scale=pcol("conv_ln_g", 8 * ci + k),
                          bias=pcol("conv_ln_b", 8 * ci + k))
                mv.append(split_to(k, o.ap, t, o))
            r.done((V.sem, V.count))
            linear(mv, 8, residual(nxt))

        def nat_layer(norm, nxt):
            mv = [None] * 8
            cur = {}
            used = [(), (), (), ()]
            colmask = cc("colmask", 64).unsqueeze(1).to_broadcast([128, 14, 64])

            def evac(m, bank, tok):
                c, kind = divmod(m, 3)
                b = tiles.get()
                t = scaled(b.ap, bank, norm, tok, *b.w)
                if kind < 2:
                    cur[kind] = (b, head_norm(b, t, G8[:, 2:3] if kind == 0 else pcol("nat_k")))
                    return
                vt = tiles.get()
                got = to_tokens(b.ap, t, vt.ap, *vt.w, done=lambda x: b.done(x))
                q, qt = cur[0]
                k, kt = cur[1]
                ob = []
                heads = []
                for p in range(2):
                    h = 2 * c + p
                    slot = h % 4
                    a = load_bi(slot, natb[h, :, :], *used[slot])
                    view = BI[:, slot, :].rearrange("p (a b) -> p a b", b=64)
                    bt = p_tt(view, view, colmask, ADD, a)

                    def out(p=p):
                        if p == 0:
                            ob.append(banks.get())
                            return half(ob[0].ap, 0), ob[0].w
                        return half(ob[0].ap, 1), ()

                    def after(t, p=p, slot=slot):
                        used[slot] = ((V.sem, V.count),)
                        if p == 1:
                            for x in (q, k, vt):
                                x.done(t)
                            y = tiles.get()
                            t2 = v_copy(y.ap, ob[0].ap, t, *y.w)
                            ob[0].done(t2)
                            mv[c] = split_to(c, y.ap, t2, y)
                    heads.append(head(
                        half(q.ap, p), half(k.ap, p),
                        lambda jj, p=p: vt.ap[:, 128 * jj + 64 * p:128 * jj + 64 * p + 64], (qt, kt), (got,),
                        lambda u, view=view: view[:, 6 - 2 * u:14 - 2 * u, :], lambda bt=bt: bt, False, out,
                        True, True, after=after, bias2d=True))
                attend(heads)

            linear(norm["mv"], 24, evac, mid=lambda: norm_stats(norm))
            flush()
            norm_end(norm)
            linear(mv, 8, residual(nxt))

        def ret_layer(norm, nxt):
            dec = PRM[:, POFF["ret_dec"]:POFF["ret_dec"] + 8]
            e_, u, l, w_, lg, nl = (small(8) for _ in range(6))
            t = a_act(e_, dec, ACT.Exp, (V.sem, V.count), scale=-math.log(2.0))
            log1p_of(lg, e_, -1.0, u, l, w_, t)
            lt = v_ts(nl, lg, -1.0, None, MUL, None)
            LG = SM[:, 142:150]
            NL = SM[:, 150:158]
            v_copy(LG, lg)
            lt = v_copy(NL, nl)
            free = (V.sem, V.count)
            rt = [load_bi(1, rope[0, :, :], free), load_bi(2, rope[1, :, :], free)]
            dt_ = load_bi(3, dist, free)
            cosv, sinv, dv = BI[:, 1, 0:T], BI[:, 2, 0:T], BI[:, 3, :]
            dm = BI[:, 0, :]
            mvs = [None] * 8
            dfree = [()]

            def head(h):
                qk, vts, gs = {}, [], []
                v_ts(dm, dv, NL[:, 4 + h:5 + h], None, MUL, None, dt_, lt, *dfree[0])
                t = v_stt(dm, dv, LG[:, h:h + 1], dm, MUL, ALU.min)
                dmt = a_act(dm, dm, ACT.Exp, t)

                def evac(m, bank, tok):
                    b = tiles.get()
                    t = scaled(b.ap, bank, norm, tok, *b.w)
                    if m < 4:
                        kind, part = divmod(m, 2)
                        qk[m] = (b, t)
                        if part == 1:
                            x1, x2 = qk[2 * kind][0], b
                            a, c = tiles.get(), tiles.get()
                            v_tt(a.ap, x2.ap, sinv, MUL, rt[1], *a.w)
                            v_tt(c.ap, x1.ap, sinv, MUL, *c.w)
                            v_tt(x1.ap, x1.ap, cosv, MUL, rt[0])
                            t1 = v_tt(x1.ap, x1.ap, a.ap, SUB)
                            v_tt(x2.ap, x2.ap, cosv, MUL)
                            t2 = v_tt(x2.ap, x2.ap, c.ap, ADD)
                            a.done(t2)
                            c.done(t2)
                            if kind == 1:
                                t1 = v_ts(x1.ap, x1.ap, 0.0625, None, MUL, None)
                                t2 = v_ts(x2.ap, x2.ap, 0.0625, None, MUL, None)
                            qk[2 * kind] = (x1, t1)
                            qk[2 * kind + 1] = (x2, t2)
                    elif m < 8:
                        vt = tiles.get()
                        vts.append((vt, to_tokens(b.ap, t, vt.ap, *vt.w, done=lambda x: b.done(x))))
                    else:
                        gs.append((b, a_act(b.ap, b.ap, ACT.Silu, t)))

                linear(norm["mv"], 12, evac, mid=lambda: norm_stats(norm) if h == 0 else None)
                flush()
                pt = h % 2
                for j in range(4):
                    bank = banks.get()
                    for d in range(2):
                        t = mm(bank.ap, qk[2 + d][0].ap[:, 128 * j:128 * j + 128], qk[d][0].ap, d == 0,
                               d == 1, qk[2 + d][1], qk[d][1], *bank.w, inc=d == 1)
                    t = v_tt(PT[:, pt, j, :], bank.ap, dm[:, 384 - 128 * j:896 - 128 * j], MUL, t, dmt,
                             *pt_free[pt])
                    bank.done(t)
                    pts = t
                dfree[0] = (pts,)
                for i in range(4):
                    qk[i][0].done((V.sem, V.count), (PE.sem, PE.count))
                os = []
                for c in range(4):
                    bank = banks.get()
                    for j in range(4):
                        t = mm(bank.ap, vts[c][0].ap[:, 128 * j:128 * j + 128], PT[:, pt, j, :], j == 0,
                               j == 3, pts, vts[c][1][0], *bank.w, inc=j == 3)
                    vts[c][0].done(t)
                    o = tiles.get()
                    t = a_copy(o.ap, bank.ap, t, *o.w)
                    bank.done(t)
                    os.append((o, t))
                pt_free[pt] = ((PE.sem, PE.count),)
                bank = banks.get()
                for c in range(4):
                    t = mm(bank.ap, ones, os[c][0].ap, c == 0, c == 3, os[c][1], *bank.w, inc=c == 3)
                mu = tiles.get()
                tm = a_act(mu.ap, bank.ap, ACT.Copy, t, *mu.w, scale=1.0 / 512)
                bank.done(tm)
                bank = banks.get()
                for c in range(4):
                    o = os[c][0]
                    t = v_tt(o.ap, o.ap, mu.ap, SUB, tm)
                    s = tiles.get()
                    t2 = a_act(s.ap, o.ap, ACT.Square, t, *s.w)
                    t3 = mm(bank.ap, ones, s.ap, c == 0, c == 3, t2, *bank.w, inc=True)
                    s.done(t3)
                mu.done(t)
                r = tiles.get()
                t3 = a_act(r.ap, bank.ap, ACT.Ln, t3, *r.w, scale=1.0 / 512, bias=eps)
                bank.done(t3)
                t3 = a_act(r.ap, r.ap, ACT.Exp, scale=-0.5)
                for c in range(4):
                    o = os[c][0]
                    v_stt(o.ap, o.ap, pcol("ret_gn", 4 * h + c), r.ap, MUL, MUL, t3)
                    g, gt = gs[c]
                    t = v_tt(o.ap, o.ap, g.ap, MUL, gt)
                    g.done(t)
                    mvs[4 * (h % 2) + c] = split_to(4 * (h % 2) + c, o.ap, t, o)
                r.done(t)

            for h in range(4):
                head(h)
                if h == 1:
                    linear(list(mvs), 8, lambda m, bank, tok: add_x(bank, m, tok))
            norm_end(norm)
            linear(list(mvs), 8, residual(nxt))

        for layer in range(4):
            n2 = new_norm("norm2", 8 * layer)
            if layer in (0, 3):
                conv_layer(norm, n2, layer // 3)
            elif layer == 1:
                nat_layer(norm, n2)
            else:
                ret_layer(norm, n2)
            norm = new_norm("norm1", 8 * (layer + 1)) if layer < 3 else None
            ffn(n2, norm, layer, final=layer == 3)
        assert at["tile"] == N_TILES and not bg

        block = ctx.enter_context(nc.Block())

        @block.sync
        def _(e):
            SP.run(e)
            e.wait_ge(s_out, 128)

        @block.vector
        def _(e):
            V.run(e)

        @block.scalar
        def _(e):
            A.run(e)

        @block.gpsimd
        def _(e):
            P.run(e)

        @block.tensor
        def _(e):
            PE.run(e)


def rel_buckets():
    d = np.arange(0, 1024)
    large = 16 + (np.log(np.maximum(d, 1).astype(np.float32) / np.float32(16))
                  / np.float32(math.log(128 / 16)) * np.float32(16)).astype(np.int32)
    return np.where(d < 16, d, np.minimum(large, 31))


def constants():
    q = np.arange(128)
    c = {}
    c["ident"] = np.eye(128)
    c["ones"] = np.ones((128, 128))
    c["bones"] = np.kron(np.eye(2), np.ones((64, 64)))
    dist = q[:, None] + 384 - np.arange(ML)[None, :]
    c["mask"] = np.where(dist < 0, NEG, 0.0)
    sel = np.zeros((128, 4, 128))
    for h in range(4):
        sel[h, h, :] = -1.0
    c["selneg"] = sel.reshape(128, 512)
    col = q % 64
    first = np.clip(col - 8, 0, 48)
    kc = np.arange(64)
    c["colmask"] = np.where((kc[None] >= first[:, None]) & (kc[None] < first[:, None] + 16), 0.0, NEG)
    c["rowmask"] = (q >= 31).astype(float)[:, None]
    cst = np.concatenate([c[n] for n, _ in CONSTS], axis=1).astype(np.float32)
    theta = (np.float32(1.0) / (np.float32(10000.0) ** np.linspace(0.0, 1.0, 128, dtype=np.float32))).astype(np.float32)
    ang = (theta[:, None] * np.arange(T, dtype=np.float32)[None, :]).astype(np.float32)
    rope = np.stack([np.cos(ang.astype(np.float64)), np.sin(ang.astype(np.float64))]).astype(np.float32)
    rdist = (np.arange(ML)[None, :] - 384 - q[:, None]).astype(np.float32)
    return cst, rope, rdist


def kernel(**inp):
    import concourse.bacc as bacc
    from concourse.bass_utils import run_bass_kernel_spmd

    g = {k: np.asarray(v) for k, v in inp.items()}
    f32 = np.float32

    def cols(v):
        return np.ascontiguousarray(v.reshape(-1, 128).T)

    def twice(v):
        return np.concatenate([v, v], axis=-1)

    w_in = g["w_in"][0]
    order = list(range(0, 512))
    for c in range(2):
        for base in (512, 768, 1024):
            order += list(range(base + 128 * c, base + 128 * c + 128))
    parts = [w_in[:, order]]
    fgw = np.zeros((D, 128), f32)
    fgw[:, 0:4] = w_in[:, 2048:2052]
    fgw[:, 32:44] = w_in[:, 2692:2704]
    parts.append(fgw)
    for c in range(2):
        for base in (1280, 1536, 1792):
            parts.append(w_in[:, base + 128 * c:base + 128 * c + 128])
    kv = [w_in[:, 2308 + 64 * j:2372 + 64 * j] for j in range(6)]
    parts += [kv[0], kv[1], kv[2], kv[2], kv[4], kv[4], kv[3], kv[5], w_in[:, 2052:2308]]
    W = {"w_in": np.concatenate(parts, axis=1), "w_out": g["w_out"][0]}

    def pairs(first, second):
        n = first.shape[1] // 128
        a = first.reshape(D, n, 1, 128)
        b = second.reshape(D, n, 1, 128)
        return np.concatenate([a, b], axis=2).reshape(D, 2 * n * 128)

    def ffn(name, up, down):
        for i, (a, b) in enumerate(FF_PARTS):
            W[f"{name}_up{i}"] = up[:, 256 * a:256 * b]
            W[f"{name}_down{i}"] = down[128 * a:128 * b, :]

    F = 2816
    gu = g["w_gate_up"][0]
    ffn("ffn", pairs(gu[:, :F], gu[:, F:]), g["w_down"][0])
    for i in range(2):
        w = g["conv_w_in_2"][i]
        W[f"conv_in{i}"] = pairs(w[:, D:], w[:, :D])
        W[f"conv_out{i}"] = g["conv_w_out_2"][i]
    w = g["nat_w_qkv_2"][0]
    W["nat_qkv"] = w.reshape(D, 3, 8, 128).transpose(0, 2, 1, 3).reshape(D, 3072)
    W["nat_out"] = g["nat_w_out_2"][0]
    w = g["ret_w_in_2"][0]
    for h in range(4):
        W[f"ret_in{h}"] = np.concatenate([w[:, 256 * h:256 * h + 256], w[:, 1024 + 256 * h:1280 + 256 * h],
                                          w[:, 2048 + 512 * h:2560 + 512 * h],
                                          w[:, 4096 + 512 * h:4608 + 512 * h]], axis=1)
    for i in range(2):
        W[f"ret_out{i}"] = g["ret_w_out_2"][0][1024 * i:1024 * i + 1024]
    for layer in range(4):
        up = g["ffn_w_up_2"][layer]
        ffn(f"ffn2_{layer}", pairs(up[:, F:], up[:, :F]), g["ffn_w_down_2"][layer])
    flat = np.zeros((N_BLOCKS * 8, 128, 128), f32)
    at = 0
    for name, kc, mc in linears():
        w = W[name]
        flat[at:at + kc * mc] = w.reshape(kc, 128, mc, 128).transpose(2, 0, 1, 3).reshape(-1, 128, 128)
        at += kc * mc
    wst = np.ascontiguousarray(flat.reshape(N_BLOCKS, 8, 128, 128).transpose(0, 2, 1, 3)).reshape(
        N_BLOCKS, 128, 1024)

    p = {}
    p["norm_mix"] = cols(g["norm_mix"])
    p["lru_conv_w"] = cols(g["lru_conv_w"])
    p["lru_conv_b"] = cols(g["lru_conv_b"])
    p["lru_b"] = cols(g["lru_b_gates"])
    p["lru_lambda"] = cols(g["lru_lambda"])
    p["sc_conv_w"] = cols(g["sc_conv_w"])
    p["fox_qk"] = cols(twice(g["fox_qk_norm"]))
    p["nsa_qk"] = cols(twice(g["nsa_qk_norm"]))
    fb = np.zeros((128, 1), f32)
    fb[0:4, 0] = g["fox_f_bias"][0]
    fb[32:44, 0] = g["nsa_gate_bias"][0]
    p["fg_bias"] = fb
    p["cmp_pos"] = g["nsa_cmp_pos"][0].transpose(0, 2, 1).reshape(128, 32)
    p["out_norm"] = cols(g["out_norm"])
    p["norm_ffn"] = cols(g["norm_ffn"])
    p["norm1"] = cols(g["norm1_g_2"])
    p["norm2"] = cols(g["norm2_g_2"])
    p["conv_b_in"] = cols(g["conv_b_in_2"])
    p["conv_dw_w"] = g["conv_dw_w_2"].reshape(2, 31, 8, 128).transpose(3, 0, 2, 1).reshape(128, 496)
    p["conv_dw_b"] = cols(g["conv_dw_b_2"])
    p["conv_ln_g"] = cols(g["conv_ln_g_2"])
    p["conv_ln_b"] = cols(g["conv_ln_b_2"])
    p["nat_q"] = cols(twice(g["nat_q_norm_g_2"]))
    p["nat_k"] = cols(twice(g["nat_k_norm_g_2"]))
    p["ret_dec"] = np.broadcast_to(g["ret_log2_inv_decay_2"].reshape(1, 8), (128, 8))
    p["ret_gn"] = cols(g["ret_gn_g_2"])
    p["ffn_dw_w"] = cols(g["ffn_dw_w_2"])
    p["ffn_dw_b"] = cols(g["ffn_dw_b_2"])
    prm = np.ascontiguousarray(np.concatenate([p[n] for n, _ in PARAMS], axis=1))
    cst, rope, rdist = constants()

    gw = g["lru_w_gates"][0]
    gatew = np.zeros((128, 2, 2, 128), f32)
    for i in range(2):
        for h in range(4):
            r = 64 * (h % 2)
            gatew[r:r + 64, i, h // 2, r:r + 64] = gw[i, h]
    cmpw1 = np.ascontiguousarray(g["nsa_cmp_w1"][0].transpose(0, 2, 1, 3)).reshape(128, 4096)
    w2 = g["nsa_cmp_w2"][0]
    cmpw2 = np.ascontiguousarray(np.concatenate([w2[0], w2[0], w2[1]], axis=1))
    q = np.arange(128)
    dd = np.maximum(q[:, None] + 384 - np.arange(ML)[None, :], 0)
    relm = np.ascontiguousarray(g["rel_bias"][rel_buckets()[dd]].transpose(2, 0, 1))
    rpb = g["nat_rpb_2"][0]
    ri, col = q // 64, q % 64
    jj = np.arange(1, 15)[None, :, None] - ri[:, None, None]
    xx = np.clip(np.arange(64)[None, None, :] - col[:, None, None] + 15, 0, 30)
    natb = np.ascontiguousarray(rpb[:, jj, xx]).reshape(16, 128, ML)

    arrays = {
        "wst": wst, "xin": np.ascontiguousarray(g["x"][0].T).reshape(8, 128, T), "prm": prm, "cst": cst,
        "gatew": gatew.reshape(128, 512), "cmpw1": cmpw1, "cmpw2": cmpw2, "relm": relm, "natb": natb,
        "rope": rope, "dist": rdist,
    }
    nc = bacc.Bacc("TRN2", target_bir_lowering=False, num_devices=1)
    aps = [nc.dram_tensor(n, a.shape, mybir.dt.float32, kind="ExternalInput").ap() for n, a in arrays.items()]
    out = nc.dram_tensor("out", (8, 128, T), mybir.dt.float32, kind="ExternalOutput").ap()
    build(nc, *aps, out)
    r = run_bass_kernel_spmd(nc, [arrays], core_ids=[0])
    return np.ascontiguousarray(r.results[0]["out"].reshape(D, T).T).reshape(1, T, D)
```

```python
import math
from collections import deque
from contextlib import ExitStack

import numpy as np
import concourse.bass as bass
from concourse import mybir

T = 512
D = 1024
DC = 8
FFC = 22
EPS = 1e-6
NEG = -1.0e30
ML = 896
FF_PARTS = ((0, 8), (8, 15), (15, 22))
NRAW = 4
NSPLIT = 3
NTILE = 17
NPAD = 4
ROOM = 7
OUT_ORDER = (4, 5, 6, 7, 0, 1, 2, 3)
TAPS_PE = 5
TAPS_POOL = 7

PARAMS = (
    ("norm_mix", 8), ("lru_conv_w", 8), ("lru_conv_b", 2), ("lru_b", 4), ("lru_lambda", 2),
    ("sc_conv_w", 6), ("fox_qk", 2), ("nsa_qk", 4), ("fg_bias", 1), ("cmp_pos", 32),
    ("out_norm", 8), ("norm_ffn", 8), ("norm1", 32), ("norm2", 32), ("conv_b_in", 32),
    ("conv_dw_w", 496), ("conv_dw_b", 16), ("conv_ln_g", 16), ("conv_ln_b", 16),
    ("nat_q", 1), ("nat_k", 1), ("ret_dec", 8), ("ret_gn", 16), ("ffn_dw_w", 528), ("ffn_dw_b", 176),
)
CONSTS = (("ident", 128), ("ones", 128), ("bones", 128), ("mask", ML), ("colmask", 64), ("rowmask", 1))


def offsets(spec):
    out, at = {}, 0
    for name, n in spec:
        out[name] = at
        at += n
    return out, at


POFF, NPRM = offsets(PARAMS)
COFF, NCST = offsets(CONSTS)


def linears():
    out = [("w_in", 8, 23), ("w_out", 8, 8)]

    def ffn(name):
        for i, (a, b) in enumerate(FF_PARTS):
            out.append((f"{name}_up{i}", 8, 2 * (b - a)))
            out.append((f"{name}_down{i}", b - a, 8))

    ffn("ffn")
    for layer in range(4):
        if layer in (0, 3):
            out.append((f"conv_in{layer // 3}", 8, 16))
            out.append((f"conv_out{layer // 3}", 8, 8))
        elif layer == 1:
            out.append(("nat_qkv", 8, 24))
            out.append(("nat_out", 8, 8))
        else:
            for name, n in (("in0", 12), ("in1", 12), ("in2", 12), ("out0", 8), ("in3", 12), ("out1", 8)):
                out.append((f"ret_{name}", 8, n))
        ffn(f"ffn2_{layer}")
    return out


N_TILES = sum(k * m for _, k, m in linears())
N_BLOCKS = (N_TILES + 7) // 8




class Engine:

    def __init__(self, sem, linked):
        self.sem, self.linked = sem, linked
        self.ops, self.count = [], 0

    def put(self, fn, waits=(), inc=True, own=True):
        waits = [w for w in waits if w is not None]
        if self.linked and own and self.count:
            waits.append((self.sem, self.count))
        self.ops.append((waits, fn, inc))
        if inc:
            self.count += 1
        return (self.sem, self.count)

    def run(self, e):
        passed = {}
        for waits, fn, inc in self.ops:
            for sem, value in waits:
                if passed.get(id(sem), 0) < value:
                    passed[id(sem)] = value
                    e.wait_ge(sem, value)
            ins = fn(e)
            if inc:
                ins.then_inc(self.sem, 1)


class Ring:

    def __init__(self, aps):
        self.free = deque((ap, ()) for ap in aps)

    def get(self):
        ap, waits = self.free.popleft()
        return Buf(self, ap, waits)


class Buf:
    def __init__(self, ring, ap, waits):
        self.ring, self.ap, self.w = ring, ap, waits

    def done(self, *after):
        self.ring.free.append((self.ap, after))


def build(nc, wst, xin, prm, cst, gatew, cmpw1, cmpw2, relm, natb, rope, dist, out):
    f32 = mybir.dt.float32
    f32r = mybir.dt.float32r
    ALU = mybir.AluOpType
    ACT = mybir.ActivationFunctionType
    MUL, ADD, SUB = ALU.mult, ALU.add, ALU.subtract

    with ExitStack() as ctx:
        def sb(name, shape, dt=f32):
            return ctx.enter_context(nc.sbuf_tensor(name, shape, dt))

        def sem(name):
            return ctx.enter_context(nc.semaphore(name))

        X = sb("X", [128, 8, T])
        XH = sb("XH", [128, 8, T], f32r)
        XL = sb("XL", [128, 8, T], f32r)
        HH = sb("HH", [128, 8, T], f32r)
        HL = sb("HL", [128, 8, T], f32r)
        RAW = sb("RAW", [128, NRAW, 1024])
        WH = sb("WH", [128, NSPLIT, 1024], f32r)
        WL = sb("WL", [128, NSPLIT, 1024], f32r)
        PT = sb("PT", [128, 2, 4, T])
        BI = sb("BI", [128, 4, ML])
        PRM = sb("PRM", [128, NPRM])
        CST = sb("CST", [128, NCST])
        TT = sb("TT", [128, NTILE, T])
        PD = sb("PD", [128, NPAD, 544])
        SM = sb("SM", [128, 160])
        GW = sb("GW", [128, 512])
        W2 = sb("W2", [128, 192])
        KC = sb("KC", [128, 32])
        VC = sb("VC", [32, 64])
        G8 = sb("G8", [128, 8])
        GT = sb("GT", [128, 4, 12])
        PSB = [ctx.enter_context(nc.psum_tensor(f"PS{i}", [128, T], f32)) for i in range(8)]

        V = Engine(sem("s_v"), True)
        A = Engine(sem("s_a"), True)
        P = Engine(sem("s_p"), True)
        PE = Engine(sem("s_pe"), False)
        SP = Engine(sem("s_sp"), False)
        s_raw = [sem(f"s_raw{i}") for i in range(NRAW)]
        s_x = [sem(f"s_x{k}") for k in range(8)]
        s_c2, s_c3, s_c4, s_gw = sem("s_c2"), sem("s_c3"), sem("s_c4"), sem("s_gw")
        s_c = sem("s_c")
        s_w1 = sem("s_w1")
        s_w2 = sem("s_w2")
        s_bi = [sem(f"s_bi{i}") for i in range(4)]
        s_out = sem("s_out")

        def v_tt(o, a, b, op, *w, own=True):
            return V.put(lambda e: e.tensor_tensor(o, a, b, op), w, own=own)

        def v_ts(o, a, s1, s2, op0, op1, *w, own=True):
            if op1 is None:
                return V.put(lambda e: e.tensor_scalar(o, a, s1, None, op0), w, own=own)
            return V.put(lambda e: e.tensor_scalar(o, a, s1, s2, op0, op1), w, own=own)

        def v_stt(o, a, s, b, op0, op1, *w, own=True):
            return V.put(lambda e: e.scalar_tensor_tensor(o, a, s, b, op0, op1), w, own=own)

        def v_add_max(o, a, b, mx, *w):
            return V.put(lambda e: e.tensor_tensor_reduce(
                out=o, in0=a, in1=b, scale=1.0, scalar=-3.0e38, op0=ADD, op1=ALU.max, accum_out=mx), w,
                own=False)

        def v_copy(o, a, *w, own=True):
            return V.put(lambda e: e.tensor_copy(o, a), w, own=own)

        def v_rec(o, a, *w):
            return V.put(lambda e: e.reciprocal(o, a), w)

        def v_set(o, value, *w):
            return V.put(lambda e: e.memset(o, value), w)

        table = [None]
        LNEXP = "natural_log_exp_and_others"

        def a_act(o, a, f, *w, scale=1.0, bias=0.0, acc=None, own=True):
            if f in (ACT.Ln, ACT.Exp):
                if table[0] != LNEXP:
                    A.put(lambda e: e.preload_act_table_set(LNEXP), (), False)
                    table[0] = LNEXP
            elif f not in (ACT.Copy, ACT.Square):
                table[0] = f
            if acc is not None:
                return A.put(lambda e: e.activation(o, a, f, scale=scale, bias=bias, accum_out=acc), w,
                             own=own)
            return A.put(lambda e: e.activation(o, a, f, scale=scale, bias=bias), w, own=own)

        def a_copy(o, a, *w, own=True):
            return A.put(lambda e: e.activation(o, a, ACT.Copy), w, own=own)

        def p_tt(o, a, b, op, *w, own=True):
            return P.put(lambda e: e.tensor_tensor(o, a, b, op), w, own=own)

        def mm(o, l, r, start, stop, *w, inc=False):
            return PE.put(lambda e: e.matmul(o, l, r, start=start, stop=stop), w, inc)

        def tr(o, a, *w, inc=False):
            return PE.put(lambda e: e.transpose(o, a, ident), (C3TOK, *w), inc)

        def load(o, a, s, *w):
            SP.put(lambda e: e.dma_start(o, a).then_inc(s, 16), w, False)

        def pcol(name, i=0):
            return PRM[:, POFF[name] + i:POFF[name] + i + 1]

        def cc(name, n):
            return CST[:, COFF[name]:COFF[name] + n]

        ident, ones, bones = cc("ident", 128), cc("ones", 128), cc("bones", 128)
        tiles = Ring([TT[:, i, :] for i in range(NTILE)])
        pads = Ring([PD[:, i, :] for i in range(NPAD)])
        banks = Ring([p[:, :] for p in PSB])
        small_at = [0]

        def small(n=1):
            if small_at[0] + n > 128:
                small_at[0] = 0
            a = small_at[0]
            small_at[0] += n
            return SM[:, a:a + n]

        eps = SM[:, 159:160]

        def load_once(o, a, s, *w):
            load(o, a, s, *w)
            return (s, 16)

        CTOK = (s_c, 16)
        C3TOK = (s_c3, 16)
        C4TOK = (s_c4, 16)
        bi_n = [0, 0, 0, 0]

        def load_bi(slot, src, *w):
            load(BI[:, slot, 0:src.shape[-1]], src, s_bi[slot], *w)
            bi_n[slot] += 16
            return (s_bi[slot], bi_n[slot])

        lo_done, used = [], []
        at = {"tile": 0, "loaded": 0}

        def load_block():
            b = at["loaded"]
            if b < N_BLOCKS:
                load(RAW[:, b % NRAW, :], wst[b, :, :], s_raw[b % NRAW],
                     lo_done[b - NRAW] if b >= NRAW else None)
                at["loaded"] += 1

        def split_block():
            b = len(lo_done)
            raw, wh, wl = RAW[:, b % NRAW, :], WH[:, b % NSPLIT, :], WL[:, b % NSPLIT, :]
            arrived = (s_raw[b % NRAW], 16 * (b // NRAW + 1))
            hi = a_copy(wh, raw, arrived, used[b - NSPLIT] if b >= NSPLIT else None, own=False)
            lo_done.append(p_tt(wl, raw, wh.bitcast(f32), SUB, hi, own=False))
            load_block()

        def take_tile():
            b, i = divmod(at["tile"], 8)
            if i == 0:
                while len(lo_done) < min(b + NSPLIT, N_BLOCKS):
                    split_block()
            at["tile"] += 1
            s = b % NSPLIT
            last = i == 7 or at["tile"] == N_TILES
            return (WH[:, s, 128 * i:128 * i + 128], WL[:, s, 128 * i:128 * i + 128], lo_done[b], last)

        load(PRM[:, 0:POFF["norm1"]], prm[:, 0:POFF["norm1"]], s_c)
        load(X[:, 0, :], xin[0, :, :], s_x[0])
        load_block()
        for k in range(1, 8):
            load(X[:, k, :], xin[k, :, :], s_x[k])
        load(CST[:, 0:384], cst[:, 0:384], s_c3)
        load_block()
        w1t = load_once(PT[:, :, :, :].rearrange("p a b n -> p (a b n)"), cmpw1, s_w1)
        w2t = load_once(W2[:, :], cmpw2, s_w2)
        load(CST[:, 384:NCST], cst[:, 384:NCST], s_c4)
        for _ in range(NRAW - 2):
            load_block()
        rel_in = [load_bi(h, relm[h, :, :]) for h in range(4)]
        gw_tok = load_once(GW[:, :], gatew, s_gw)
        load(PRM[:, POFF["norm1"]:NPRM], prm[:, POFF["norm1"]:NPRM], s_c2)
        C2TOK = (s_c2, 16)

        bg, soon = deque(), deque()

        def later(fn, delay=3, first=False):
            (soon if first else bg).append((at["tile"] + delay, fn))

        def next_step():
            (soon or bg).popleft()[1]()

        def flush():
            while bg or soon:
                next_step()

        def flush_ready():
            for queue in (soon, bg):
                if queue and queue[0][0] <= at["tile"]:
                    queue.popleft()[1]()
                    return

        def linear(mv, mc, evac, mid=None, pace=0, hold=False):
            kc = len(mv)
            for m in range(mc):
                bank = banks.get()
                for k in range(kc):
                    wh, wl, wtok, last = take_tile()
                    h, l, tok = mv[k]
                    w = (*bank.w, wtok, tok) if k == 0 else (wtok, tok)
                    mm(bank.ap, wh, h, k == 0, False, *w)
                    mm(bank.ap, wh, l, False, False)
                    t = mm(bank.ap, wl, h, False, k == kc - 1, inc=last or k == kc - 1)
                    if last:
                        used.append(t)
                    if pace and k % pace == pace - 1:
                        flush_ready()
                if m == 0 and mid is not None:
                    mid()
                if not pace and not hold:
                    flush()
                while (bg or soon) and len(tiles.free) < ROOM:
                    next_step()
                evac(m, bank, t)

        def split_to(k, src, tok, buf=None):
            hi = a_copy(HH[:, k, :], src, tok, own=False)
            lo = p_tt(HL[:, k, :], src, HH[:, k, :].bitcast(f32), SUB, hi, own=False)
            if buf is not None:
                buf.done(lo)
            return (HH[:, k, :], HL[:, k, :], lo)

        def new_norm(name, first=0):
            return {"gain": lambda k: pcol(name, first + k), "mv": []}

        def norm_chunk(n, k, *x_done, first=False):
            g = n["gain"](k)
            x = X[:, k, :]
            v_ts(XH[:, k, :], x, g, None, MUL, None, *x_done, own=False)
            lo = v_stt(XL[:, k, :], x, g, XH[:, k, :].bitcast(f32), MUL, SUB)
            n["mv"].append((XH[:, k, :], XL[:, k, :], lo))
            if k == 0:
                n["sq"] = tiles.get()
                n["sq_done"] = a_act(n["sq"].ap, x, ACT.Square, *n["sq"].w, *x_done)
            else:
                s = tiles.get()
                squared = a_act(s.ap, x, ACT.Square, *s.w, *x_done, own=False)
                add = p_tt if first else v_tt
                n["sq_done"] = add(n["sq"].ap, n["sq"].ap, s.ap, ADD, squared, n["sq_done"], own=False)
                s.done(n["sq_done"])

        def norm_stats(n):
            n["rs"] = tiles.get()
            n["rs_done"] = rsqrt_of(n["rs"], n["sq"], n["sq_done"], ones, D)

        def norm_end(n):
            n["rs"].done((V.sem, V.count))

        def rsqrt_of(rs, acc, tok, mat, n):
            bank = banks.get()
            t = mm(bank.ap, mat, acc.ap, True, True, tok, C3TOK, *bank.w, inc=True)
            acc.done(t)
            t = a_act(rs.ap, bank.ap, ACT.Ln, t, *rs.w, eps_tok, scale=1.0 / n, bias=eps, own=False)
            bank.done(t)
            return a_act(rs.ap, rs.ap, ACT.Exp, scale=-0.5)

        def add_x(bank, m, tok):
            t = v_tt(X[:, m, :], bank.ap, X[:, m, :], ADD, tok, own=False)
            bank.done(t)
            return t

        def scaled(dst, bank, norm, tok, *w):
            t = v_tt(dst, bank.ap, norm["rs"].ap, MUL, tok, norm["rs_done"], *w, own=False)
            bank.done(t)
            return t

        def head_norm(buf, tok, gain):
            got = []
            s = tiles.get()
            t = a_act(s.ap, buf.ap, ACT.Square, tok, *s.w, own=False)

            def step():
                r = tiles.get()
                q = rsqrt_of(r, s, t, bones, 64)
                got.append(v_stt(buf.ap, buf.ap, gain, r.ap, MUL, MUL, q, tok))
                r.done(got[0])
            later(step)
            return got

        def to_tokens(src, tok, dst, *w, done=None):
            got = []

            def step():
                bank = banks.get()
                for b in range(4):
                    t = tr(bank.ap[:, 128 * b:128 * b + 128], src[:, 128 * b:128 * b + 128],
                           tok, *bank.w, inc=b == 3)
                t2 = a_copy(dst, bank.ap, t, *w, own=False)
                bank.done(t2)
                got.append(t2)
                if done is not None:
                    done(t)
            later(step)
            return got

        pt_free = [(), ()]
        pt_at = [0]

        def head(q, k, v, qk_done, v_done, bias, bias_done, causal, out, start, stop, gate=None,
                 extra=None, after=None, bias2d=False):
            return dict(q=q, k=k, v=v, qk_done=qk_done, v_done=v_done, bias=bias, bias_done=bias_done,
                        causal=causal, out=out, start=start, stop=stop, gate=gate, extra=extra,
                        after=after, bias2d=bias2d)

        def scores(hd, u):
            W = 128 * (u + 1) if hd["causal"] else T
            bank = banks.get()
            s = tiles.get()
            ex = hd["extra"]
            t = mm(bank.ap[:, 0:W], hd["q"][:, 128 * u:128 * u + 128], hd["k"][:, 0:W], True, ex is None,
                   *(x[0] for x in hd["qk_done"]), *bank.w, inc=ex is None)
            if ex is not None:
                t = mm(bank.ap[:, 0:W], ex[0], ex[1][:, 0:W], False, True, ex[2], inc=True)
            mx, nm, sm, rc = small(), small(), small(), small()
            b = hd["bias"](u)
            sap, bap = s.ap[:, 0:W], bank.ap[:, 0:W]
            if hd["bias2d"]:
                sap = sap.rearrange("p (a b) -> p a b", b=64)
                bap = bap.rearrange("p (a b) -> p a b", b=64)
            t = v_add_max(sap, bap, b, mx, t, hd["bias_done"](), *s.w)
            bank.done(t)
            t = v_ts(nm, mx, -1.0, None, MUL, None)
            t = a_act(s.ap[:, 0:W], s.ap[:, 0:W], ACT.Exp, t, bias=nm, acc=sm, own=False)
            return (W, s, sm, rc, t)

        def normalise(hd, u, W, s, sm, rc, exp_done):
            V.put(lambda e: e.reciprocal(rc, sm), (exp_done,), own=False)
            if hd["gate"] is None:
                t = v_ts(s.ap[:, 0:W], s.ap[:, 0:W], rc, None, MUL, None)
            else:
                t = v_ts(s.ap[:, 0:W], s.ap[:, 0:W], rc, hd["gate"](u), MUL, MUL, st["gt"])
            return (W, s, t)

        def turn(u, W, s, p_done, pt, pt_ok):
            n = W // 128
            bank = banks.get()
            for j in range(n):
                t = tr(bank.ap[:, 128 * j:128 * j + 128], s.ap[:, 128 * j:128 * j + 128], p_done,
                       *bank.w, inc=j == n - 1)
            s.done(t)
            t = a_copy(PT[:, pt, 0:n, 128 * u:128 * u + 128],
                       bank.ap[:, 0:W].rearrange("p (a b) -> p a b", b=128), t, *pt_ok, own=False)
            bank.done(t)
            return t

        def values(hd, pt, pt_done):
            out, out_ok = hd["out"]()
            for j in range(4):
                a = 128 * j if hd["causal"] else 0
                t = mm(out[:, a:T], hd["v"](j), PT[:, pt, j, a:T], hd["start"] and j == 0,
                       hd["stop"] and j == 3, pt_done, *(x[0] for x in hd["v_done"]), *out_ok, inc=j == 3)
            return t

        def attend(heads):
            units = [(n, u) for n in range(len(heads)) for u in range(4)]
            flight, turned, pend = {}, {}, []

            def value_step(n, pt, t):
                def f():
                    done = values(heads[n], pt, t)
                    pt_free[pt] = (done,)
                    if heads[n]["after"] is not None:
                        heads[n]["after"](done)
                return f

            def step(i):
                def f():
                    ready = list(pend)
                    pend.clear()
                    if i < len(units):
                        n, u = units[i]
                        flight[i] = scores(heads[n], u)
                    if 0 <= i - 1 < len(units):
                        n, u = units[i - 1]
                        flight[i - 1] = normalise(heads[n], u, *flight[i - 1])
                    if 0 <= i - 2 < len(units):
                        n, u = units[i - 2]
                        if u == 0:
                            turned[n] = (pt_at[0] % 2, pt_free[pt_at[0] % 2])
                            pt_at[0] += 1
                        pt, pt_ok = turned[n]
                        t = turn(u, *flight.pop(i - 2), pt, pt_ok)
                        if u == 3:
                            pend.append(value_step(n, pt, t))
                    for fn in ready:
                        fn()
                return f
            for i in range(len(units) + 3):
                later(step(i), 4)

        v_set(eps, EPS)
        eps_tok = (V.sem, V.count)
        pads_tok = eps_tok
        norm = new_norm("norm_mix")
        for k in range(8):
            norm_chunk(norm, k, (s_x[k], 16), CTOK, first=True)
        lam = PRM[:, POFF["lru_lambda"]:POFF["lru_lambda"] + 2]
        c_ab, c_e, c_u, c_l, c_w, c_L, c_NL = (SM[:, 128 + 2 * i:130 + 2 * i] for i in range(7))

        def log1p_of(o, e_, sign, u, l, w_, tok):
            t = v_ts(u, e_, sign, 1.0, MUL, ADD, tok)
            t2 = a_act(l, u, ACT.Ln, t)
            v_ts(w_, u, 1.0, 1e-30, SUB, ADD)
            v_rec(w_, w_)
            v_ts(l, l, 1e-30, None, ADD, None, t2)
            v_tt(l, l, w_, MUL)
            v_tt(l, l, e_, MUL)
            return v_ts(o, l, sign, None, MUL, None)

        v_stt(c_ab, lam, -1.0, lam, MUL, ALU.max, CTOK)
        t = (V.sem, V.count)
        t = a_act(c_e, c_ab, ACT.Exp, t, scale=-1.0)
        log1p_of(c_L, c_e, 1.0, c_u, c_l, c_w, t)
        v_ts(c_u, lam, -1.0, 0.0, MUL, ALU.max)
        v_tt(c_L, c_L, c_u, ADD)
        v_ts(c_NL, c_L, 8.0, None, MUL, None)
        lam_tok = v_ts(c_L, c_L, -8.0, None, MUL, None)
        for i, src in enumerate((pcol("fox_qk"), pcol("nsa_qk"))):
            v_ts(G8[:, i:i + 1], src, 0.125, None, MUL, None)

        n_mix = norm
        mixed = [None] * 8

        def out_norm(g, bufs, toks):
            acc = tiles.get()
            s = tiles.get()
            a_act(acc.ap, bufs[0].ap, ACT.Square, toks[0], *acc.w)
            t = a_act(s.ap, bufs[1].ap, ACT.Square, toks[1], *s.w)
            t = v_tt(acc.ap, acc.ap, s.ap, ADD, t)
            s.done(t)

            def step():
                r = tiles.get()
                q = rsqrt_of(r, acc, t, ones, 256)
                for c in range(2):
                    t3 = v_stt(bufs[c].ap, bufs[c].ap, pcol("out_norm", 2 * g + c), r.ap, MUL, MUL,
                               q, toks[c])
                    mixed[2 * g + c] = split_to(2 * g + c, bufs[c].ap, t3, bufs[c])
                r.done(t3)
            later(step, first=True)

        st = {}

        def conv_taps(o, src, name, c, nch, taps, width, bias, *w):
            last = taps - 1
            if bias is None:
                t = v_ts(o, src[:, last:last + T], pcol(name, last * nch + c), None, MUL, None, *w)
            else:
                t = v_ts(o, src[:, last:last + T], pcol(name, last * nch + c), bias, MUL, ADD, *w)
            for j in range(last - 1, -1, -1):
                t = v_stt(o, src[:, j:j + T], pcol(name, j * nch + c), o, MUL, ADD)
            return t

        def lru_in(c, bank, tok):
            pad = pads.get()
            t = v_set(pad.ap[:, 0:3], 0.0, *pad.w)
            t = scaled(pad.ap[:, 3:515], bank, n_mix, tok)
            xc = tiles.get()
            t = conv_taps(xc.ap, pad.ap, "lru_conv_w", c, 2, 4, T, pcol("lru_conv_b", c), *xc.w)
            pad.done(t)
            r, i = tiles.get(), tiles.get()

            def step():
                b0, b1 = banks.get(), banks.get()
                t0 = mm(b0.ap, GW[:, 128 * c:128 * c + 128], xc.ap, True, True, t, gw_tok, *b0.w,
                        inc=True)
                t1 = mm(b1.ap, GW[:, 256 + 128 * c:384 + 128 * c], xc.ap, True, True, *b1.w, inc=True)
                t0 = a_act(r.ap, b0.ap, ACT.Sigmoid, t0, *r.w, bias=pcol("lru_b", c))
                b0.done(t0)
                t1 = a_act(i.ap, b1.ap, ACT.Sigmoid, t1, *i.w, bias=pcol("lru_b", 2 + c))
                b1.done(t1)
                th = tiles.get()
                t2 = a_act(th.ap, r.ap, ACT.Tanh, lam_tok, *th.w, scale=c_NL[:, c:c + 1])
                ta = a_act(r.ap, r.ap, ACT.Exp, scale=c_L[:, c:c + 1])
                v_tt(i.ap, i.ap, xc.ap, MUL, t1)
                v_ts(xc.ap, th.ap, 1.0, None, ADD, None, t2)
                v_rec(xc.ap, xc.ap)
                tq = v_stt(th.ap, th.ap, 2.0, xc.ap, MUL, MUL)
                tq = a_act(th.ap, th.ap, ACT.Sqrt, tq)
                v_tt(i.ap, i.ap, th.ap, MUL, tq)
                th.done((V.sem, V.count))
                t3 = V.put(lambda e: e.tensor_tensor_scan(xc.ap, r.ap, i.ap, 0.0, MUL, ADD), (ta,))
                r.done(t3)
                i.done(t3)
                st["h", c] = (xc, t3)
            later(step, first=True)

        def lru_gate(c, bank, tok):
            g = tiles.get()
            t = scaled(g.ap, bank, n_mix, tok, *g.w)
            t = a_act(g.ap, g.ap, ACT.Gelu_apprx_tanh, t)

            def step():
                h, th = st["h", c]
                t2 = v_tt(h.ap, h.ap, g.ap, MUL, t, th)
                g.done(t2)
                st["ya", c] = (h, t2)
                if c == 1:
                    out_norm(0, [st["ya", 0][0], h], [st["ya", 0][1], t2])
            later(step, first=True)

        def sc_b(c, bank, tok):
            b = tiles.get()
            st["b", c] = (b, scaled(b.ap, bank, n_mix, tok, *b.w))

        def sc_c(c, bank, tok):
            b = tiles.get()
            st["c", c] = (b, scaled(b.ap, bank, n_mix, tok, *b.w))

        def sc_x(c, bank, tok):
            pad = pads.get()
            v_set(pad.ap[:, 0:2], 0.0, *pad.w)
            scaled(pad.ap[:, 2:514], bank, n_mix, tok)
            cb = st["c", c][0]
            t = v_tt(pad.ap[:, 2:514], pad.ap[:, 2:514], cb.ap, MUL)
            t = conv_taps(cb.ap, pad.ap, "sc_conv_w", c, 2, 3, T, None)
            pad.done(t)
            bb = st["b", c][0]
            t = v_tt(cb.ap, cb.ap, bb.ap, MUL)
            bb.done(t)
            st["yb", c] = (cb, t)
            if c == 1:
                out_norm(1, [st["yb", 0][0], cb], [st["yb", 0][1], t])

        def fg(c, bank, tok):
            f = tiles.get()
            t = scaled(f.ap, bank, n_mix, tok, *f.w)
            g = tiles.get()
            tg = a_act(g.ap, f.ap, ACT.Sigmoid, t, *g.w, bias=pcol("fg_bias"))

            def gates():
                bank = banks.get()
                for b in range(4):
                    t2 = tr(bank.ap[:, 128 * b:128 * b + 128], g.ap[:, 128 * b:128 * b + 128], tg,
                            *bank.w, inc=b == 3)
                g.done(t2)
                src = bank.ap.rearrange("p (a b) -> p a b", b=128)[:, :, 32:44]
                t3 = v_copy(GT[:, :, :], src, t2)
                bank.done(t3)
                st["gt"] = v_ts(GT[:, 0, 0:4], GT[:, 0, 0:4], cc("rowmask", 1), None, MUL, None, C4TOK)
            later(gates)
            y, e_, u, l, w_, wt = f, *(tiles.get() for _ in range(5))
            free = [x for bb in (e_, u, l, w_, wt) for x in bb.w]
            c4 = slice(0, 4)
            v_ts(y.ap[c4], y.ap[c4], PRM[0:4, POFF["fg_bias"]:POFF["fg_bias"] + 1], None, ADD, None, tg,
                 *free)
            v_ts(w_.ap[c4], y.ap[c4], 0.0, None, ALU.min, None)
            t = v_stt(u.ap[c4], y.ap[c4], -1.0, y.ap[c4], MUL, ALU.max)
            t = a_act(e_.ap[c4], u.ap[c4], ACT.Exp, t, scale=-1.0)
            log1p_of(u.ap[c4], e_.ap[c4], 1.0, u.ap[c4], l.ap[c4], wt.ap[c4], t)
            v_tt(w_.ap[c4], u.ap[c4], w_.ap[c4], SUB)
            v_set(u.ap[c4], 1.0)
            cbuf = tiles.get()
            t = V.put(lambda e: e.tensor_tensor_scan(cbuf.ap[c4], u.ap[c4], w_.ap[c4], 0.0, MUL, ADD),
                      cbuf.w)
            for b in (y, e_, u, l, w_, wt):
                b.done(t, (A.sem, A.count))
            st["cum"] = (cbuf, t)

        mask = cc("mask", ML)

        def master(view):
            return lambda u: view[:, 384 - 128 * u:512]

        def half(ap, p):
            return ap[64 * p:64 * p + 64, :]

        def finish_pair(obank, t, g, c, key):
            y = tiles.get()
            t2 = v_copy(y.ap, obank.ap, t, *y.w)
            obank.done(t2)
            st[key, c] = (y, t2)
            if c == 1:
                out_norm(g, [st[key, 0][0], y], [st[key, 0][1], t2])

        def fox(j, bank, tok):
            c, kind = divmod(j, 3)
            b = tiles.get()
            t = scaled(b.ap, bank, n_mix, tok, *b.w)
            if kind < 2:
                got = head_norm(b, t, G8[:, 0:1] if kind == 0 else pcol("fox_qk", 1))
                st["fox", kind] = (b, got)
                return
            vt = tiles.get()
            got = to_tokens(b.ap, t, vt.ap, *vt.w, done=lambda x: b.done(x))
            q, qt = st["fox", 0]
            k, kt = st["fox", 1]
            ob = []
            cum, ctok = st["cum"]
            heads = []
            for p in range(2):
                h = 2 * c + p
                sel = ident[0:4, h:h + 1].to_broadcast([4, 128])

                def out(p=p):
                    if p == 0:
                        ob.append(banks.get())
                        return half(ob[0].ap, 0), ob[0].w
                    return half(ob[0].ap, 1), ()

                def after(t, p=p):
                    if p == 1:
                        for x in (q, k, vt):
                            x.done(t)
                        if c == 1:
                            cum.done(t)
                        finish_pair(ob[0], t, 2, c, "yc")
                heads.append(head(
                    half(q.ap, p), half(k.ap, p),
                    lambda jj, p=p: vt.ap[:, 128 * jj + 64 * p:128 * jj + 64 * p + 64], (qt, kt), (got,),
                    master(mask), lambda: C4TOK, True, out, True, True, extra=(sel, cum.ap[0:4], ctok),
                    after=after))
            attend(heads)

        W1 = PT[:, :, :, :].rearrange("p a b n -> p (a b n)")

        def nsa_kv(j, bank, tok):
            b = tiles.get()
            t = scaled(b.ap, bank, n_mix, tok, *b.w)
            if j == 0:
                blk = [tiles.get() for _ in range(4)]
                pos = PRM[:, POFF["cmp_pos"]:POFF["cmp_pos"] + 32]
                for i in range(4):
                    v_set(blk[i].ap, 0.0, *blk[i].w)
                for i in range(4):
                    l0 = 8 * i
                    for br in range(2):
                        r = slice(64 * br, 64 * br + 64)
                        o = blk[i].ap[r].rearrange("p (l n) -> p l n", n=64)[:, :, 32 * br:32 * br + 31]
                        src = b.ap[r, 16 * (l0 // 16):16 * (l0 // 16) + 496]
                        src = src.rearrange("p (n l) -> p l n", l=16)[:, l0 % 16:l0 % 16 + 8, :]
                        pp = pos[r, l0:l0 + 8].unsqueeze(2).to_broadcast([64, 8, 31])
                        tb = v_tt(o, src, pp, ADD)
                b.done(tb)

                def product(l0):
                    def f():
                        if l0 == 0:
                            st["cb"] = banks.get()
                        bk = st["cb"]
                        for l in range(l0, l0 + 8):
                            th = mm(bk.ap[0:64, 0:128], blk[l // 8].ap[:, 64 * (l % 8):64 * (l % 8) + 64],
                                    W1[:, 128 * l:128 * l + 128], l == 0, l == 31, w1t, tb, *bk.w,
                                    inc=l == 31)
                        if l0 < 24:
                            return
                        hid = tiles.get()
                        t = a_act(hid.ap[0:64, 0:128], bk.ap[0:64, 0:128], ACT.Gelu_apprx_tanh, th, *hid.w)
                        bk.done(t)
                        st["hid"] = (hid, t)
                        for x in blk:
                            x.done(th)
                        pt_free[0] = pt_free[1] = (th,)
                    return f

                def step():
                    bk = banks.get()
                    hid, t = st["hid"]
                    t = PE.put(lambda e, bk=bk: e.transpose(bk.ap[:, 0:64], hid.ap[0:64, 0:128],
                                                            ident[0:64, 0:64]), (t, C3TOK, *bk.w), True)
                    hid.done(t)
                    ht = tiles.get()
                    t = v_copy(ht.ap[:, 0:64], bk.ap[:, 0:64], t, *ht.w)
                    bk.done(t)
                    bk = banks.get()
                    tk = mm(bk.ap[:, 0:31], W2[:, 0:128], ht.ap[:, 0:31], True, True, w2t, t, *bk.w, inc=True)
                    tk = v_copy(KC[:, 0:31], bk.ap[:, 0:31], tk)
                    bk.done(tk)
                    bv = banks.get()
                    tv = mm(bv.ap[0:31, 0:64], ht.ap[:, 32:63], W2[:, 128:192], True, True, *bv.w, inc=True)
                    ht.done(tv)
                    st["vc"] = v_copy(VC[0:31, 0:64], bv.ap[0:31, 0:64], tv)
                    bv.done(st["vc"])
                    sq = tiles.get()
                    r = tiles.get()
                    t = a_act(sq.ap[:, 0:31], KC[:, 0:31], ACT.Square, tk, *sq.w)

                    def fin():
                        bk = banks.get()
                        t2 = mm(bk.ap[:, 0:31], bones, sq.ap[:, 0:31], True, True, t, *bk.w, inc=True)
                        sq.done(t2)
                        t2 = a_act(r.ap[:, 0:31], bk.ap[:, 0:31], ACT.Ln, t2, *r.w, scale=1.0 / 64, bias=eps)
                        bk.done(t2)
                        t2 = a_act(r.ap[:, 0:31], r.ap[:, 0:31], ACT.Exp, scale=-0.5)
                        st["kc"] = v_stt(KC[:, 0:31], KC[:, 0:31], pcol("nsa_qk", 1), r.ap[:, 0:31], MUL, MUL,
                                         t2)
                        r.done(st["kc"])
                    bg.appendleft((at["tile"] + 3, fin))
                for l0 in range(0, 32, 8):
                    later(product(l0))
                later(step)
            elif j < 3:
                st["nk", j] = (b, head_norm(b, t, pcol("nsa_qk", 1 + j)))
            else:
                vt = tiles.get()
                st["nv"] = (vt, to_tokens(b.ap, t, vt.ap, *vt.w, done=lambda x: b.done(x)))

        def nsa_q(c, bank, tok):
            b = tiles.get()
            t = scaled(b.ap, bank, n_mix, tok, *b.w)
            qt = head_norm(b, t, G8[:, 1:2])
            vt, vtok = st["nv"]
            ob = []
            heads = []

            def cmp_head(p):
                h = 2 * c + p

                def f():
                    pc = tiles.get()
                    hold = []
                    for u in range(4):
                        bk = banks.get()
                        s = tiles.get()
                        t1 = mm(bk.ap[:, 0:31], half(b.ap, p)[:, 128 * u:128 * u + 128],
                                half(KC, p)[:, 0:31], True, True, qt[0], st["kc"], *bk.w, inc=True)
                        mx, nm, sm, rc = small(), small(), small(), small()
                        a0 = 415 - 128 * u
                        bias = BI[:, h, a0:a0 + 481:16]
                        t1 = v_add_max(s.ap[:, 0:31], bk.ap[:, 0:31], bias, mx, t1, st["rel"], *s.w)
                        bk.done(t1)
                        t1 = v_ts(nm, mx, -1.0, None, MUL, None)
                        t1 = a_act(s.ap[:, 0:31], s.ap[:, 0:31], ACT.Exp, t1, bias=nm, acc=sm)
                        hold.append((s, sm, rc, t1))
                    bk = banks.get()
                    for u in range(4):
                        s, sm, rc, t1 = hold[u]
                        v_rec(rc, sm, t1)
                        t1 = v_ts(s.ap[:, 0:31], s.ap[:, 0:31], rc, GT[:, u, h:h + 1], MUL, MUL, st["gt"])
                        t2 = PE.put(lambda e, s=s, u=u, bk=bk: e.transpose(
                            bk.ap[0:31, 128 * u:128 * u + 128], s.ap[:, 0:31], ident), (t1, *bk.w), True)
                        s.done(t2)
                    t3 = a_copy(pc.ap[0:31, :], bk.ap[0:31, :], t2, *pc.w)
                    bk.done(t3)
                    if p == 0:
                        ob.append(banks.get())
                    t4 = mm(half(ob[0].ap, p), VC[0:31, 0:64], pc.ap[0:31, :], True, False, t3, st["vc"],
                            *(ob[0].w if p == 0 else ()), inc=True)
                    pc.done(t4)
                return f

            for p in range(2):
                later(cmp_head(p))
                h = 2 * c + p
                for br in range(2):
                    kb, kt = st["nk", 1 + br]

                    def out(p=p):
                        return half(ob[0].ap, p), ()

                    def after(t, p=p, br=br):
                        if br == 1 and p == 1:
                            b.done(t)
                            if c == 1:
                                vt.done(t)
                                for i in (1, 2):
                                    st["nk", i][0].done(t)
                            finish_pair(ob[0], t, 3, c, "yd")
                    heads.append(head(
                        half(b.ap, p), half(kb.ap, p),
                        lambda jj, br=br: vt.ap[:, 128 * jj + 64 * br:128 * jj + 64 * br + 64], (qt, kt),
                        (vtok,), master(BI[:, h, :]), lambda: st["rel"], True, out, False, br == 1,
                        gate=lambda u, br=br, h=h: GT[:, u, 4 + 4 * br + h:5 + 4 * br + h], after=after))
            attend(heads)

        MIX = ([(nsa_kv, j) for j in range(4)] + [(fg, 0)] + [(fox, j) for j in range(6)]
               + [(nsa_q, 0), (nsa_q, 1)] + [(lru_in, 0), (lru_in, 1), (lru_gate, 0), (lru_gate, 1)]
               + [(f, c) for c in range(2) for f in (sc_b, sc_c, sc_x)])

        def mix_evac(m, bank, tok):
            if m == 2:
                for h in range(4):
                    st["rel"] = p_tt(BI[:, h, :], BI[:, h, :], mask, ADD, rel_in[h], C4TOK)
            f, arg = MIX[m]
            f(arg, bank, tok)

        linear(norm["mv"], 23, mix_evac, mid=lambda: norm_stats(norm), pace=1)
        flush()
        norm_end(norm)

        def residual(nxt):
            def evac(m, bank, tok):
                t = add_x(bank, m, tok)
                if nxt is not None:
                    norm_chunk(nxt, m, t)
            return evac

        def ffn(norm, nxt, layer, final=False):
            hid = {}
            cur = {}

            def plain(m, bank, tok, off, base):
                g, up = m % 2 == 0, m % 2 == 1
                b = tiles.get()
                t = scaled(b.ap, bank, norm, tok, *b.w)
                if g:
                    t = a_act(b.ap, b.ap, ACT.Silu, t)
                    cur["g"] = (b, t)
                else:
                    gb, gt = cur["g"]
                    t = v_tt(b.ap, b.ap, gb.ap, MUL, gt)
                    gb.done(t)
                    hid[m // 2] = split_to(m // 2, b.ap, t, b)

            def conv(m, bank, tok, off, base):
                ch = (off + m // 2) + (22 if m % 2 == 0 else 0)
                pad = pads.get()
                v_set(pad.ap[:, 0:1], 0.0, *pad.w)
                v_set(pad.ap[:, 513:514], 0.0)
                scaled(pad.ap[:, 1:513], bank, norm, tok)
                b = tiles.get()
                wn = 132 * layer
                t = v_ts(b.ap, pad.ap[:, 1:513], pcol("ffn_dw_w", wn + 44 + ch),
                         pcol("ffn_dw_b", 44 * layer + ch), MUL, ADD, *b.w)
                v_stt(b.ap, pad.ap[:, 0:512], pcol("ffn_dw_w", wn + ch), b.ap, MUL, ADD)
                t = v_stt(b.ap, pad.ap[:, 2:514], pcol("ffn_dw_w", wn + 88 + ch), b.ap, MUL, ADD)
                pad.done(t)
                if m % 2 == 0:
                    t = a_act(b.ap, b.ap, ACT.Gelu_apprx_tanh, t)
                    cur["g"] = (b, t)
                else:
                    gb, gt = cur["g"]
                    t = v_tt(b.ap, b.ap, gb.ap, MUL, gt)
                    gb.done(t)
                    hid[m // 2] = split_to(m // 2, b.ap, t, b)

            fn = plain if layer is None else conv
            for i, (a, b) in enumerate(FF_PARTS):
                hid.clear()
                linear(norm["mv"], 2 * (b - a), lambda m, bank, tok: fn(m, bank, tok, a, i),
                       mid=lambda: norm_stats(norm) if i == 0 else None)
                mv = [hid[k] for k in range(b - a)]
                if i < len(FF_PARTS) - 1:
                    linear(mv, 8, lambda m, bank, tok: add_x(bank, m, tok))
                else:
                    norm_end(norm)
                    if final:
                        def last(m, bank, tok):
                            t = add_x(bank, m, tok)
                            load(out[m, :, :], X[:, m, :], s_out, t)
                        linear(mv, 8, last)
                    else:
                        linear(mv, 8, residual(nxt))

        v_ts(G8[:, 2:3], pcol("nat_q"), 0.125, None, MUL, None, C2TOK)
        n_ffn = new_norm("norm_ffn")
        linear([mixed[k] for k in OUT_ORDER], 8, residual(n_ffn))
        norm = new_norm("norm1")
        ffn(n_ffn, norm, None)

        def conv_layer(norm, nxt, ci):
            cur = {}
            outs = []
            sums = []
            idle = (*pt_free[0], *pt_free[1], (V.sem, V.count), (P.sem, P.count))
            diag = Ring([PT[:, i, j, :] for i in range(2) for j in range(4)])
            flat = BI[:, :, :].rearrange("p a b -> p (a b)")
            stage = Ring([flat[:, T * i:T * i + T] for i in range(7)])
            for ring in (diag, stage):
                ring.free = deque((ap, idle) for ap, _ in ring.free)

            def tap(c, j):
                return pcol("conv_dw_w", 248 * ci + 31 * c + j)

            def evac(m, bank, tok):
                c = m // 2
                if m % 2 == 0:
                    g = tiles.get()
                    t = scaled(g.ap, bank, norm, tok, *g.w)
                    cur["g"] = (g, a_act(g.ap, g.ap, ACT.Sigmoid, t, bias=pcol("conv_b_in", 16 * ci + 8 + c)))
                    return
                pad = pads.get()
                v_set(pad.ap[:, 0:15], 0.0, *pad.w)
                v_set(pad.ap[:, 527:542], 0.0)
                scaled(pad.ap[:, 15:527], bank, norm, tok)
                g, gt = cur["g"]
                u_done = v_stt(pad.ap[:, 15:527], pad.ap[:, 15:527], pcol("conv_b_in", 16 * ci + c), g.ap,
                               ADD, MUL, gt)
                g.done(u_done)
                dg = [diag.get() for _ in range((TAPS_PE + 3) // 4)]
                dgs = [dg[j // 4].ap[:, 128 * (j % 4):128 * (j % 4) + 128] for j in range(TAPS_PE)]
                for j in range(TAPS_PE):
                    dg_done = a_act(dgs[j], ident, ACT.Copy, *dg[j // 4].w, scale=tap(c, j), own=False)
                po = stage.get()
                free = po.w
                for j in range(TAPS_PE, TAPS_PE + TAPS_POOL):
                    s = stage.get()
                    t = a_act(s.ap, pad.ap[:, j:j + T], ACT.Copy, u_done, *s.w, *free, scale=tap(c, j),
                              own=False)
                    if j == TAPS_PE:
                        first = s
                        continue
                    pool_done = p_tt(po.ap, first.ap if j == TAPS_PE + 1 else po.ap, s.ap, ADD, t)
                    s.done(pool_done)
                    if j == TAPS_PE + 1:
                        first.done(pool_done)
                o = tiles.get()
                j0 = TAPS_PE + TAPS_POOL
                v_ts(o.ap, pad.ap[:, j0:j0 + T], tap(c, j0), pcol("conv_dw_b", 8 * ci + c), MUL, ADD, *o.w)
                o2 = tiles.get()
                two = [(o, (V.sem, V.count))]
                two.append((o2, v_ts(o2.ap, pad.ap[:, j0 + 1:j0 + 1 + T], tap(c, j0 + 1), None, MUL, None,
                                     *o2.w, own=False)))
                for j in range(j0 + 2, 31):
                    x, before = two[0]
                    two = [two[1], (x, v_stt(x.ap, pad.ap[:, j:j + T], tap(c, j), x.ap, MUL, ADD, before,
                                             own=False))]
                v_done = v_tt(o.ap, o.ap, o2.ap, ADD)
                o2.done(v_done)

                def join():
                    bk = banks.get()
                    for j in range(TAPS_PE):
                        t = mm(bk.ap, dgs[j], pad.ap[:, j:j + T], j == 0, j == TAPS_PE - 1, dg_done,
                               u_done, *bk.w, inc=j == TAPS_PE - 1)
                    for x in dg:
                        x.done(t)
                    pad.done(t, v_done, pool_done)
                    v_tt(o.ap, o.ap, bk.ap, ADD, t)
                    bk.done((V.sem, V.count))
                    t = v_tt(o.ap, o.ap, po.ap, ADD, pool_done)
                    po.done(t)
                    outs.append((o, t))
                    if len(outs) > 1:
                        add_up()
                later(join)

            def add_up():
                k = len(sums)
                if k == 0:
                    cur["sum"] = banks.get()
                o, t = outs[k]
                sums.append(mm(cur["sum"].ap, ones, o.ap, k == 0, k == 7, t, *cur["sum"].w, inc=k == 7))

            linear(norm["mv"], 16, evac, mid=lambda: norm_stats(norm))
            norm_end(norm)
            flush()
            add_up()
            bank, tm = cur["sum"], sums[7]
            pt_free[0] = pt_free[1] = ((PE.sem, PE.count),)
            mu = tiles.get()
            tm = a_act(mu.ap, bank.ap, ACT.Copy, tm, *mu.w, scale=1.0 / D)
            bank.done(tm)
            bank = banks.get()
            for k, (o, t) in enumerate(outs):
                t = v_tt(o.ap, o.ap, mu.ap, SUB, tm, t, own=False)
                s = tiles.get()
                t2 = a_act(s.ap, o.ap, ACT.Square, t, *s.w, own=False)
                t3 = mm(bank.ap, ones, s.ap, k == 0, k == 7, t2, *bank.w, inc=True)
                s.done(t3)
            mu.done(t)
            r = tiles.get()
            t3 = a_act(r.ap, bank.ap, ACT.Ln, t3, *r.w, scale=1.0 / D, bias=eps)
            bank.done(t3)
            t3 = a_act(r.ap, r.ap, ACT.Exp, scale=-0.5)
            mv = []
            for k, (o, _) in enumerate(outs):
                t = v_tt(o.ap, o.ap, r.ap, MUL, t3)
                t = a_act(o.ap, o.ap, ACT.Silu, t, scale=pcol("conv_ln_g", 8 * ci + k),
                          bias=pcol("conv_ln_b", 8 * ci + k))
                mv.append(split_to(k, o.ap, t, o))
            r.done((V.sem, V.count))
            linear(mv, 8, residual(nxt))

        def nat_layer(norm, nxt):
            mv = [None] * 8
            cur = {}
            used = [((V.sem, V.count), (P.sem, P.count))] * 4
            colmask = cc("colmask", 64).unsqueeze(1).to_broadcast([128, 14, 64])

            def evac(m, bank, tok):
                c, kind = divmod(m, 3)
                b = tiles.get()
                t = scaled(b.ap, bank, norm, tok, *b.w)
                if kind < 2:
                    cur[kind] = (b, head_norm(b, t, G8[:, 2:3] if kind == 0 else pcol("nat_k")))
                    return
                vt = tiles.get()
                got = to_tokens(b.ap, t, vt.ap, *vt.w, done=lambda x: b.done(x))
                q, qt = cur[0]
                k, kt = cur[1]
                ob = []
                heads = []
                for p in range(2):
                    h = 2 * c + p
                    slot = h % 4
                    a = load_bi(slot, natb[h, :, :], *used[slot])
                    view = BI[:, slot, :].rearrange("p (a b) -> p a b", b=64)
                    bt = p_tt(view, view, colmask, ADD, a)

                    def out(p=p):
                        if p == 0:
                            ob.append(banks.get())
                            return half(ob[0].ap, 0), ob[0].w
                        return half(ob[0].ap, 1), ()

                    def after(t, p=p, slot=slot):
                        used[slot] = ((V.sem, V.count),)
                        if p == 1:
                            for x in (q, k, vt):
                                x.done(t)
                            y = tiles.get()
                            t2 = v_copy(y.ap, ob[0].ap, t, *y.w)
                            ob[0].done(t2)
                            mv[c] = split_to(c, y.ap, t2, y)
                    heads.append(head(
                        half(q.ap, p), half(k.ap, p),
                        lambda jj, p=p: vt.ap[:, 128 * jj + 64 * p:128 * jj + 64 * p + 64], (qt, kt), (got,),
                        lambda u, view=view: view[:, 6 - 2 * u:14 - 2 * u, :], lambda bt=bt: bt, False, out,
                        True, True, after=after, bias2d=True))
                attend(heads)

            linear(norm["mv"], 24, evac, mid=lambda: norm_stats(norm), pace=1)
            flush()
            norm_end(norm)
            linear(mv, 8, residual(nxt))

        def ret_layer(norm, nxt):
            dec = PRM[:, POFF["ret_dec"]:POFF["ret_dec"] + 8]
            e_, u, l, w_, lg, nl = (small(8) for _ in range(6))
            t = a_act(e_, dec, ACT.Exp, (V.sem, V.count), scale=-math.log(2.0))
            log1p_of(lg, e_, -1.0, u, l, w_, t)
            lt = v_ts(nl, lg, -1.0, None, MUL, None)
            LG = SM[:, 142:150]
            NL = SM[:, 150:158]
            v_copy(LG, lg)
            lt = v_copy(NL, nl)
            free = ((V.sem, V.count), (P.sem, P.count))
            rt = [load_bi(1, rope[0, :, :], *free), load_bi(2, rope[1, :, :], *free)]
            dt_ = load_bi(3, dist, *free)
            cosv, sinv, dv = BI[:, 1, 0:T], BI[:, 2, 0:T], BI[:, 3, :]
            dm = BI[:, 0, :]
            mvs = [None] * 8
            dfree = [()]

            def head(h):
                qk, vts, gs = {}, [], []
                v_ts(dm, dv, NL[:, 4 + h:5 + h], None, MUL, None, dt_, lt, *dfree[0])
                t = v_stt(dm, dv, LG[:, h:h + 1], dm, MUL, ALU.min)
                dmt = a_act(dm, dm, ACT.Exp, t)

                def evac(m, bank, tok):
                    b = tiles.get()
                    t = scaled(b.ap, bank, norm, tok, *b.w)
                    if m < 4:
                        kind, part = divmod(m, 2)
                        qk[m] = (b, t)
                        if part == 1:
                            x1, x2 = qk[2 * kind][0], b
                            a, c = tiles.get(), tiles.get()
                            v_tt(a.ap, x2.ap, sinv, MUL, rt[1], *a.w)
                            v_tt(c.ap, x1.ap, sinv, MUL, *c.w)
                            v_tt(x1.ap, x1.ap, cosv, MUL, rt[0])
                            t1 = v_tt(x1.ap, x1.ap, a.ap, SUB)
                            v_tt(x2.ap, x2.ap, cosv, MUL)
                            t2 = v_tt(x2.ap, x2.ap, c.ap, ADD)
                            a.done(t2)
                            c.done(t2)
                            if kind == 1:
                                t1 = v_ts(x1.ap, x1.ap, 0.0625, None, MUL, None)
                                t2 = v_ts(x2.ap, x2.ap, 0.0625, None, MUL, None)
                            qk[2 * kind] = (x1, t1)
                            qk[2 * kind + 1] = (x2, t2)
                    elif m < 8:
                        vt = tiles.get()
                        vts.append((vt, to_tokens(b.ap, t, vt.ap, *vt.w, done=lambda x: b.done(x))))
                    else:
                        gs.append((b, a_act(b.ap, b.ap, ACT.Silu, t)))

                linear(norm["mv"], 12, evac, mid=(lambda: norm_stats(norm)) if h == 0 else None, pace=1)
                flush()
                pt = h % 2
                for j in range(4):
                    bank = banks.get()
                    for d in range(2):
                        t = mm(bank.ap, qk[2 + d][0].ap[:, 128 * j:128 * j + 128], qk[d][0].ap, d == 0,
                               d == 1, qk[2 + d][1], qk[d][1], *bank.w, inc=d == 1)
                    t = v_tt(PT[:, pt, j, :], bank.ap, dm[:, 384 - 128 * j:896 - 128 * j], MUL, t, dmt,
                             *pt_free[pt])
                    bank.done(t)
                    pts = t
                dfree[0] = (pts,)
                for i in range(4):
                    qk[i][0].done((V.sem, V.count), (PE.sem, PE.count))
                os = []
                for c in range(4):
                    bank = banks.get()
                    for j in range(4):
                        t = mm(bank.ap, vts[c][0].ap[:, 128 * j:128 * j + 128], PT[:, pt, j, :], j == 0,
                               j == 3, pts, vts[c][1][0], *bank.w, inc=j == 3)
                    vts[c][0].done(t)
                    o = tiles.get()
                    t = a_copy(o.ap, bank.ap, t, *o.w)
                    bank.done(t)
                    os.append((o, t))
                pt_free[pt] = ((PE.sem, PE.count),)
                hold = {}

                def mean():
                    bank = banks.get()
                    for c in range(4):
                        t = mm(bank.ap, ones, os[c][0].ap, c == 0, c == 3, os[c][1], *bank.w, inc=c == 3)
                    mu = tiles.get()
                    tm = a_act(mu.ap, bank.ap, ACT.Copy, t, *mu.w, scale=1.0 / 512)
                    bank.done(tm)
                    hold["sq"] = []
                    for c in range(4):
                        o = os[c][0]
                        t = v_tt(o.ap, o.ap, mu.ap, SUB, tm)
                        s = tiles.get()
                        hold["sq"].append((s, a_act(s.ap, o.ap, ACT.Square, t, *s.w)))
                    mu.done(t)

                def variance():
                    bank = banks.get()
                    for c in range(4):
                        s, t2 = hold["sq"][c]
                        t3 = mm(bank.ap, ones, s.ap, c == 0, c == 3, t2, *bank.w, inc=True)
                        s.done(t3)
                    r = tiles.get()
                    t3 = a_act(r.ap, bank.ap, ACT.Ln, t3, *r.w, scale=1.0 / 512, bias=eps)
                    bank.done(t3)
                    t3 = a_act(r.ap, r.ap, ACT.Exp, scale=-0.5)
                    for c in range(4):
                        o = os[c][0]
                        v_stt(o.ap, o.ap, pcol("ret_gn", 4 * h + c), r.ap, MUL, MUL, t3)
                        g, gt = gs[c]
                        t = v_tt(o.ap, o.ap, g.ap, MUL, gt)
                        g.done(t)
                        mvs[4 * (h % 2) + c] = split_to(4 * (h % 2) + c, o.ap, t, o)
                    r.done(t)
                later(mean, 2)
                later(variance, 9)

            for h in range(4):
                head(h)
                if h == 2:
                    linear(list(mvs), 8, lambda m, bank, tok: add_x(bank, m, tok), hold=True)
            norm_end(norm)
            flush()
            linear(list(mvs), 8, residual(nxt))

        for layer in range(4):
            n2 = new_norm("norm2", 8 * layer)
            if layer in (0, 3):
                conv_layer(norm, n2, layer // 3)
            elif layer == 1:
                nat_layer(norm, n2)
            else:
                ret_layer(norm, n2)
            norm = new_norm("norm1", 8 * (layer + 1)) if layer < 3 else None
            ffn(n2, norm, layer, final=layer == 3)
        assert at["tile"] == N_TILES and not bg and not soon

        block = ctx.enter_context(nc.Block())

        @block.sync
        def _(e):
            SP.run(e)
            e.wait_ge(s_out, 128)

        @block.vector
        def _(e):
            V.run(e)

        @block.scalar
        def _(e):
            A.run(e)

        @block.gpsimd
        def _(e):
            P.run(e)

        @block.tensor
        def _(e):
            PE.run(e)


def rel_buckets():
    d = np.arange(0, 1024)
    large = 16 + (np.log(np.maximum(d, 1).astype(np.float32) / np.float32(16))
                  / np.float32(math.log(128 / 16)) * np.float32(16)).astype(np.int32)
    return np.where(d < 16, d, np.minimum(large, 31))


def constants():
    q = np.arange(128)
    c = {}
    c["ident"] = np.eye(128)
    c["ones"] = np.ones((128, 128))
    c["bones"] = np.kron(np.eye(2), np.ones((64, 64)))
    dist = q[:, None] + 384 - np.arange(ML)[None, :]
    c["mask"] = np.where(dist < 0, NEG, 0.0)
    col = q % 64
    first = np.clip(col - 8, 0, 48)
    kc = np.arange(64)
    c["colmask"] = np.where((kc[None] >= first[:, None]) & (kc[None] < first[:, None] + 16), 0.0, NEG)
    c["rowmask"] = (q >= 31).astype(float)[:, None]
    cst = np.concatenate([c[n] for n, _ in CONSTS], axis=1).astype(np.float32)
    theta = (np.float32(1.0) / (np.float32(10000.0) ** np.linspace(0.0, 1.0, 128, dtype=np.float32))).astype(np.float32)
    ang = (theta[:, None] * np.arange(T, dtype=np.float32)[None, :]).astype(np.float32)
    rope = np.stack([np.cos(ang.astype(np.float64)), np.sin(ang.astype(np.float64))]).astype(np.float32)
    rdist = (np.arange(ML)[None, :] - 384 - q[:, None]).astype(np.float32)
    return cst, rope, rdist


def kernel(**inp):
    import concourse.bacc as bacc
    from concourse.bass_utils import run_bass_kernel_spmd

    g = {k: np.asarray(v) for k, v in inp.items()}
    f32 = np.float32

    def cols(v):
        return np.ascontiguousarray(v.reshape(-1, 128).T)

    def twice(v):
        return np.concatenate([v, v], axis=-1)

    w_in = g["w_in"][0]
    order = list(range(0, 512))
    for c in range(2):
        for base in (512, 768, 1024):
            order += list(range(base + 128 * c, base + 128 * c + 128))
    parts = []
    fgw = np.zeros((D, 128), f32)
    fgw[:, 0:4] = w_in[:, 2048:2052]
    fgw[:, 32:44] = w_in[:, 2692:2704]
    parts.append(fgw)
    for c in range(2):
        for base in (1280, 1536, 1792):
            parts.append(w_in[:, base + 128 * c:base + 128 * c + 128])
    kv = [w_in[:, 2308 + 64 * j:2372 + 64 * j] for j in range(6)]
    parts = ([kv[0], kv[1], kv[2], kv[2], kv[4], kv[4], kv[3], kv[5]] + parts
             + [w_in[:, 2052:2308], w_in[:, order]])
    W = {"w_in": np.concatenate(parts, axis=1), "w_out": np.concatenate([g["w_out"][0][128 * k:128 * k + 128] for k in OUT_ORDER])}

    def pairs(first, second):
        n = first.shape[1] // 128
        a = first.reshape(D, n, 1, 128)
        b = second.reshape(D, n, 1, 128)
        return np.concatenate([a, b], axis=2).reshape(D, 2 * n * 128)

    def ffn(name, up, down):
        for i, (a, b) in enumerate(FF_PARTS):
            W[f"{name}_up{i}"] = up[:, 256 * a:256 * b]
            W[f"{name}_down{i}"] = down[128 * a:128 * b, :]

    F = 2816
    gu = g["w_gate_up"][0]
    ffn("ffn", pairs(gu[:, :F], gu[:, F:]), g["w_down"][0])
    for i in range(2):
        w = g["conv_w_in_2"][i]
        W[f"conv_in{i}"] = pairs(w[:, D:], w[:, :D])
        W[f"conv_out{i}"] = g["conv_w_out_2"][i]
    w = g["nat_w_qkv_2"][0]
    W["nat_qkv"] = w.reshape(D, 3, 8, 128).transpose(0, 2, 1, 3).reshape(D, 3072)
    W["nat_out"] = g["nat_w_out_2"][0]
    w = g["ret_w_in_2"][0]
    for h in range(4):
        W[f"ret_in{h}"] = np.concatenate([w[:, 256 * h:256 * h + 256], w[:, 1024 + 256 * h:1280 + 256 * h],
                                          w[:, 2048 + 512 * h:2560 + 512 * h],
                                          w[:, 4096 + 512 * h:4608 + 512 * h]], axis=1)
    for i in range(2):
        W[f"ret_out{i}"] = g["ret_w_out_2"][0][1024 * i:1024 * i + 1024]
    for layer in range(4):
        up = g["ffn_w_up_2"][layer]
        ffn(f"ffn2_{layer}", pairs(up[:, F:], up[:, :F]), g["ffn_w_down_2"][layer])
    flat = np.zeros((N_BLOCKS * 8, 128, 128), f32)
    at = 0
    for name, kc, mc in linears():
        w = W[name]
        flat[at:at + kc * mc] = w.reshape(kc, 128, mc, 128).transpose(2, 0, 1, 3).reshape(-1, 128, 128)
        at += kc * mc
    wst = np.ascontiguousarray(flat.reshape(N_BLOCKS, 8, 128, 128).transpose(0, 2, 1, 3)).reshape(
        N_BLOCKS, 128, 1024)

    p = {}
    p["norm_mix"] = cols(g["norm_mix"])
    p["lru_conv_w"] = cols(g["lru_conv_w"])
    p["lru_conv_b"] = cols(g["lru_conv_b"])
    p["lru_b"] = cols(g["lru_b_gates"])
    p["lru_lambda"] = cols(g["lru_lambda"])
    p["sc_conv_w"] = cols(g["sc_conv_w"])
    p["fox_qk"] = cols(twice(g["fox_qk_norm"]))
    p["nsa_qk"] = cols(twice(g["nsa_qk_norm"]))
    fb = np.zeros((128, 1), f32)
    fb[0:4, 0] = g["fox_f_bias"][0]
    fb[32:44, 0] = g["nsa_gate_bias"][0]
    p["fg_bias"] = fb
    p["cmp_pos"] = g["nsa_cmp_pos"][0].transpose(0, 2, 1).reshape(128, 32)
    p["out_norm"] = cols(g["out_norm"])
    p["norm_ffn"] = cols(g["norm_ffn"])
    p["norm1"] = cols(g["norm1_g_2"])
    p["norm2"] = cols(g["norm2_g_2"])
    p["conv_b_in"] = cols(g["conv_b_in_2"])
    p["conv_dw_w"] = g["conv_dw_w_2"].reshape(2, 31, 8, 128).transpose(3, 0, 2, 1).reshape(128, 496)
    p["conv_dw_b"] = cols(g["conv_dw_b_2"])
    p["conv_ln_g"] = cols(g["conv_ln_g_2"])
    p["conv_ln_b"] = cols(g["conv_ln_b_2"])
    p["nat_q"] = cols(twice(g["nat_q_norm_g_2"]))
    p["nat_k"] = cols(twice(g["nat_k_norm_g_2"]))
    p["ret_dec"] = np.broadcast_to(g["ret_log2_inv_decay_2"].reshape(1, 8), (128, 8))
    p["ret_gn"] = cols(g["ret_gn_g_2"])
    p["ffn_dw_w"] = cols(g["ffn_dw_w_2"])
    p["ffn_dw_b"] = cols(g["ffn_dw_b_2"])
    prm = np.ascontiguousarray(np.concatenate([p[n] for n, _ in PARAMS], axis=1))
    cst, rope, rdist = constants()

    gw = g["lru_w_gates"][0]
    gatew = np.zeros((128, 2, 2, 128), f32)
    for i in range(2):
        for h in range(4):
            r = 64 * (h % 2)
            gatew[r:r + 64, i, h // 2, r:r + 64] = gw[i, h]
    cmpw1 = np.ascontiguousarray(g["nsa_cmp_w1"][0].transpose(0, 2, 1, 3)).reshape(128, 4096)
    w2 = g["nsa_cmp_w2"][0]
    cmpw2 = np.ascontiguousarray(np.concatenate([w2[0], w2[0], w2[1]], axis=1))
    q = np.arange(128)
    dd = np.maximum(q[:, None] + 384 - np.arange(ML)[None, :], 0)
    relm = np.ascontiguousarray(g["rel_bias"][rel_buckets()[dd]].transpose(2, 0, 1))
    rpb = g["nat_rpb_2"][0]
    ri, col = q // 64, q % 64
    jj = np.arange(1, 15)[None, :, None] - ri[:, None, None]
    xx = np.clip(np.arange(64)[None, None, :] - col[:, None, None] + 15, 0, 30)
    natb = np.ascontiguousarray(rpb[:, jj, xx]).reshape(16, 128, ML)

    arrays = {
        "wst": wst, "xin": np.ascontiguousarray(g["x"][0].T).reshape(8, 128, T), "prm": prm, "cst": cst,
        "gatew": gatew.reshape(128, 512), "cmpw1": cmpw1, "cmpw2": cmpw2, "relm": relm, "natb": natb,
        "rope": rope, "dist": rdist,
    }
    nc = bacc.Bacc("TRN2", target_bir_lowering=False, num_devices=1)
    aps = [nc.dram_tensor(n, a.shape, mybir.dt.float32, kind="ExternalInput").ap() for n, a in arrays.items()]
    out = nc.dram_tensor("out", (8, 128, T), mybir.dt.float32, kind="ExternalOutput").ap()
    build(nc, *aps, out)
    r = run_bass_kernel_spmd(nc, [arrays], core_ids=[0])
    return np.ascontiguousarray(r.results[0]["out"].reshape(D, T).T).reshape(1, T, D)
```

```python
import math
from collections import deque
from contextlib import ExitStack

import numpy as np
import concourse.bass as bass
from concourse import mybir

T = 512
D = 1024
DC = 8
FFC = 22
EPS = 1e-6
NEG = -1.0e30
ML = 896
FF_PARTS = ((0, 8), (8, 15), (15, 22))
NRAW = 4
NSPLIT = 3
NTILE = 18
NPAD = 3
ROOM = 7
WIDE = 4
OUT_ORDER = (4, 5, 0, 1, 2, 3, 6, 7)
TAPS_PE = (6, 6, 6, 6, 6, 6, 7, 10)
TAPS_POOL = (8, 8, 8, 8, 8, 8, 8, 5)

PARAMS = (
    ("norm_mix", 8), ("lru_conv_w", 8), ("lru_conv_b", 2), ("lru_b", 4), ("lru_lambda", 2),
    ("sc_conv_w", 6), ("fox_qk", 2), ("nsa_qk", 4), ("fg_bias", 1), ("cmp_pos", 32),
    ("out_norm", 8), ("norm_ffn", 8), ("norm1", 32), ("norm2", 32), ("conv_b_in", 32),
    ("conv_dw_w", 496), ("conv_dw_b", 16), ("conv_ln_g", 16), ("conv_ln_b", 16),
    ("nat_q", 1), ("nat_k", 1), ("ret_dec", 8), ("ret_gn", 16), ("ffn_dw_w", 528), ("ffn_dw_b", 176),
)
CONSTS = (("ident", 128), ("ones", 128), ("bones", 128), ("mask", ML), ("colmask", 64), ("rowmask", 1))


def offsets(spec):
    out, at = {}, 0
    for name, n in spec:
        out[name] = at
        at += n
    return out, at


POFF, NPRM = offsets(PARAMS)
COFF, NCST = offsets(CONSTS)


def linears():
    out = [("w_in", 8, 23), ("w_out", 8, 8)]

    def ffn(name):
        for i, (a, b) in enumerate(FF_PARTS):
            out.append((f"{name}_up{i}", 8, 2 * (b - a)))
            out.append((f"{name}_down{i}", b - a, 8))

    ffn("ffn")
    for layer in range(4):
        if layer in (0, 3):
            out.append((f"conv_in{layer // 3}", 8, 16))
            out.append((f"conv_out{layer // 3}", 8, 8))
        elif layer == 1:
            out.append(("nat_qkv", 8, 24))
            out.append(("nat_out", 8, 8))
        else:
            for name, n in (("in0", 12), ("in1", 12), ("in2", 12), ("out0", 8), ("in3", 12), ("out1", 8)):
                out.append((f"ret_{name}", 8, n))
        ffn(f"ffn2_{layer}")
    return out


def wide(name):
    return WIDE if "_down" in name or name.startswith(("w_out", "conv_out", "nat_out", "ret_out1")) else 0


N_TILES = sum(k * m for _, k, m in linears())
N_BLOCKS = (N_TILES + 7) // 8




class Engine:

    def __init__(self, sem, linked):
        self.sem, self.linked = sem, linked
        self.ops, self.count = [], 0

    def put(self, fn, waits=(), inc=True, own=True):
        waits = [w for w in waits if w is not None]
        if self.linked and own and self.count:
            waits.append((self.sem, self.count))
        self.ops.append((waits, fn, inc))
        if inc:
            self.count += 1
        return (self.sem, self.count)

    def run(self, e):
        passed = {}
        for waits, fn, inc in self.ops:
            for sem, value in waits:
                if passed.get(id(sem), 0) < value:
                    passed[id(sem)] = value
                    e.wait_ge(sem, value)
            ins = fn(e)
            if inc:
                ins.then_inc(self.sem, 1)


class Ring:

    def __init__(self, aps):
        self.free = deque((ap, ()) for ap in aps)

    def get(self):
        ap, waits = self.free.popleft()
        return Buf(self, ap, waits)


class Buf:
    def __init__(self, ring, ap, waits):
        self.ring, self.ap, self.w = ring, ap, waits

    def done(self, *after):
        self.ring.free.append((self.ap, after))


def build(nc, wst, xin, prm, cst, gatew, cmpw1, cmpw2, relm, natb, rope, dist, out):
    f32 = mybir.dt.float32
    f32r = mybir.dt.float32r
    ALU = mybir.AluOpType
    ACT = mybir.ActivationFunctionType
    MUL, ADD, SUB = ALU.mult, ALU.add, ALU.subtract
    AX = mybir.AxisListType.X

    with ExitStack() as ctx:
        def sb(name, shape, dt=f32):
            return ctx.enter_context(nc.sbuf_tensor(name, shape, dt))

        def sem(name):
            return ctx.enter_context(nc.semaphore(name))

        X = sb("X", [128, 8, T])
        XH = sb("XH", [128, 8, T], f32r)
        XL = sb("XL", [128, 8, T], f32r)
        HH = sb("HH", [128, 8, T], f32r)
        HL = sb("HL", [128, 8, T], f32r)
        RAW = sb("RAW", [128, NRAW, 1024])
        WH = sb("WH", [128, NSPLIT, 1024], f32r)
        WL = sb("WL", [128, NSPLIT, 1024], f32r)
        PT = sb("PT", [128, 2, 4, T])
        BI = sb("BI", [128, 4, ML])
        PRM = sb("PRM", [128, NPRM])
        CST = sb("CST", [128, NCST])
        TT = sb("TT", [128, NTILE, T])
        PD = sb("PD", [128, NPAD, 544])
        SM = sb("SM", [128, 160])
        GW = sb("GW", [128, 512])
        W2 = sb("W2", [128, 192])
        KC = sb("KC", [128, 32])
        VC = sb("VC", [32, 64])
        G8 = sb("G8", [128, 8])
        GT = sb("GT", [128, 4, 12])
        PSB = [ctx.enter_context(nc.psum_tensor(f"PS{i}", [128, T], f32)) for i in range(8)]

        V = Engine(sem("s_v"), True)
        A = Engine(sem("s_a"), True)
        P = Engine(sem("s_p"), True)
        PE = Engine(sem("s_pe"), False)
        SP = Engine(sem("s_sp"), False)
        s_raw = [sem(f"s_raw{i}") for i in range(NRAW)]
        s_x = [sem(f"s_x{k}") for k in range(8)]
        s_c2, s_c3, s_c4, s_gw = sem("s_c2"), sem("s_c3"), sem("s_c4"), sem("s_gw")
        s_c = sem("s_c")
        s_w1 = sem("s_w1")
        s_w2 = sem("s_w2")
        s_bi = [sem(f"s_bi{i}") for i in range(4)]
        s_out = sem("s_out")

        def v_tt(o, a, b, op, *w, own=True):
            return V.put(lambda e: e.tensor_tensor(o, a, b, op), w, own=own)

        def v_ts(o, a, s1, s2, op0, op1, *w, own=True):
            if op1 is None:
                return V.put(lambda e: e.tensor_scalar(o, a, s1, None, op0), w, own=own)
            return V.put(lambda e: e.tensor_scalar(o, a, s1, s2, op0, op1), w, own=own)

        def v_stt(o, a, s, b, op0, op1, *w, own=True):
            return V.put(lambda e: e.scalar_tensor_tensor(o, a, s, b, op0, op1), w, own=own)

        def v_add_max(o, a, b, mx, *w):
            return V.put(lambda e: e.tensor_tensor_reduce(
                out=o, in0=a, in1=b, scale=1.0, scalar=-3.0e38, op0=ADD, op1=ALU.max, accum_out=mx), w,
                own=False)

        def v_copy(o, a, *w, own=True):
            return V.put(lambda e: e.tensor_copy(o, a), w, own=own)

        def v_rec(o, a, *w):
            return V.put(lambda e: e.reciprocal(o, a), w)

        def v_set(o, value, *w):
            return V.put(lambda e: e.memset(o, value), w)

        table = [None]
        LNEXP = "natural_log_exp_and_others"

        def to_lnexp():
            if table[0] != LNEXP:
                A.put(lambda e: e.preload_act_table_set(LNEXP), (), False)
                table[0] = LNEXP

        def a_act(o, a, f, *w, scale=1.0, bias=0.0, acc=None, own=True):
            if f in (ACT.Ln, ACT.Exp):
                to_lnexp()
            elif f not in (ACT.Copy, ACT.Square):
                table[0] = f
            if acc is not None:
                return A.put(lambda e: e.activation(o, a, f, scale=scale, bias=bias, accum_out=acc), w,
                             own=own)
            return A.put(lambda e: e.activation(o, a, f, scale=scale, bias=bias), w, own=own)

        def a_copy(o, a, *w, own=True):
            return A.put(lambda e: e.activation(o, a, ACT.Copy), w, own=own)

        def p_tt(o, a, b, op, *w, own=True):
            return P.put(lambda e: e.tensor_tensor(o, a, b, op), w, own=own)

        def mm(o, l, r, start, stop, *w, inc=False):
            return PE.put(lambda e: e.matmul(o, l, r, start=start, stop=stop), w, inc)

        def tr(o, a, *w, inc=False):
            return PE.put(lambda e: e.transpose(o, a, ident), (C3TOK, *w), inc)

        def load(o, a, s, *w):
            SP.put(lambda e: e.dma_start(o, a).then_inc(s, 16), w, False)

        def pcol(name, i=0):
            return PRM[:, POFF[name] + i:POFF[name] + i + 1]

        def cc(name, n):
            return CST[:, COFF[name]:COFF[name] + n]

        ident, ones, bones = cc("ident", 128), cc("ones", 128), cc("bones", 128)
        tiles = Ring([TT[:, i, :] for i in range(NTILE)])
        pads = Ring([PD[:, i, :] for i in range(NPAD)])
        banks = Ring([p[:, :] for p in PSB])
        small_at = [0]

        def small(n=1):
            if small_at[0] + n > 128:
                small_at[0] = 0
            a = small_at[0]
            small_at[0] += n
            return SM[:, a:a + n]

        eps = SM[:, 159:160]

        def load_once(o, a, s, *w):
            load(o, a, s, *w)
            return (s, 16)

        CTOK = (s_c, 16)
        C3TOK = (s_c3, 16)
        C4TOK = (s_c4, 16)
        bi_n = [0, 0, 0, 0]

        def load_bi(slot, src, *w):
            load(BI[:, slot, 0:src.shape[-1]], src, s_bi[slot], *w)
            bi_n[slot] += 16
            return (s_bi[slot], bi_n[slot])

        lo_done, used = [], []
        at = {"tile": 0, "loaded": 0}

        def load_block():
            b = at["loaded"]
            if b < N_BLOCKS:
                load(RAW[:, b % NRAW, :], wst[b, :, :], s_raw[b % NRAW],
                     lo_done[b - NRAW] if b >= NRAW else None)
                at["loaded"] += 1

        def split_block():
            b = len(lo_done)
            raw, wh, wl = RAW[:, b % NRAW, :], WH[:, b % NSPLIT, :], WL[:, b % NSPLIT, :]
            arrived = (s_raw[b % NRAW], 16 * (b // NRAW + 1))
            hi = a_copy(wh, raw, arrived, used[b - NSPLIT] if b >= NSPLIT else None, own=False)
            lo_done.append(p_tt(wl, raw, wh.bitcast(f32), SUB, hi, own=False))
            load_block()

        def take_tile():
            b, i = divmod(at["tile"], 8)
            if i == 0:
                while len(lo_done) < min(b + (NSPLIT if b else 2), N_BLOCKS):
                    split_block()
            at["tile"] += 1
            s = b % NSPLIT
            last = i == 7 or at["tile"] == N_TILES
            return (WH[:, s, 128 * i:128 * i + 128], WL[:, s, 128 * i:128 * i + 128], lo_done[b], last)

        load(PRM[:, 0:POFF["norm1"]], prm[:, 0:POFF["norm1"]], s_c)
        load(X[:, 0, :], xin[0, :, :], s_x[0])
        load_block()
        for k in range(1, 8):
            load(X[:, k, :], xin[k, :, :], s_x[k])
        load(CST[:, 0:384], cst[:, 0:384], s_c3)
        load_block()
        load_block()
        w1t = load_once(PT[:, :, :, :].rearrange("p a b n -> p (a b n)"), cmpw1, s_w1)
        w2t = load_once(W2[:, :], cmpw2, s_w2)
        load(CST[:, 384:NCST], cst[:, 384:NCST], s_c4)
        for _ in range(NRAW - 3):
            load_block()
        rel_in = [load_bi(h, relm[h, :, :]) for h in range(4)]
        gw_tok = load_once(GW[:, :], gatew, s_gw)
        load(PRM[:, POFF["norm1"]:NPRM], prm[:, POFF["norm1"]:NPRM], s_c2)
        C2TOK = (s_c2, 16)

        bg, soon = deque(), deque()

        def later(fn, delay=3, first=False):
            (soon if first else bg).append((at["tile"] + delay, fn))

        def next_step():
            (soon or bg).popleft()[1]()

        def flush():
            while bg or soon:
                next_step()

        def flush_ready():
            for queue in (soon, bg):
                if queue and queue[0][0] <= at["tile"]:
                    queue.popleft()[1]()
                    return

        def first_wide(mv, evac, mid, late):
            kc = len(mv)
            group = [banks.get() for _ in range(WIDE)]
            for k in range(kc):
                if k == late:
                    flush()
                for bank in group:
                    wh, wl, wtok, last = take_tile()
                    h, l, tok = mv[k]
                    mm(bank.ap, wh, h, k == 0, False, *bank.w, wtok, tok)
                    mm(bank.ap, wh, l, False, False)
                    t = mm(bank.ap, wl, h, False, k == kc - 1, inc=last or k == kc - 1)
                    if last:
                        used.append(t)
                    if k == kc - 1:
                        group_done.append(t)
                    flush_ready()
            if mid is not None:
                mid()
            flush()
            for m in range(WIDE):
                evac(m, group[m], group_done[m])
            group_done.clear()

        group_done = []

        def linear(mv, mc, evac, mid=None, pace=0, wide=False, late=0):
            kc = len(mv)
            if wide:
                first_wide(mv, evac, mid, late)
            for m in range(WIDE if wide else 0, mc):
                bank = banks.get()
                for k in range(kc):
                    wh, wl, wtok, last = take_tile()
                    h, l, tok = mv[k]
                    w = (*bank.w, wtok, tok) if k == 0 else (wtok, tok)
                    mm(bank.ap, wh, h, k == 0, False, *w)
                    mm(bank.ap, wh, l, False, False)
                    t = mm(bank.ap, wl, h, False, k == kc - 1, inc=last or k == kc - 1)
                    if last:
                        used.append(t)
                    if pace and k % pace == pace - 1:
                        flush_ready()
                if m == 0 and mid is not None:
                    mid()
                if not pace:
                    flush()
                while (bg or soon) and len(tiles.free) < ROOM:
                    next_step()
                evac(m, bank, t)

        def split_to(k, src, tok, buf=None):
            hi = a_copy(HH[:, k, :], src, tok, own=False)
            lo = p_tt(HL[:, k, :], src, HH[:, k, :].bitcast(f32), SUB, hi, own=False)
            if buf is not None:
                buf.done(lo)
            return (HH[:, k, :], HL[:, k, :], lo)

        def new_norm(name, first=0):
            return {"gain": lambda k: pcol(name, first + k), "mv": []}

        def norm_chunk(n, k, *x_done, first=False):
            g = n["gain"](k)
            x = X[:, k, :]
            if first:
                hi = a_act(XH[:, k, :], x, ACT.Copy, CTOK, *x_done, scale=g, own=False)
            else:
                hi = v_ts(XH[:, k, :], x, g, None, MUL, None, *x_done, own=False)
            lo = v_stt(XL[:, k, :], x, g, XH[:, k, :].bitcast(f32), MUL, SUB, hi, own=False)
            n["mv"].append((XH[:, k, :], XL[:, k, :], lo))
            if k == 0:
                n["sq"] = tiles.get()
                n["sq_done"] = a_act(n["sq"].ap, x, ACT.Square, *n["sq"].w, *x_done)
            else:
                s = tiles.get()
                squared = a_act(s.ap, x, ACT.Square, *s.w, *x_done, own=False)
                add = p_tt if first and k % 2 else v_tt
                n["sq_done"] = add(n["sq"].ap, n["sq"].ap, s.ap, ADD, squared, n["sq_done"], own=False)
                s.done(n["sq_done"])

        def norm_stats(n):
            n["rs"] = tiles.get()
            n["rs_done"] = rsqrt_of(n["rs"], n["sq"], n["sq_done"], ones, D)

        def norm_end(n):
            n["rs"].done((V.sem, V.count))

        def rsqrt_of(rs, acc, tok, mat, n):
            bank = banks.get()
            t = mm(bank.ap, mat, acc.ap, True, True, tok, C3TOK, *bank.w, inc=True)
            acc.done(t)
            t = a_act(rs.ap, bank.ap, ACT.Ln, t, *rs.w, eps_tok, scale=1.0 / n, bias=eps, own=False)
            bank.done(t)
            return a_act(rs.ap, rs.ap, ACT.Exp, scale=-0.5)

        def add_x(bank, m, tok):
            t = v_tt(X[:, m, :], bank.ap, X[:, m, :], ADD, tok, own=False)
            bank.done(t)
            return t

        def scaled(dst, bank, norm, tok, *w):
            t = v_tt(dst, bank.ap, norm["rs"].ap, MUL, tok, norm["rs_done"], *w, own=False)
            bank.done(t)
            return t

        def head_norm(buf, tok, gain):
            got = []
            s = tiles.get()
            t = a_act(s.ap, buf.ap, ACT.Square, tok, *s.w, own=False)

            def step():
                r = tiles.get()
                q = rsqrt_of(r, s, t, bones, 64)
                got.append(v_stt(buf.ap, buf.ap, gain, r.ap, MUL, MUL, q, tok))
                r.done(got[0])
            later(step, first=True)
            return got

        def to_tokens(src, tok, dst, *w, done=None):
            got = []

            def step():
                bank = banks.get()
                for b in range(4):
                    t = tr(bank.ap[:, 128 * b:128 * b + 128], src[:, 128 * b:128 * b + 128],
                           tok, *bank.w, inc=b == 3)
                t2 = a_copy(dst, bank.ap, t, *w, own=False)
                bank.done(t2)
                got.append(t2)
                if done is not None:
                    done(t)
            later(step, first=True)
            return got

        pt_free = [(), ()]
        pt_at = [0]

        def head(q, k, v, qk_done, v_done, bias, bias_done, causal, out, start, stop, gate=None,
                 extra=None, after=None, bias2d=False):
            return dict(q=q, k=k, v=v, qk_done=qk_done, v_done=v_done, bias=bias, bias_done=bias_done,
                        causal=causal, out=out, start=start, stop=stop, gate=gate, extra=extra,
                        after=after, bias2d=bias2d)

        def scores(hd, u):
            W = 128 * (u + 1) if hd["causal"] else T
            bank = banks.get()
            s = tiles.get()
            ex = hd["extra"]
            t = mm(bank.ap[:, 0:W], hd["q"][:, 128 * u:128 * u + 128], hd["k"][:, 0:W], True, ex is None,
                   *(x[0] for x in hd["qk_done"]), *bank.w, inc=ex is None)
            if ex is not None:
                t = mm(bank.ap[:, 0:W], ex[0], ex[1][:, 0:W], False, True, ex[2], inc=True)
            mx, nm, sm, rc = small(), small(), small(), small()
            b = hd["bias"](u)
            sap, bap = s.ap[:, 0:W], bank.ap[:, 0:W]
            if hd["bias2d"]:
                sap = sap.rearrange("p (a b) -> p a b", b=64)
                bap = bap.rearrange("p (a b) -> p a b", b=64)
            t = v_add_max(sap, bap, b, mx, t, hd["bias_done"](), *s.w)
            bank.done(t)
            t = v_ts(nm, mx, -1.0, None, MUL, None)
            t = a_act(s.ap[:, 0:W], s.ap[:, 0:W], ACT.Exp, t, bias=nm, acc=sm, own=False)
            return (W, s, sm, rc, t)

        def normalise(hd, u, W, s, sm, rc, exp_done):
            V.put(lambda e: e.reciprocal(rc, sm), (exp_done,), own=False)
            if hd["gate"] is None:
                t = v_ts(s.ap[:, 0:W], s.ap[:, 0:W], rc, None, MUL, None)
            else:
                t = v_ts(s.ap[:, 0:W], s.ap[:, 0:W], rc, hd["gate"](u), MUL, MUL, st["gt"])
            return (W, s, t)

        def turn(u, W, s, p_done, pt, pt_ok):
            n = W // 128
            bank = banks.get()
            for j in range(n):
                t = tr(bank.ap[:, 128 * j:128 * j + 128], s.ap[:, 128 * j:128 * j + 128], p_done,
                       *bank.w, inc=j == n - 1)
            s.done(t)
            t = a_copy(PT[:, pt, 0:n, 128 * u:128 * u + 128],
                       bank.ap[:, 0:W].rearrange("p (a b) -> p a b", b=128), t, *pt_ok, own=False)
            bank.done(t)
            return t

        def values(hd, pt, pt_done):
            out, out_ok = hd["out"]()
            for j in range(4):
                a = 128 * j if hd["causal"] else 0
                t = mm(out[:, a:T], hd["v"](j), PT[:, pt, j, a:T], hd["start"] and j == 0,
                       hd["stop"] and j == 3, pt_done, *(x[0] for x in hd["v_done"]), *out_ok, inc=j == 3)
            return t

        def attend(heads, beside={}, every=2):
            units = [(n, u) for n in range(len(heads)) for u in range(4)]
            flight, turned, pend = {}, {}, []

            def value_step(n, pt, t):
                def f():
                    done = values(heads[n], pt, t)
                    pt_free[pt] = (done,)
                    if heads[n]["after"] is not None:
                        heads[n]["after"](done)
                return f

            def step(i):
                def f():
                    if i in beside:
                        beside[i]()
                    ready = list(pend)
                    pend.clear()
                    if i < len(units):
                        n, u = units[i]
                        flight[i] = scores(heads[n], u)
                    if 0 <= i - 1 < len(units):
                        n, u = units[i - 1]
                        flight[i - 1] = normalise(heads[n], u, *flight[i - 1])
                    if 0 <= i - 2 < len(units):
                        n, u = units[i - 2]
                        if u == 0:
                            turned[n] = (pt_at[0] % 2, pt_free[pt_at[0] % 2])
                            pt_at[0] += 1
                        pt, pt_ok = turned[n]
                        t = turn(u, *flight.pop(i - 2), pt, pt_ok)
                        if u == 3:
                            pend.append(value_step(n, pt, t))
                    for fn in ready:
                        fn()
                return f
            for i in range(len(units) + 3):
                later(step(i), 4 + every * i)

        v_set(eps, EPS)
        eps_tok = (V.sem, V.count)
        pads_tok = eps_tok
        norm = new_norm("norm_mix")
        for k in range(8):
            norm_chunk(norm, k, (s_x[k], 16), CTOK, first=True)
            if k == 0:
                split_block()
        lam = PRM[:, POFF["lru_lambda"]:POFF["lru_lambda"] + 2]
        c_ab, c_e, c_u, c_l, c_w, c_L, c_NL = (SM[:, 128 + 2 * i:130 + 2 * i] for i in range(7))

        def log1p_of(o, e_, sign, u, l, w_, tok):
            t = v_ts(u, e_, sign, 1.0, MUL, ADD, tok)
            t2 = a_act(l, u, ACT.Ln, t)
            v_ts(w_, u, 1.0, 1e-30, SUB, ADD)
            v_rec(w_, w_)
            v_ts(l, l, 1e-30, None, ADD, None, t2)
            v_tt(l, l, w_, MUL)
            v_tt(l, l, e_, MUL)
            return v_ts(o, l, sign, None, MUL, None)

        def decay_gains():
            v_stt(c_ab, lam, -1.0, lam, MUL, ALU.max, CTOK)
            t = (V.sem, V.count)
            t = a_act(c_e, c_ab, ACT.Exp, t, scale=-1.0)
            log1p_of(c_L, c_e, 1.0, c_u, c_l, c_w, t)
            v_ts(c_u, lam, -1.0, 0.0, MUL, ALU.max)
            v_tt(c_L, c_L, c_u, ADD)
            v_ts(c_NL, c_L, 8.0, None, MUL, None)
            st["lam"] = v_ts(c_L, c_L, -8.0, None, MUL, None)

        for i, src in enumerate((pcol("fox_qk"), pcol("nsa_qk"))):
            v_ts(G8[:, i:i + 1], src, 0.125, None, MUL, None)

        n_mix = norm
        mixed = [None] * 8
        st = {}

        def out_norm(g, bufs, toks):
            acc = tiles.get()
            s = tiles.get()
            a_act(acc.ap, bufs[0].ap, ACT.Square, toks[0], *acc.w)
            t = a_act(s.ap, bufs[1].ap, ACT.Square, toks[1], *s.w)
            t = v_tt(acc.ap, acc.ap, s.ap, ADD, t)
            s.done(t)

            def step():
                r = tiles.get()
                q = rsqrt_of(r, acc, t, ones, 256)
                for c in range(2):
                    t3 = v_stt(bufs[c].ap, bufs[c].ap, pcol("out_norm", 2 * g + c), r.ap, MUL, MUL,
                               q, toks[c])
                    mixed[OUT_ORDER.index(2 * g + c)] = split_to(2 * g + c, bufs[c].ap, t3, bufs[c])
                r.done(t3)
            later(step, 8 if g == 1 else 3, first=True)


        def conv_taps(o, src, name, c, nch, taps, width, bias, *w):
            last = taps - 1
            if bias is None:
                t = v_ts(o, src[:, last:last + T], pcol(name, last * nch + c), None, MUL, None, *w)
            else:
                t = v_ts(o, src[:, last:last + T], pcol(name, last * nch + c), bias, MUL, ADD, *w)
            for j in range(last - 1, -1, -1):
                t = v_stt(o, src[:, j:j + T], pcol(name, j * nch + c), o, MUL, ADD)
            return t

        def lru_in(c, bank, tok):
            pad = pads.get()
            t = v_set(pad.ap[:, 0:3], 0.0, *pad.w)
            t = scaled(pad.ap[:, 3:515], bank, n_mix, tok)
            xc = tiles.get()
            t = conv_taps(xc.ap, pad.ap, "lru_conv_w", c, 2, 4, T, pcol("lru_conv_b", c), *xc.w)
            pad.done(t)
            r, i = tiles.get(), tiles.get()

            st["lru", c] = (xc, r, i, t)
            if c == 1:
                later(lru_gates, first=True)

        def lru_gates():
            parts = []
            for c in range(2):
                xc, r, i, t = st["lru", c]
                b0, b1 = banks.get(), banks.get()
                t0 = mm(b0.ap, GW[:, 128 * c:128 * c + 128], xc.ap, True, True, t, gw_tok, *b0.w,
                        inc=True)
                t1 = mm(b1.ap, GW[:, 256 + 128 * c:384 + 128 * c], xc.ap, True, True, *b1.w, inc=True)
                th = tiles.get()
                t0 = a_act(r.ap, b0.ap, ACT.Sigmoid, t0, *r.w, bias=pcol("lru_b", c), own=False)
                b0.done(t0)
                t1 = a_act(i.ap, b1.ap, ACT.Sigmoid, t1, *i.w, bias=pcol("lru_b", 2 + c), own=False)
                b1.done(t1)
                t2 = a_act(th.ap, r.ap, ACT.Tanh, t0, st["lam"], *th.w, scale=c_NL[:, c:c + 1], own=False)
                parts.append((xc, r, i, th, t1, t2))
            for c, (xc, r, i, th, t1, t2) in enumerate(parts):
                v_tt(i.ap, i.ap, xc.ap, MUL, t1, own=False)
                v_ts(xc.ap, th.ap, 1.0, None, ADD, None, t2)
                t3 = v_ts(th.ap, th.ap, 1e-30, None, ALU.max, None, own=False)
                a_act(r.ap, r.ap, ACT.Exp, scale=c_L[:, c:c + 1], own=False)
                a_act(xc.ap, xc.ap, ACT.Ln, t3, own=False)
                tq = a_act(th.ap, th.ap, ACT.Ln, t3, scale=2.0, own=False)

                def step(c=c, xc=xc, r=r, i=i, th=th, tq=tq):
                    t4 = v_tt(th.ap, th.ap, xc.ap, SUB, tq)
                    t4 = a_act(th.ap, th.ap, ACT.Exp, t4, scale=0.5, own=False)
                    v_tt(i.ap, i.ap, th.ap, MUL, t4)
                    th.done((V.sem, V.count))
                    t5 = V.put(lambda e: e.tensor_tensor_scan(xc.ap, r.ap, i.ap, 0.0, MUL, ADD))
                    r.done(t5)
                    i.done(t5)
                    st["h", c] = (xc, t5)
                later(step, first=True)

        def lru_gate(c, bank, tok):
            g = tiles.get()
            st["g", c] = (g, scaled(g.ap, bank, n_mix, tok, *g.w))
            if c == 0:
                return

            def step():
                for c in range(2):
                    g, t = st["g", c]
                    st["g", c] = (g, a_act(g.ap, g.ap, ACT.Gelu_apprx_tanh, t, own=False))
            later(step, first=True)

            def last():
                for c in range(2):
                    h, th = st["h", c]
                    g, t = st["g", c]
                    t2 = v_tt(h.ap, h.ap, g.ap, MUL, t, th)
                    g.done(t2)
                    st["ya", c] = (h, t2)
                out_norm(0, [st["ya", 0][0], h], [st["ya", 0][1], t2])
            later(last, first=True)

        def sc_b(c, bank, tok):
            b = tiles.get()
            st["b", c] = (b, scaled(b.ap, bank, n_mix, tok, *b.w))

        def sc_c(c, bank, tok):
            b = tiles.get()
            st["c", c] = (b, scaled(b.ap, bank, n_mix, tok, *b.w))

        def sc_x(c, bank, tok):
            pad = pads.get()
            v_set(pad.ap[:, 0:2], 0.0, *pad.w)
            scaled(pad.ap[:, 2:514], bank, n_mix, tok)
            cb = st["c", c][0]
            t = v_tt(pad.ap[:, 2:514], pad.ap[:, 2:514], cb.ap, MUL)
            t = conv_taps(cb.ap, pad.ap, "sc_conv_w", c, 2, 3, T, None)
            pad.done(t)
            bb = st["b", c][0]
            t = v_tt(cb.ap, cb.ap, bb.ap, MUL)
            bb.done(t)
            st["yb", c] = (cb, t)
            if c == 1:
                out_norm(1, [st["yb", 0][0], cb], [st["yb", 0][1], t])

        def fg(c, bank, tok):
            f = tiles.get()
            t = scaled(f.ap, bank, n_mix, tok, *f.w)
            g = tiles.get()
            tg = a_act(g.ap, f.ap, ACT.Sigmoid, t, *g.w, bias=pcol("fg_bias"))

            def gates():
                bank = banks.get()
                for b in range(4):
                    t2 = tr(bank.ap[:, 128 * b:128 * b + 128], g.ap[:, 128 * b:128 * b + 128], tg,
                            *bank.w, inc=b == 3)
                g.done(t2)
                src = bank.ap.rearrange("p (a b) -> p a b", b=128)[:, :, 32:44]
                t3 = v_copy(GT[:, :, :], src, t2)
                bank.done(t3)
                st["gt"] = v_ts(GT[:, 0, 0:4], GT[:, 0, 0:4], cc("rowmask", 1), None, MUL, None, C4TOK)
            later(gates)
            y, e_, u, l, w_, wt = f, *(tiles.get() for _ in range(5))
            free = [x for bb in (e_, u, l, w_, wt) for x in bb.w]
            c4 = slice(0, 4)
            v_ts(y.ap[c4], y.ap[c4], PRM[0:4, POFF["fg_bias"]:POFF["fg_bias"] + 1], None, ADD, None, tg,
                 *free)
            v_ts(w_.ap[c4], y.ap[c4], 0.0, None, ALU.min, None)
            t = v_stt(u.ap[c4], y.ap[c4], -1.0, y.ap[c4], MUL, ALU.max)
            te = a_act(e_.ap[c4], u.ap[c4], ACT.Exp, t, scale=-1.0)

            def ratio():
                t = v_ts(u.ap[c4], e_.ap[c4], 1.0, 1.0, MUL, ADD, te)
                st["log"] = a_act(l.ap[c4], u.ap[c4], ACT.Ln, t)
                v_ts(wt.ap[c4], u.ap[c4], 1.0, 1e-30, SUB, ADD)
                v_rec(wt.ap[c4], wt.ap[c4])

            def total():
                v_ts(l.ap[c4], l.ap[c4], 1e-30, None, ADD, None, st["log"])
                v_tt(l.ap[c4], l.ap[c4], wt.ap[c4], MUL)
                v_tt(u.ap[c4], l.ap[c4], e_.ap[c4], MUL)
                v_tt(w_.ap[c4], u.ap[c4], w_.ap[c4], SUB)
                v_set(u.ap[c4], 1.0)
                cbuf = tiles.get()
                t = V.put(lambda e: e.tensor_tensor_scan(cbuf.ap[c4], u.ap[c4], w_.ap[c4], 0.0, MUL, ADD),
                          cbuf.w)
                for b in (y, e_, u, l, w_, wt):
                    b.done(t, (A.sem, A.count))
                st["cum"] = (cbuf, t)
            later(ratio, 6, first=True)
            later(total, 13, first=True)

        mask = cc("mask", ML)

        def master(view):
            return lambda u: view[:, 384 - 128 * u:512]

        def half(ap, p):
            return ap[64 * p:64 * p + 64, :]

        def finish_pair(obank, t, g, c, key):
            y = tiles.get()
            t2 = v_copy(y.ap, obank.ap, t, *y.w)
            obank.done(t2)
            st[key, c] = (y, t2)
            if c == 1:
                out_norm(g, [st[key, 0][0], y], [st[key, 0][1], t2])

        def fox(j, bank, tok):
            c, kind = divmod(j, 3)
            b = tiles.get()
            t = scaled(b.ap, bank, n_mix, tok, *b.w)
            if kind < 2:
                got = head_norm(b, t, G8[:, 0:1] if kind == 0 else pcol("fox_qk", 1))
                st["fox", kind] = (b, got)
                return
            vt = tiles.get()
            got = to_tokens(b.ap, t, vt.ap, *vt.w, done=lambda x: b.done(x))
            q, qt = st["fox", 0]
            k, kt = st["fox", 1]
            ob = []
            cum, ctok = st["cum"]
            heads = []
            for p in range(2):
                h = 2 * c + p
                sel = ident[0:4, h:h + 1].to_broadcast([4, 128])

                def out(p=p):
                    if p == 0:
                        ob.append(banks.get())
                        return half(ob[0].ap, 0), ob[0].w
                    return half(ob[0].ap, 1), ()

                def after(t, p=p):
                    if p == 1:
                        for x in (q, k, vt):
                            x.done(t)
                        if c == 1:
                            cum.done(t)
                        finish_pair(ob[0], t, 2, c, "yc")
                heads.append(head(
                    half(q.ap, p), half(k.ap, p),
                    lambda jj, p=p: vt.ap[:, 128 * jj + 64 * p:128 * jj + 64 * p + 64], (qt, kt), (got,),
                    master(mask), lambda: C4TOK, True, out, True, True, extra=(sel, cum.ap[0:4], ctok),
                    after=after))
            attend(heads)

        W1 = PT[:, :, :, :].rearrange("p a b n -> p (a b n)")

        def nsa_kv(j, bank, tok):
            b = tiles.get()
            t = scaled(b.ap, bank, n_mix, tok, *b.w)
            if j == 0:
                blk = [tiles.get() for _ in range(4)]
                pos = PRM[:, POFF["cmp_pos"]:POFF["cmp_pos"] + 32]
                for i in range(4):
                    v_set(blk[i].ap, 0.0, *blk[i].w)
                for i in range(4):
                    l0 = 8 * i
                    for br in range(2):
                        r = slice(64 * br, 64 * br + 64)
                        o = blk[i].ap[r].rearrange("p (l n) -> p l n", n=64)[:, :, 32 * br:32 * br + 31]
                        src = b.ap[r, 16 * (l0 // 16):16 * (l0 // 16) + 496]
                        src = src.rearrange("p (n l) -> p l n", l=16)[:, l0 % 16:l0 % 16 + 8, :]
                        pp = pos[r, l0:l0 + 8].unsqueeze(2).to_broadcast([64, 8, 31])
                        tb = v_tt(o, src, pp, ADD)
                b.done(tb)

                def product(l0):
                    def f():
                        if l0 == 0:
                            st["cb"] = banks.get()
                        bk = st["cb"]
                        for l in range(l0, l0 + 8):
                            th = mm(bk.ap[0:64, 0:128], blk[l // 8].ap[:, 64 * (l % 8):64 * (l % 8) + 64],
                                    W1[:, 128 * l:128 * l + 128], l == 0, l == 31, w1t, tb, *bk.w,
                                    inc=l == 31)
                        if l0 < 24:
                            return
                        hid = tiles.get()
                        t = a_act(hid.ap[0:64, 0:128], bk.ap[0:64, 0:128], ACT.Gelu_apprx_tanh, th, *hid.w)
                        bk.done(t)
                        st["hid"] = (hid, t)
                        for x in blk:
                            x.done(th)
                        pt_free[0] = pt_free[1] = (th,)
                    return f

                def step():
                    bk = banks.get()
                    hid, t = st["hid"]
                    t = PE.put(lambda e, bk=bk: e.transpose(bk.ap[:, 0:64], hid.ap[0:64, 0:128],
                                                            ident[0:64, 0:64]), (t, C3TOK, *bk.w), True)
                    hid.done(t)
                    ht = tiles.get()
                    t = v_copy(ht.ap[:, 0:64], bk.ap[:, 0:64], t, *ht.w)
                    bk.done(t)
                    bk = banks.get()
                    tk = mm(bk.ap[:, 0:31], W2[:, 0:128], ht.ap[:, 0:31], True, True, w2t, t, *bk.w, inc=True)
                    tk = v_copy(KC[:, 0:31], bk.ap[:, 0:31], tk)
                    bk.done(tk)
                    bv = banks.get()
                    tv = mm(bv.ap[0:31, 0:64], ht.ap[:, 32:63], W2[:, 128:192], True, True, *bv.w, inc=True)
                    ht.done(tv)
                    st["vc"] = v_copy(VC[0:31, 0:64], bv.ap[0:31, 0:64], tv)
                    bv.done(st["vc"])
                    sq = tiles.get()
                    r = tiles.get()
                    t = a_act(sq.ap[:, 0:31], KC[:, 0:31], ACT.Square, tk, *sq.w)

                    def fin():
                        bk = banks.get()
                        t2 = mm(bk.ap[:, 0:31], bones, sq.ap[:, 0:31], True, True, t, *bk.w, inc=True)
                        sq.done(t2)
                        t2 = a_act(r.ap[:, 0:31], bk.ap[:, 0:31], ACT.Ln, t2, *r.w, scale=1.0 / 64, bias=eps)
                        bk.done(t2)
                        t2 = a_act(r.ap[:, 0:31], r.ap[:, 0:31], ACT.Exp, scale=-0.5)
                        st["kc"] = v_stt(KC[:, 0:31], KC[:, 0:31], pcol("nsa_qk", 1), r.ap[:, 0:31], MUL, MUL,
                                         t2)
                        r.done(st["kc"])
                    bg.appendleft((at["tile"] + 3, fin))
                for l0 in range(0, 32, 8):
                    later(product(l0), 8)
                later(step)
            elif j < 3:
                st["nk", j] = (b, head_norm(b, t, pcol("nsa_qk", 1 + j)))
            else:
                vt = tiles.get()
                st["nv"] = (vt, to_tokens(b.ap, t, vt.ap, *vt.w, done=lambda x: b.done(x)))

        def nsa_q(c, bank, tok):
            b = tiles.get()
            t = scaled(b.ap, bank, n_mix, tok, *b.w)
            qt = head_norm(b, t, G8[:, 1:2])
            vt, vtok = st["nv"]
            ob = []
            heads = []

            cmp = {}

            def cmp_scores():
                sc = tiles.get()
                pair = [banks.get(), banks.get()]
                made = []
                for p in range(2):
                    bk = pair[p]
                    for i in range(4):
                        t = mm(bk.ap[:, 32 * i:32 * i + 31], half(b.ap, p)[:, 128 * i:128 * i + 128],
                               half(KC, p)[:, 0:31], True, True, qt[0], st["kc"], *bk.w, inc=True)
                    made.append(t)
                w = sc.ap[:, 0:256].rearrange("p (a n) -> p a n", n=32)[:, :, 0:31]
                for p in range(2):
                    ps = pair[p].ap[:, 0:128].rearrange("p (a n) -> p a n", n=32)[:, :, 0:31]
                    for i in range(4):
                        t2 = v_tt(w[:, 4 * p + i, :], ps[:, i, :],
                                  BI[:, 2 * c + p, 415 - 128 * i:415 - 128 * i + 481:16], ADD, made[p],
                                  st["rel"], *sc.w, own=False)
                    pair[p].done(t2)
                mx, sm, rc = small(8), small(8), small(8)
                V.put(lambda e: e.reduce_max(mx, w, AX))
                t = v_tt(w, w, mx.unsqueeze(2).to_broadcast([128, 8, 31]), SUB)
                cmp["a"] = (sc, w, sm, rc, a_act(w, w, ACT.Exp, t))

            def cmp_turn():
                sc, w, sm, rc, t = cmp["a"]
                V.put(lambda e: e.reduce_sum(sm, w, AX), (t,))
                v_rec(rc, sm)
                for p in range(2):
                    v_tt(rc[:, 4 * p:4 * p + 4], rc[:, 4 * p:4 * p + 4], GT[:, :, 2 * c + p], MUL, st["gt"])
                t = v_tt(w, w, rc.unsqueeze(2).to_broadcast([128, 8, 31]), MUL)
                cmp["b"] = []
                for p in range(2):
                    bk, pc = banks.get(), pads.get()
                    for i in range(4):
                        t2 = PE.put(lambda e, bk=bk, p=p, i=i: e.transpose(
                            bk.ap[0:31, 128 * i:128 * i + 128], w[:, 4 * p + i, :], ident),
                            (t, *bk.w), True)
                    t3 = a_copy(pc.ap[0:31, 0:T], bk.ap[0:31, :], t2, *pc.w, own=False)
                    bk.done(t3)
                    cmp["b"].append((pc, t3))
                sc.done(t2)

            def cmp_values():
                ob.append(banks.get())
                for p in range(2):
                    pc, t3 = cmp["b"][p]
                    t4 = mm(half(ob[0].ap, p), VC[0:31, 0:64], pc.ap[0:31, 0:T], True, False, t3, st["vc"],
                            *(ob[0].w if p == 0 else ()), inc=True)
                    pc.done(t4)

            for p in range(2):
                h = 2 * c + p
                for br in range(2):
                    kb, kt = st["nk", 1 + br]

                    def out(p=p):
                        return half(ob[0].ap, p), ()

                    def after(t, p=p, br=br):
                        if br == 1 and p == 1:
                            b.done(t)
                            if c == 1:
                                vt.done(t)
                                for i in (1, 2):
                                    st["nk", i][0].done(t)
                            finish_pair(ob[0], t, 3, c, "yd")
                    heads.append(head(
                        half(b.ap, p), half(kb.ap, p),
                        lambda jj, br=br: vt.ap[:, 128 * jj + 64 * br:128 * jj + 64 * br + 64], (qt, kt),
                        (vtok,), master(BI[:, h, :]), lambda: st["rel"], True, out, False, br == 1,
                        gate=lambda u, br=br, h=h: GT[:, u, 4 + 4 * br + h:5 + 4 * br + h], after=after))
            attend(heads, {0: cmp_scores, 4: cmp_turn, 6: cmp_values})

        MIX = ([(nsa_kv, j) for j in range(4)] + [(fg, 0)] + [(fox, j) for j in range(6)]
               + [(nsa_q, 0), (nsa_q, 1)] + [(lru_in, 0), (lru_in, 1), (lru_gate, 0), (lru_gate, 1)]
               + [(f, c) for c in range(2) for f in (sc_b, sc_c, sc_x)])

        def mix_evac(m, bank, tok):
            if m == 2:
                for h in range(4):
                    st["rel"] = p_tt(BI[:, h, :], BI[:, h, :], mask, ADD, rel_in[h], C4TOK)
            f, arg = MIX[m]
            f(arg, bank, tok)
            if m == 6:
                decay_gains()

        linear(norm["mv"], 23, mix_evac, mid=lambda: norm_stats(norm), pace=1)
        norm_end(norm)

        def residual(nxt):
            def evac(m, bank, tok):
                t = add_x(bank, m, tok)
                if nxt is not None:
                    norm_chunk(nxt, m, t)
            return evac

        def ffn(norm, nxt, layer, final=False):
            hid = {}
            cur = {}

            def plain(m, bank, tok, off, base):
                g, up = m % 2 == 0, m % 2 == 1
                b = tiles.get()
                t = scaled(b.ap, bank, norm, tok, *b.w)
                if g:
                    t = a_act(b.ap, b.ap, ACT.Silu, t)
                    cur["g"] = (b, t)
                else:
                    gb, gt = cur["g"]
                    t = v_tt(b.ap, b.ap, gb.ap, MUL, gt)
                    gb.done(t)
                    hid[m // 2] = split_to(m // 2, b.ap, t, b)

            def conv(m, bank, tok, off, base):
                ch = (off + m // 2) + (22 if m % 2 == 0 else 0)
                pad = pads.get()
                v_set(pad.ap[:, 0:1], 0.0, *pad.w)
                v_set(pad.ap[:, 513:514], 0.0)
                scaled(pad.ap[:, 1:513], bank, norm, tok)
                b = tiles.get()
                wn = 132 * layer
                t = v_ts(b.ap, pad.ap[:, 1:513], pcol("ffn_dw_w", wn + 44 + ch),
                         pcol("ffn_dw_b", 44 * layer + ch), MUL, ADD, *b.w)
                v_stt(b.ap, pad.ap[:, 0:512], pcol("ffn_dw_w", wn + ch), b.ap, MUL, ADD)
                t = v_stt(b.ap, pad.ap[:, 2:514], pcol("ffn_dw_w", wn + 88 + ch), b.ap, MUL, ADD)
                pad.done(t)
                if m % 2 == 0:
                    t = a_act(b.ap, b.ap, ACT.Gelu_apprx_tanh, t)
                    cur["g"] = (b, t)
                else:
                    gb, gt = cur["g"]
                    t = v_tt(b.ap, b.ap, gb.ap, MUL, gt)
                    gb.done(t)
                    hid[m // 2] = split_to(m // 2, b.ap, t, b)

            fn = plain if layer is None else conv
            for i, (a, b) in enumerate(FF_PARTS):
                hid.clear()
                linear(norm["mv"], 2 * (b - a), lambda m, bank, tok: fn(m, bank, tok, a, i),
                       mid=lambda: norm_stats(norm) if i == 0 else None)
                mv = [hid[k] for k in range(b - a)]
                if i < len(FF_PARTS) - 1:
                    linear(mv, 8, lambda m, bank, tok: add_x(bank, m, tok), wide=True)
                else:
                    norm_end(norm)
                    if final:
                        def last(m, bank, tok):
                            t = add_x(bank, m, tok)
                            load(out[m, :, :], X[:, m, :], s_out, t)
                        linear(mv, 8, last, wide=True)
                    else:
                        linear(mv, 8, residual(nxt), wide=True)

        v_ts(G8[:, 2:3], pcol("nat_q"), 0.125, None, MUL, None, C2TOK)
        n_ffn = new_norm("norm_ffn")
        linear(mixed, 8, residual(n_ffn), wide=True, late=6)
        norm = new_norm("norm1")
        ffn(n_ffn, norm, None)

        def conv_layer(norm, nxt, ci):
            cur = {}
            outs = []
            sums = []
            idle = (*pt_free[0], *pt_free[1], (V.sem, V.count), (P.sem, P.count))
            diag = Ring([PT[:, i, j, :] for i in range(2) for j in range(4)])
            flat = BI[:, :, :].rearrange("p a b -> p (a b)")
            stage = Ring([flat[:, T * i:T * i + T] for i in range(7)])
            for ring in (diag, stage):
                ring.free = deque((ap, idle) for ap, _ in ring.free)

            def tap(c, j):
                return pcol("conv_dw_w", 248 * ci + 31 * c + j)

            def evac(m, bank, tok):
                c = m // 2
                n_pe = TAPS_PE[c]
                if m % 2 == 0:
                    g = tiles.get()
                    t = scaled(g.ap, bank, norm, tok, *g.w)
                    cur["g"] = (g, a_act(g.ap, g.ap, ACT.Sigmoid, t, bias=pcol("conv_b_in", 16 * ci + 8 + c)))
                    dg = [diag.get() for _ in range((n_pe + 3) // 4)]
                    dgs = [dg[j // 4].ap[:, 128 * (j % 4):128 * (j % 4) + 128] for j in range(n_pe)]
                    for j in range(n_pe):
                        dg_done = a_act(dgs[j], ident, ACT.Copy, *dg[j // 4].w, scale=tap(c, j), own=False)
                    cur["dg"] = (dg, dgs, dg_done)
                    squares()
                    return
                pad = pads.get()
                v_set(pad.ap[:, 0:15], 0.0, *pad.w)
                v_set(pad.ap[:, 527:542], 0.0)
                scaled(pad.ap[:, 15:527], bank, norm, tok)
                g, gt = cur["g"]
                u_done = v_stt(pad.ap[:, 15:527], pad.ap[:, 15:527], pcol("conv_b_in", 16 * ci + c), g.ap,
                               ADD, MUL, gt)
                g.done(u_done)
                dg, dgs, dg_done = cur["dg"]
                po = stage.get()
                free = po.w
                for j in range(n_pe, n_pe + TAPS_POOL[c]):
                    s = stage.get()
                    t = a_act(s.ap, pad.ap[:, j:j + T], ACT.Copy, u_done, *s.w, *free, scale=tap(c, j),
                              own=False)
                    if j == n_pe:
                        first = s
                        continue
                    pool_done = p_tt(po.ap, first.ap if j == n_pe + 1 else po.ap, s.ap, ADD, t)
                    s.done(pool_done)
                    if j == n_pe + 1:
                        first.done(pool_done)
                o = tiles.get()
                j0 = n_pe + TAPS_POOL[c]
                v_ts(o.ap, pad.ap[:, j0:j0 + T], tap(c, j0), pcol("conv_dw_b", 8 * ci + c), MUL, ADD, *o.w)
                o2 = tiles.get()
                two = [(o, (V.sem, V.count))]
                two.append((o2, v_ts(o2.ap, pad.ap[:, j0 + 1:j0 + 1 + T], tap(c, j0 + 1), None, MUL, None,
                                     *o2.w, own=False)))
                for j in range(j0 + 2, 31):
                    x, before = two[0]
                    two = [two[1], (x, v_stt(x.ap, pad.ap[:, j:j + T], tap(c, j), x.ap, MUL, ADD, before,
                                             own=False))]
                v_done = v_tt(o.ap, o.ap, o2.ap, ADD)
                o2.done(v_done)

                def join():
                    if c == 7:
                        add_up(5)
                        add_up(6)
                    bk = banks.get()
                    for j in range(n_pe):
                        t = mm(bk.ap, dgs[j], pad.ap[:, j:j + T], j == 0, j == n_pe - 1, dg_done,
                               u_done, *bk.w, inc=j == n_pe - 1)
                    for x in dg:
                        x.done(t)
                    pad.done(t, v_done, pool_done)
                    v_tt(o.ap, o.ap, bk.ap, ADD, t)
                    bk.done((V.sem, V.count))
                    t = v_tt(o.ap, o.ap, po.ap, ADD, pool_done)
                    po.done(t)
                    outs.append((o, t))
                    if c == 1:
                        bk = banks.get()
                        t = mm(bk.ap, ones, outs[0][0].ap, True, True, outs[0][1], *bk.w, inc=True)
                        cur["shift"] = tiles.get()
                        cur["shift_done"] = a_act(cur["shift"].ap, bk.ap, ACT.Copy, t, *cur["shift"].w,
                                                  scale=1.0 / 128)
                        bk.done(cur["shift_done"])
                        less_shift(0)
                    if c >= 1:
                        less_shift(c)
                    if 2 <= c < 7:
                        add_up(c - 2)
                later(join)

            def less_shift(c):
                o, t = outs[c]
                sub = v_tt if c == 7 else p_tt
                t = sub(o.ap, o.ap, cur["shift"].ap, SUB, t, cur["shift_done"])
                outs[c] = (o, t)

            def squares():
                while len(sums) < len(outs) and cur.get("shift"):
                    s = tiles.get()
                    o, t = outs[len(sums)]
                    sums.append((s, a_act(s.ap, o.ap, ACT.Square, t, *s.w, own=False)))

            def add_up(k):
                if k == 0:
                    cur["d"], cur["dd"] = banks.get(), banks.get()
                s, t2 = sums[k]
                mm(cur["d"].ap, ones, outs[k][0].ap, k == 0, k == 7, outs[k][1], *cur["d"].w)
                t = mm(cur["dd"].ap, ones, s.ap, k == 0, k == 7, t2, *cur["dd"].w, inc=True)
                s.done(t)
                return t

            linear(norm["mv"], 16, evac, mid=lambda: norm_stats(norm))
            norm_end(norm)
            flush()
            squares()
            tm = add_up(7)
            to_lnexp()
            pt_free[0] = pt_free[1] = (tm,)
            cur["shift"].done((V.sem, V.count))
            mu, r = tiles.get(), tiles.get()
            m_done = v_ts(mu.ap, cur["d"].ap, 1.0 / D, None, MUL, None, tm, *mu.w)
            t = a_act(r.ap, mu.ap, ACT.Square, m_done, *r.w)
            t = v_stt(r.ap, cur["dd"].ap, 1.0 / D, r.ap, MUL, SUB, t)
            cur["dd"].done(t)
            cur["d"].done(t)
            t3 = v_ts(r.ap, r.ap, 0.0, None, ALU.max, None)
            t3 = a_act(r.ap, r.ap, ACT.Ln, t3, bias=eps)
            t3 = a_act(r.ap, r.ap, ACT.Exp, scale=-0.5)
            less = {k: p_tt(o.ap, o.ap, mu.ap, SUB, t, m_done)
                    for k, (o, t) in enumerate(outs) if k >= 5}
            less[0] = v_tt(outs[0][0].ap, outs[0][0].ap, mu.ap, SUB, outs[0][1])
            less[1] = v_tt(outs[1][0].ap, outs[1][0].ap, mu.ap, SUB, outs[1][1], own=False)
            mv = []
            for k, (o, t) in enumerate(outs):
                if k not in less:
                    less[k] = v_tt(o.ap, o.ap, mu.ap, SUB, t, own=False)
                t = v_tt(o.ap, o.ap, r.ap, MUL, t3, less[k], own=False)
                t = a_act(o.ap, o.ap, ACT.Silu, t, scale=pcol("conv_ln_g", 8 * ci + k),
                          bias=pcol("conv_ln_b", 8 * ci + k), own=False)
                outs[k] = (o, t)
                if k < 5:
                    mv.append(split_to(k, o.ap, t, o))
            for k in range(5, 8):
                o, t = outs[k]
                v_copy(HH[:, k, :], o.ap, t)
                t = v_tt(HL[:, k, :], o.ap, HH[:, k, :].bitcast(f32), SUB)
                o.done(t)
                mv.append((HH[:, k, :], HL[:, k, :], t))
            r.done((V.sem, V.count))
            mu.done((V.sem, V.count), (P.sem, P.count))
            linear(mv, 8, residual(nxt), wide=True)

        def nat_layer(norm, nxt):
            mv = [None] * 8
            cur = {}
            used = [((V.sem, V.count), (P.sem, P.count))] * 4
            colmask = cc("colmask", 64).unsqueeze(1).to_broadcast([128, 14, 64])

            def evac(m, bank, tok):
                c, kind = divmod(m, 3)
                b = tiles.get()
                t = scaled(b.ap, bank, norm, tok, *b.w)
                if kind < 2:
                    cur[kind] = (b, head_norm(b, t, G8[:, 2:3] if kind == 0 else pcol("nat_k")))
                    return
                vt = tiles.get()
                got = to_tokens(b.ap, t, vt.ap, *vt.w, done=lambda x: b.done(x))
                q, qt = cur[0]
                k, kt = cur[1]
                ob = []
                heads = []
                for p in range(2):
                    h = 2 * c + p
                    slot = h % 4
                    a = load_bi(slot, natb[h, :, :], *used[slot])
                    view = BI[:, slot, :].rearrange("p (a b) -> p a b", b=64)
                    bt = p_tt(view, view, colmask, ADD, a)

                    def out(p=p):
                        if p == 0:
                            ob.append(banks.get())
                            return half(ob[0].ap, 0), ob[0].w
                        return half(ob[0].ap, 1), ()

                    def after(t, p=p, slot=slot):
                        used[slot] = ((V.sem, V.count),)
                        if p == 1:
                            for x in (q, k, vt):
                                x.done(t)
                            y = tiles.get()
                            t2 = v_copy(y.ap, ob[0].ap, t, *y.w)
                            ob[0].done(t2)
                            mv[c] = split_to(c, y.ap, t2, y)
                    heads.append(head(
                        half(q.ap, p), half(k.ap, p),
                        lambda jj, p=p: vt.ap[:, 128 * jj + 64 * p:128 * jj + 64 * p + 64], (qt, kt), (got,),
                        lambda u, view=view: view[:, 6 - 2 * u:14 - 2 * u, :], lambda bt=bt: bt, False, out,
                        True, True, after=after, bias2d=True))
                attend(heads)

            linear(norm["mv"], 24, evac, mid=lambda: norm_stats(norm), pace=1)
            norm_end(norm)
            ret_gains()
            linear(mv, 8, residual(nxt), wide=True, late=7)

        LG = SM[:, 142:150]
        NL = SM[:, 150:158]

        def ret_gains():
            dec = PRM[:, POFF["ret_dec"]:POFF["ret_dec"] + 8]
            e_, u, l, w_, lg, nl = (small(8) for _ in range(6))
            t = a_act(e_, dec, ACT.Exp, (V.sem, V.count), scale=-math.log(2.0))
            log1p_of(lg, e_, -1.0, u, l, w_, t)
            v_ts(nl, lg, -1.0, None, MUL, None)
            v_copy(LG, lg)
            st["lg"] = v_copy(NL, nl)

        def ret_layer(norm, nxt):
            free = ((V.sem, V.count), (P.sem, P.count))
            rt = [load_bi(1, rope[0, :, :], *free), load_bi(2, rope[1, :, :], *free)]
            dt_ = load_bi(3, dist, *free)
            cosv, sinv, dv = BI[:, 1, 0:T], BI[:, 2, 0:T], BI[:, 3, :]
            dm = BI[:, 0, :]
            mvs = [None] * 8
            dfree = [()]

            def head(h):
                qk, vts, gs = {}, [], []

                def decay():
                    v_ts(dm, dv, NL[:, 4 + h:5 + h], None, MUL, None, dt_, st["lg"], *dfree[0])
                    t = v_stt(dm, dv, LG[:, h:h + 1], dm, MUL, ALU.min)
                    st["dm"] = a_act(dm, dm, ACT.Exp, t)
                later(decay, 24)

                def evac(m, bank, tok):
                    b = tiles.get()
                    t = scaled(b.ap, bank, norm, tok, *b.w)
                    if m < 4:
                        kind, part = divmod(m, 2)
                        qk[m] = (b, t)
                        if part == 1:
                            x1, x2 = qk[2 * kind][0], b
                            a, c = tiles.get(), tiles.get()
                            v_tt(a.ap, x2.ap, sinv, MUL, rt[1], *a.w)
                            v_tt(c.ap, x1.ap, sinv, MUL, *c.w)
                            v_tt(x1.ap, x1.ap, cosv, MUL, rt[0])
                            t1 = v_tt(x1.ap, x1.ap, a.ap, SUB)
                            v_tt(x2.ap, x2.ap, cosv, MUL)
                            t2 = v_tt(x2.ap, x2.ap, c.ap, ADD)
                            a.done(t2)
                            c.done(t2)
                            if kind == 1:
                                t1 = v_ts(x1.ap, x1.ap, 0.0625, None, MUL, None)
                                t2 = v_ts(x2.ap, x2.ap, 0.0625, None, MUL, None)
                            qk[2 * kind] = (x1, t1)
                            qk[2 * kind + 1] = (x2, t2)
                    elif m < 8:
                        vt = tiles.get()
                        vts.append((vt, to_tokens(b.ap, t, vt.ap, *vt.w, done=lambda x: b.done(x))))
                    else:
                        gs.append((b, a_act(b.ap, b.ap, ACT.Silu, t)))

                linear(norm["mv"], 12, evac, mid=(lambda: norm_stats(norm)) if h == 0 else None, pace=1)
                flush()
                pt = h % 2
                for j in range(4):
                    bank = banks.get()
                    for d in range(2):
                        t = mm(bank.ap, qk[2 + d][0].ap[:, 128 * j:128 * j + 128], qk[d][0].ap, d == 0,
                               d == 1, qk[2 + d][1], qk[d][1], *bank.w, inc=d == 1)
                    t = v_tt(PT[:, pt, j, :], bank.ap, dm[:, 384 - 128 * j:896 - 128 * j], MUL, t, st["dm"],
                             *pt_free[pt])
                    bank.done(t)
                    pts = t
                dfree[0] = (pts,)
                for i in range(4):
                    qk[i][0].done((V.sem, V.count), (PE.sem, PE.count))
                os = []
                for c in range(4):
                    bank = banks.get()
                    for j in range(4):
                        t = mm(bank.ap, vts[c][0].ap[:, 128 * j:128 * j + 128], PT[:, pt, j, :], j == 0,
                               j == 3, pts, vts[c][1][0], *bank.w, inc=j == 3)
                    vts[c][0].done(t)
                    o = tiles.get()
                    t = a_copy(o.ap, bank.ap, t, *o.w)
                    bank.done(t)
                    os.append((o, t))
                    if c == 1:
                        tot = tiles.get()
                    if c > 0:
                        tot_done = v_tt(tot.ap, tot.ap if c > 1 else os[0][0].ap, o.ap, ADD, t, *tot.w)
                pt_free[pt] = ((PE.sem, PE.count),)
                hold = {}

                def mean():
                    bank = banks.get()
                    t = mm(bank.ap, ones, tot.ap, True, True, tot_done, *bank.w, inc=True)
                    tot.done(t)
                    mu = tiles.get()
                    tm = a_act(mu.ap, bank.ap, ACT.Copy, t, *mu.w, scale=1.0 / 512)
                    bank.done(tm)
                    hold["sq"] = []
                    for c in range(4):
                        o = os[c][0]
                        t = v_tt(o.ap, o.ap, mu.ap, SUB, tm)
                        s = tiles.get()
                        hold["sq"].append((s, a_act(s.ap, o.ap, ACT.Square, t, *s.w)))
                    mu.done(t)
                    s0 = hold["sq"][0][0]
                    for s, t in hold["sq"][1:]:
                        hold["sum"] = v_tt(s0.ap, s0.ap, s.ap, ADD, t)
                        s.done(hold["sum"])

                def variance():
                    bank = banks.get()
                    s0 = hold["sq"][0][0]
                    t3 = mm(bank.ap, ones, s0.ap, True, True, hold["sum"], *bank.w, inc=True)
                    s0.done(t3)
                    r = tiles.get()
                    t3 = a_act(r.ap, bank.ap, ACT.Ln, t3, *r.w, scale=1.0 / 512, bias=eps)
                    bank.done(t3)
                    t3 = a_act(r.ap, r.ap, ACT.Exp, scale=-0.5)
                    for c in range(4):
                        o = os[c][0]
                        v_stt(o.ap, o.ap, pcol("ret_gn", 4 * h + c), r.ap, MUL, MUL, t3)
                        g, gt = gs[c]
                        t = v_tt(o.ap, o.ap, g.ap, MUL, gt)
                        g.done(t)
                        mvs[4 * (h % 2) + c] = split_to(4 * (h % 2) + c, o.ap, t, o)
                    r.done(t)
                later(mean, 4)
                later(variance, 14 if h != 2 else 64 + 8)

            for h in range(4):
                head(h)
                if h == 2:
                    linear(list(mvs), 8, lambda m, bank, tok: add_x(bank, m, tok), pace=1)
            norm_end(norm)
            linear(mvs, 8, residual(nxt), wide=True, late=4)

        for layer in range(4):
            n2 = new_norm("norm2", 8 * layer)
            if layer in (0, 3):
                conv_layer(norm, n2, layer // 3)
            elif layer == 1:
                nat_layer(norm, n2)
            else:
                ret_layer(norm, n2)
            norm = new_norm("norm1", 8 * (layer + 1)) if layer < 3 else None
            ffn(n2, norm, layer, final=layer == 3)
        assert at["tile"] == N_TILES and not bg and not soon

        block = ctx.enter_context(nc.Block())

        @block.sync
        def _(e):
            SP.run(e)
            e.wait_ge(s_out, 128)

        @block.vector
        def _(e):
            V.run(e)

        @block.scalar
        def _(e):
            A.run(e)

        @block.gpsimd
        def _(e):
            P.run(e)

        @block.tensor
        def _(e):
            PE.run(e)


def rel_buckets():
    d = np.arange(0, 1024)
    large = 16 + (np.log(np.maximum(d, 1).astype(np.float32) / np.float32(16))
                  / np.float32(math.log(128 / 16)) * np.float32(16)).astype(np.int32)
    return np.where(d < 16, d, np.minimum(large, 31))


def constants():
    q = np.arange(128)
    c = {}
    c["ident"] = np.eye(128)
    c["ones"] = np.ones((128, 128))
    c["bones"] = np.kron(np.eye(2), np.ones((64, 64)))
    dist = q[:, None] + 384 - np.arange(ML)[None, :]
    c["mask"] = np.where(dist < 0, NEG, 0.0)
    col = q % 64
    first = np.clip(col - 8, 0, 48)
    kc = np.arange(64)
    c["colmask"] = np.where((kc[None] >= first[:, None]) & (kc[None] < first[:, None] + 16), 0.0, NEG)
    c["rowmask"] = (q >= 31).astype(float)[:, None]
    cst = np.concatenate([c[n] for n, _ in CONSTS], axis=1).astype(np.float32)
    theta = (np.float32(1.0) / (np.float32(10000.0) ** np.linspace(0.0, 1.0, 128, dtype=np.float32))).astype(np.float32)
    ang = (theta[:, None] * np.arange(T, dtype=np.float32)[None, :]).astype(np.float32)
    rope = np.stack([np.cos(ang.astype(np.float64)), np.sin(ang.astype(np.float64))]).astype(np.float32)
    rdist = (np.arange(ML)[None, :] - 384 - q[:, None]).astype(np.float32)
    return cst, rope, rdist


def kernel(**inp):
    import concourse.bacc as bacc
    from concourse.bass_utils import run_bass_kernel_spmd

    g = {k: np.asarray(v) for k, v in inp.items()}
    f32 = np.float32

    def cols(v):
        return np.ascontiguousarray(v.reshape(-1, 128).T)

    def twice(v):
        return np.concatenate([v, v], axis=-1)

    w_in = g["w_in"][0]
    order = list(range(0, 512))
    for c in range(2):
        for base in (512, 768, 1024):
            order += list(range(base + 128 * c, base + 128 * c + 128))
    parts = []
    fgw = np.zeros((D, 128), f32)
    fgw[:, 0:4] = w_in[:, 2048:2052]
    fgw[:, 32:44] = w_in[:, 2692:2704]
    parts.append(fgw)
    for c in range(2):
        for base in (1280, 1536, 1792):
            parts.append(w_in[:, base + 128 * c:base + 128 * c + 128])
    kv = [w_in[:, 2308 + 64 * j:2372 + 64 * j] for j in range(6)]
    parts = ([kv[0], kv[1], kv[2], kv[2], kv[4], kv[4], kv[3], kv[5]] + parts
             + [w_in[:, 2052:2308], w_in[:, order]])
    W = {"w_in": np.concatenate(parts, axis=1), "w_out": np.concatenate([g["w_out"][0][128 * k:128 * k + 128] for k in OUT_ORDER])}

    def pairs(first, second):
        n = first.shape[1] // 128
        a = first.reshape(D, n, 1, 128)
        b = second.reshape(D, n, 1, 128)
        return np.concatenate([a, b], axis=2).reshape(D, 2 * n * 128)

    def ffn(name, up, down):
        for i, (a, b) in enumerate(FF_PARTS):
            W[f"{name}_up{i}"] = up[:, 256 * a:256 * b]
            W[f"{name}_down{i}"] = down[128 * a:128 * b, :]

    F = 2816
    gu = g["w_gate_up"][0]
    ffn("ffn", pairs(gu[:, :F], gu[:, F:]), g["w_down"][0])
    for i in range(2):
        w = g["conv_w_in_2"][i]
        W[f"conv_in{i}"] = pairs(w[:, D:], w[:, :D])
        W[f"conv_out{i}"] = g["conv_w_out_2"][i]
    w = g["nat_w_qkv_2"][0]
    W["nat_qkv"] = w.reshape(D, 3, 8, 128).transpose(0, 2, 1, 3).reshape(D, 3072)
    W["nat_out"] = g["nat_w_out_2"][0]
    w = g["ret_w_in_2"][0]
    for h in range(4):
        W[f"ret_in{h}"] = np.concatenate([w[:, 256 * h:256 * h + 256], w[:, 1024 + 256 * h:1280 + 256 * h],
                                          w[:, 2048 + 512 * h:2560 + 512 * h],
                                          w[:, 4096 + 512 * h:4608 + 512 * h]], axis=1)
    for i in range(2):
        W[f"ret_out{i}"] = g["ret_w_out_2"][0][1024 * i:1024 * i + 1024]
    for layer in range(4):
        up = g["ffn_w_up_2"][layer]
        ffn(f"ffn2_{layer}", pairs(up[:, F:], up[:, :F]), g["ffn_w_down_2"][layer])
    flat = np.zeros((N_BLOCKS * 8, 128, 128), f32)
    at = 0
    for name, kc, mc in linears():
        w = W[name]
        w = w.reshape(kc, 128, mc, 128)
        n = wide(name)
        flat[at:at + kc * n] = w[:, :, :n].transpose(0, 2, 1, 3).reshape(-1, 128, 128)
        flat[at + kc * n:at + kc * mc] = w[:, :, n:].transpose(2, 0, 1, 3).reshape(-1, 128, 128)
        at += kc * mc
    wst = np.ascontiguousarray(flat.reshape(N_BLOCKS, 8, 128, 128).transpose(0, 2, 1, 3)).reshape(
        N_BLOCKS, 128, 1024)

    p = {}
    p["norm_mix"] = cols(g["norm_mix"])
    p["lru_conv_w"] = cols(g["lru_conv_w"])
    p["lru_conv_b"] = cols(g["lru_conv_b"])
    p["lru_b"] = cols(g["lru_b_gates"])
    p["lru_lambda"] = cols(g["lru_lambda"])
    p["sc_conv_w"] = cols(g["sc_conv_w"])
    p["fox_qk"] = cols(twice(g["fox_qk_norm"]))
    p["nsa_qk"] = cols(twice(g["nsa_qk_norm"]))
    fb = np.zeros((128, 1), f32)
    fb[0:4, 0] = g["fox_f_bias"][0]
    fb[32:44, 0] = g["nsa_gate_bias"][0]
    p["fg_bias"] = fb
    p["cmp_pos"] = g["nsa_cmp_pos"][0].transpose(0, 2, 1).reshape(128, 32)
    p["out_norm"] = cols(g["out_norm"])
    p["norm_ffn"] = cols(g["norm_ffn"])
    p["norm1"] = cols(g["norm1_g_2"])
    p["norm2"] = cols(g["norm2_g_2"])
    p["conv_b_in"] = cols(g["conv_b_in_2"])
    p["conv_dw_w"] = g["conv_dw_w_2"].reshape(2, 31, 8, 128).transpose(3, 0, 2, 1).reshape(128, 496)
    p["conv_dw_b"] = cols(g["conv_dw_b_2"])
    p["conv_ln_g"] = cols(g["conv_ln_g_2"])
    p["conv_ln_b"] = cols(g["conv_ln_b_2"])
    p["nat_q"] = cols(twice(g["nat_q_norm_g_2"]))
    p["nat_k"] = cols(twice(g["nat_k_norm_g_2"]))
    p["ret_dec"] = np.broadcast_to(g["ret_log2_inv_decay_2"].reshape(1, 8), (128, 8))
    p["ret_gn"] = cols(g["ret_gn_g_2"])
    p["ffn_dw_w"] = cols(g["ffn_dw_w_2"])
    p["ffn_dw_b"] = cols(g["ffn_dw_b_2"])
    prm = np.ascontiguousarray(np.concatenate([p[n] for n, _ in PARAMS], axis=1))
    cst, rope, rdist = constants()

    gw = g["lru_w_gates"][0]
    gatew = np.zeros((128, 2, 2, 128), f32)
    for i in range(2):
        for h in range(4):
            r = 64 * (h % 2)
            gatew[r:r + 64, i, h // 2, r:r + 64] = gw[i, h]
    cmpw1 = np.ascontiguousarray(g["nsa_cmp_w1"][0].transpose(0, 2, 1, 3)).reshape(128, 4096)
    w2 = g["nsa_cmp_w2"][0]
    cmpw2 = np.ascontiguousarray(np.concatenate([w2[0], w2[0], w2[1]], axis=1))
    q = np.arange(128)
    dd = np.maximum(q[:, None] + 384 - np.arange(ML)[None, :], 0)
    relm = np.ascontiguousarray(g["rel_bias"][rel_buckets()[dd]].transpose(2, 0, 1))
    rpb = g["nat_rpb_2"][0]
    ri, col = q // 64, q % 64
    jj = np.arange(1, 15)[None, :, None] - ri[:, None, None]
    xx = np.clip(np.arange(64)[None, None, :] - col[:, None, None] + 15, 0, 30)
    natb = np.ascontiguousarray(rpb[:, jj, xx]).reshape(16, 128, ML)

    arrays = {
        "wst": wst, "xin": np.ascontiguousarray(g["x"][0].T).reshape(8, 128, T), "prm": prm, "cst": cst,
        "gatew": gatew.reshape(128, 512), "cmpw1": cmpw1, "cmpw2": cmpw2, "relm": relm, "natb": natb,
        "rope": rope, "dist": rdist,
    }
    nc = bacc.Bacc("TRN2", target_bir_lowering=False, num_devices=1)
    aps = [nc.dram_tensor(n, a.shape, mybir.dt.float32, kind="ExternalInput").ap() for n, a in arrays.items()]
    out = nc.dram_tensor("out", (8, 128, T), mybir.dt.float32, kind="ExternalOutput").ap()
    build(nc, *aps, out)
    r = run_bass_kernel_spmd(nc, [arrays], core_ids=[0])
    return np.ascontiguousarray(r.results[0]["out"].reshape(D, T).T).reshape(1, T, D)
```
